# Optimizing a Trainium2 kernel written in Bass

```python
import math
import jax, jax.numpy as jnp
from jax import lax
import numpy as np

D_MODEL = 1024
BATCH = 1
SEQ = 256
DEPTH = 2

HEAD_DIM = 64
N_HEADS_A = 4
N_HEADS_B = 4
N_HEADS_C = 4
N_HEADS_D = 4
N_KV_D = 2
DIFF_DIM = HEAD_DIM // 2
IDX_HEADS = 8
IDX_DIM = 64
TOPK_MAX = 256
WINDOW = 128
BLOCK = 128
D_FF = 4 * D_MODEL
D_PLE = 256
ROPE_THETA = 10000.0
EPS = 1e-6
NEG_INF = -1e30
MIX_WIDTH = (N_HEADS_A + N_HEADS_B + N_HEADS_C + N_HEADS_D) * HEAD_DIM
SPLIT_WIDTHS = (
    N_HEADS_A * HEAD_DIM, N_HEADS_A * HEAD_DIM, N_HEADS_A * HEAD_DIM,
    IDX_HEADS * IDX_DIM, IDX_DIM, IDX_HEADS,
    N_HEADS_B * HEAD_DIM, N_HEADS_B * HEAD_DIM, N_HEADS_B * HEAD_DIM,
    N_HEADS_B,
    N_HEADS_C * HEAD_DIM, N_HEADS_C * HEAD_DIM, N_HEADS_C * HEAD_DIM,
    N_HEADS_D * HEAD_DIM, N_KV_D * HEAD_DIM, N_KV_D * HEAD_DIM,
)
D_IN = sum(SPLIT_WIDTHS)


def rmsnorm(x, g):
    xf = x.astype(jnp.float32)
    y = xf * lax.rsqrt(jnp.mean(xf * xf, axis=-1, keepdims=True) + EPS)
    return (y * g.astype(jnp.float32)).astype(x.dtype)

def rope_tables(positions, dim):
    half = dim // 2
    inv_freq = ROPE_THETA ** (-jnp.arange(half, dtype=jnp.float32) / half)
    ang = positions.astype(jnp.float32)[..., None] * inv_freq
    return jnp.cos(ang)[:, :, None, :], jnp.sin(ang)[:, :, None, :]

def apply_rope(x, tables):
    cos, sin = tables
    half = x.shape[-1] // 2
    xf = x.astype(jnp.float32)
    x1, x2 = xf[..., :half], xf[..., half:]
    return jnp.concatenate([x1 * cos - x2 * sin, x2 * cos + x1 * sin], axis=-1).astype(x.dtype)

def to_blocks(a):
    b, s = a.shape[:2]
    return jnp.moveaxis(a.reshape(b, s // BLOCK, BLOCK, *a.shape[2:]), 1, 0)

def from_blocks(o):
    nb, b = o.shape[:2]
    return jnp.moveaxis(o, 0, 1).reshape(b, nb * BLOCK, *o.shape[3:])

def dsa_attention(q, k, v, iq, ik, iw):
    s_len = k.shape[1]
    topk = min(TOPK_MAX, s_len // 4)
    key_pos = jnp.arange(s_len)
    scale = HEAD_DIM ** -0.5

    def one_block(args):
        qb, iqb, iwb, n = args
        t = n * BLOCK + jnp.arange(BLOCK)
        causal = key_pos[None, :] <= t[:, None]
        dots = jnp.einsum('bthd,bsd->bths', iqb, ik)
        score = jnp.einsum('bth,bths->bts', iwb, jax.nn.relu(dots)).astype(jnp.float32)
        score = jnp.where(causal[None], score, NEG_INF)
        _, idx = lax.top_k(score, topk)
        valid = idx <= t[None, :, None]
        k_sel = jax.vmap(lambda kk, ii: kk[ii])(k, idx)
        v_sel = jax.vmap(lambda vv, ii: vv[ii])(v, idx)
        logits = jnp.einsum('bthd,btjhd->bhtj', qb, k_sel).astype(jnp.float32) * scale
        logits = jnp.where(valid[:, None], logits, NEG_INF)
        probs = jax.nn.softmax(logits, axis=-1).astype(v.dtype)
        return jnp.einsum('bhtj,btjhd->bthd', probs, v_sel)

    nb = s_len // BLOCK
    out = lax.map(one_block, (to_blocks(q), to_blocks(iq), to_blocks(iw), jnp.arange(nb)))
    return from_blocks(out)

def forgetting_attention(q, k, v, log_f):
    s_len = k.shape[1]
    cum_bsh = jnp.cumsum(log_f, axis=1)
    cum = jnp.moveaxis(cum_bsh, 2, 1)
    key_pos = jnp.arange(s_len)
    scale = HEAD_DIM ** -0.5

    def one_block(args):
        qb, cb, n = args
        t = n * BLOCK + jnp.arange(BLOCK)
        causal = key_pos[None, :] <= t[:, None]
        logits = jnp.einsum('bthd,bshd->bhts', qb, k).astype(jnp.float32) * scale
        decay = jnp.moveaxis(cb, 2, 1)[..., :, None] - cum[:, :, None, :]
        logits = jnp.where(causal[None, None], logits + decay, NEG_INF)
        probs = jax.nn.softmax(logits, axis=-1).astype(v.dtype)
        return jnp.einsum('bhts,bshd->bthd', probs, v)

    nb = s_len // BLOCK
    out = lax.map(one_block, (to_blocks(q), to_blocks(cum_bsh), jnp.arange(nb)))
    return from_blocks(out)

def differential_attention(q, k, v, lam, lam_init, subln_g):
    s_len = k.shape[1]
    key_pos = jnp.arange(s_len)
    scale = DIFF_DIM ** -0.5

    def one_block(args):
        qb, n = args
        t = n * BLOCK + jnp.arange(BLOCK)
        causal = key_pos[None, :] <= t[:, None]
        logits = jnp.einsum('bthmd,bshmd->bmhts', qb, k).astype(jnp.float32) * scale
        logits = jnp.where(causal[None, None, None], logits, NEG_INF)
        probs = jax.nn.softmax(logits, axis=-1)
        diff = probs[:, 0] - lam * probs[:, 1]
        return jnp.einsum('bhts,bshd->bthd', diff.astype(v.dtype), v)

    nb = s_len // BLOCK
    out = from_blocks(lax.map(one_block, (to_blocks(q), jnp.arange(nb))))
    return rmsnorm(out, subln_g) * (1.0 - lam_init)

def sliding_window_sink_attention(q, k, v, sinks):
    b, s_len, n_h, dh = q.shape
    n_kv = k.shape[2]
    grp = n_h // n_kv
    nb = s_len // BLOCK
    qb = q.reshape(b, nb, BLOCK, n_kv, grp, dh)
    kb = k.reshape(b, nb, BLOCK, n_kv, dh)
    vb = v.reshape(b, nb, BLOCK, n_kv, dh)
    pad = ((0, 0), (1, 0), (0, 0), (0, 0), (0, 0))
    k_win = jnp.concatenate([jnp.pad(kb, pad)[:, :-1], kb], axis=2)
    v_win = jnp.concatenate([jnp.pad(vb, pad)[:, :-1], vb], axis=2)
    logits = jnp.einsum('bnikgd,bnjkd->bnkgij', qb, k_win).astype(jnp.float32) * (dh ** -0.5)
    i = jnp.arange(BLOCK)[:, None]
    j = jnp.arange(2 * BLOCK)[None, :]
    rel = i + BLOCK - j
    band = (rel >= 0) & (rel < WINDOW)
    in_range = (jnp.arange(nb)[:, None, None] > 0) | (j[None] >= BLOCK)
    mask = band[None] & in_range
    logits = jnp.where(mask[None, :, None, None], logits, NEG_INF)
    sink = jnp.broadcast_to(sinks.astype(jnp.float32).reshape(n_kv, grp)[None, None, :, :, None, None],
                            logits.shape[:-1] + (1,))
    probs = jax.nn.softmax(jnp.concatenate([logits, sink], axis=-1), axis=-1)[..., :-1]
    out = jnp.einsum('bnkgij,bnjkd->bnikgd', probs.astype(v.dtype), v_win)
    return out.reshape(b, s_len, n_h, dh)

def hybrid_layer(x, p_i, rope64, rope32, lam_init, w_in, b_forget, lq1, lk1, lq2, lk2,
                 diff_subln, sinks, w_out, g_pre_mix, g_post_mix, g_pre_mlp, g_post_mlp,
                 w_up, w_down, w_ple_proj, w_ple_gate):
    b, s_len, _ = x.shape
    h = rmsnorm(x, g_pre_mix)
    proj = h @ w_in
    points = np.cumsum(SPLIT_WIDTHS)[:-1].tolist()
    (a_q, a_k, a_v, a_iq, a_ik, a_iw, b_q, b_k, b_v, b_f,
     c_q, c_k, c_v, d_q, d_k, d_v) = jnp.split(proj, points, axis=-1)

    def heads(t, n, d):
        return t.reshape(b, s_len, n, d)

    iw = a_iw * (IDX_HEADS ** -0.5 * IDX_DIM ** -0.5)
    o_a = dsa_attention(apply_rope(heads(a_q, N_HEADS_A, HEAD_DIM), rope64),
                        apply_rope(heads(a_k, N_HEADS_A, HEAD_DIM), rope64),
                        heads(a_v, N_HEADS_A, HEAD_DIM),
                        apply_rope(heads(a_iq, IDX_HEADS, IDX_DIM), rope64),
                        apply_rope(a_ik[:, :, None, :], rope64)[:, :, 0],
                        iw)
    log_f = jax.nn.log_sigmoid((b_f + b_forget).astype(jnp.float32))
    o_b = forgetting_attention(heads(b_q, N_HEADS_B, HEAD_DIM), heads(b_k, N_HEADS_B, HEAD_DIM),
                               heads(b_v, N_HEADS_B, HEAD_DIM), log_f)
    cq = apply_rope(heads(c_q, 2 * N_HEADS_C, DIFF_DIM), rope32).reshape(b, s_len, N_HEADS_C, 2, DIFF_DIM)
    ck = apply_rope(heads(c_k, 2 * N_HEADS_C, DIFF_DIM), rope32).reshape(b, s_len, N_HEADS_C, 2, DIFF_DIM)
    f32 = jnp.float32
    lam = (jnp.exp(jnp.sum(lq1.astype(f32) * lk1.astype(f32)))
           - jnp.exp(jnp.sum(lq2.astype(f32) * lk2.astype(f32))) + lam_init)
    o_c = differential_attention(cq, ck, heads(c_v, N_HEADS_C, HEAD_DIM), lam, lam_init, diff_subln)
    o_d = sliding_window_sink_attention(apply_rope(heads(d_q, N_HEADS_D, HEAD_DIM), rope64),
                                        apply_rope(heads(d_k, N_KV_D, HEAD_DIM), rope64),
                                        heads(d_v, N_KV_D, HEAD_DIM), sinks)

    mix = jnp.concatenate([o_a.reshape(b, s_len, -1), o_b.reshape(b, s_len, -1),
                           o_c.reshape(b, s_len, -1), o_d.reshape(b, s_len, -1)], axis=-1)
    x = x + rmsnorm(mix @ w_out, g_post_mix)

    h = rmsnorm(x, g_pre_mlp)
    m = jnp.square(jax.nn.relu(h @ w_up)) @ w_down
    x = x + rmsnorm(m, g_post_mlp)

    x = x + jax.nn.sigmoid(x @ w_ple_gate) * (p_i @ w_ple_proj)
    return x

def first_inputs(seed: int = 0) -> dict:
    key = jax.random.key(seed)
    ks = jax.random.split(key, 22)

    def normal(k, shape, scale):
        return jax.random.normal(k, shape, jnp.float32) * scale

    def gain(k, shape):
        return 1.0 + 0.02 * jax.random.normal(k, shape, jnp.float32)

    return {
        'x': normal(ks[0], (BATCH, SEQ, D_MODEL), 1.0),
        'p': normal(ks[1], (DEPTH, BATCH, SEQ, D_PLE), 1.0),
        'positions': jnp.broadcast_to(jnp.arange(SEQ, dtype=jnp.int32), (BATCH, SEQ)),
        'w_in': normal(ks[2], (DEPTH, D_MODEL, D_IN), D_MODEL ** -0.5),
        'b_forget': 2.0 + normal(ks[3], (DEPTH, N_HEADS_B), 0.5),
        'lambda_q1': normal(ks[4], (DEPTH, DIFF_DIM), 0.1),
        'lambda_k1': normal(ks[5], (DEPTH, DIFF_DIM), 0.1),
        'lambda_q2': normal(ks[6], (DEPTH, DIFF_DIM), 0.1),
        'lambda_k2': normal(ks[7], (DEPTH, DIFF_DIM), 0.1),
        'diff_subln': gain(ks[8], (DEPTH, HEAD_DIM)),
        'sinks': normal(ks[9], (DEPTH, N_HEADS_D), 1.0),
        'w_out': normal(ks[10], (DEPTH, MIX_WIDTH, D_MODEL), MIX_WIDTH ** -0.5),
        'norm_pre_mix': gain(ks[11], (DEPTH, D_MODEL)),
        'norm_post_mix': gain(ks[12], (DEPTH, D_MODEL)),
        'norm_pre_mlp': gain(ks[13], (DEPTH, D_MODEL)),
        'norm_post_mlp': gain(ks[14], (DEPTH, D_MODEL)),
        'w_mlp_up': normal(ks[15], (DEPTH, D_MODEL, D_FF), D_MODEL ** -0.5),
        'w_mlp_down': normal(ks[16], (DEPTH, D_FF, D_MODEL), D_FF ** -0.5),
        'w_ple_proj': normal(ks[17], (DEPTH, D_PLE, D_MODEL), D_PLE ** -0.5),
        'w_ple_gate': normal(ks[18], (DEPTH, D_MODEL, D_MODEL), D_MODEL ** -0.5),
    }

def first_block(x, p, positions, w_in, b_forget, lambda_q1, lambda_k1, lambda_q2, lambda_k2,
              diff_subln, sinks, w_out, norm_pre_mix, norm_post_mix, norm_pre_mlp, norm_post_mlp,
              w_mlp_up, w_mlp_down, w_ple_proj, w_ple_gate):
    rope64 = rope_tables(positions, HEAD_DIM)
    rope32 = rope_tables(positions, DIFF_DIM)
    for i in range(DEPTH):
        lam_init = 0.8 - 0.6 * math.exp(-0.3 * i)
        x = hybrid_layer(x, p[i], rope64, rope32, lam_init, w_in[i], b_forget[i],
                         lambda_q1[i], lambda_k1[i], lambda_q2[i], lambda_k2[i],
                         diff_subln[i], sinks[i], w_out[i], norm_pre_mix[i], norm_post_mix[i],
                         norm_pre_mlp[i], norm_post_mlp[i], w_mlp_up[i], w_mlp_down[i],
                         w_ple_proj[i], w_ple_gate[i])
    return x


ATTN_GROUPS = ((128, 1), (512, 4), (2048, 16))
N_GROUPS = len(ATTN_GROUPS)
HEADS_PER_GROUP = 6
N_ATTN_HEADS = N_GROUPS * HEADS_PER_GROUP
ATTN_WIDTH = N_ATTN_HEADS * HEAD_DIM
ATTN_OUT_WIDTH = HEADS_PER_GROUP * HEAD_DIM
NUM_BUCKETS = 32
MAX_DISTANCE = 2048
RET_HEADS = 4
RET_QK_DIM = 256
RET_V_DIM = 2 * RET_QK_DIM
RET_QK_WIDTH = RET_HEADS * RET_QK_DIM
RET_V_WIDTH = RET_HEADS * RET_V_DIM
RET_CHUNK = 128
ROPE_BASE = 10000.0
D_FF_2 = -(-8 * D_MODEL // (3 * 256)) * 256
ALPHA = (2 * DEPTH) ** 0.25
BETA = (8 * DEPTH) ** -0.25
LN_EPS = 1e-5
GN_EPS = 1e-5
SPLIT_SIZES = (ATTN_WIDTH, ATTN_WIDTH, ATTN_WIDTH,
               RET_QK_WIDTH, RET_QK_WIDTH, RET_V_WIDTH, RET_V_WIDTH,
               D_MODEL, D_MODEL)
IN_COLS = sum(SPLIT_SIZES)
SPLIT_POINTS = tuple(int(v) for v in np.cumsum(SPLIT_SIZES)[:-1])


def _t5_bucket(dist):
    max_exact = NUM_BUCKETS // 2
    large = max_exact + (np.log(np.maximum(dist, max_exact) / max_exact)
                         / np.log(MAX_DISTANCE / max_exact)
                         * (NUM_BUCKETS - max_exact)).astype(np.int32)
    large = np.minimum(large, NUM_BUCKETS - 1)
    return np.where(dist < max_exact, dist, large).astype(np.int32)

def _layer_norm(x, g, b):
    xf = x.astype(jnp.float32)
    mu = jnp.mean(xf, axis=-1, keepdims=True)
    var = jnp.mean(jnp.square(xf - mu), axis=-1, keepdims=True)
    return ((xf - mu) * lax.rsqrt(var + LN_EPS) * g + b).astype(x.dtype)

def _dilated_window_attention(q, k, v, bias_table, window, dilation):
    B, S, H, Dh = q.shape
    W = window // dilation
    L = S // dilation
    nb = -(-L // W)
    Lp = nb * W

    def to_sub(t):
        t = t.reshape(B, L, dilation, H, Dh).transpose(0, 2, 3, 1, 4)
        return jnp.pad(t, ((0, 0), (0, 0), (0, 0), (0, Lp - L), (0, 0)))

    def band(t):
        t = jnp.pad(to_sub(t), ((0, 0), (0, 0), (0, 0), (W, 0), (0, 0)))
        prev = t[:, :, :, :Lp].reshape(B, dilation, H, nb, W, Dh)
        cur = t[:, :, :, W:].reshape(B, dilation, H, nb, W, Dh)
        return jnp.concatenate([prev, cur], axis=-2)

    qs = to_sub(q).reshape(B, dilation, H, nb, W, Dh)
    kb, vb = band(k), band(v)

    qi = np.arange(W)[:, None]
    kj = np.arange(2 * W)[None, :]
    rel = qi + W - kj
    in_win = (rel >= 0) & (rel <= W)
    key_idx = np.arange(nb)[:, None, None] * W + kj[None] - W
    mask = in_win[None] & (key_idx >= 0)
    buckets = _t5_bucket(np.clip(rel, 0, W) * dilation)
    bias = jnp.moveaxis(jnp.take(bias_table, buckets, axis=0), -1, 0).astype(jnp.float32)

    s = jnp.einsum('bghnqe,bghnke->bghnqk', qs, kb).astype(jnp.float32) * (Dh ** -0.5)
    s = s + bias[None, None, :, None]
    s = jnp.where(mask[None, None, None], s, -jnp.inf)
    m = jnp.max(s, axis=-1, keepdims=True)
    p = jnp.exp(s - m)
    l = jnp.sum(p, axis=-1, keepdims=True)
    o = jnp.einsum('bghnqk,bghnke->bghnqe', (p / l).astype(v.dtype), vb)
    lse = (m + jnp.log(l))[..., 0]
    o = o.reshape(B, dilation, H, Lp, Dh)[:, :, :, :L].transpose(0, 3, 1, 2, 4).reshape(B, S, H, Dh)
    lse = lse.reshape(B, dilation, H, Lp)[..., :L].transpose(0, 3, 1, 2).reshape(B, S, H)
    return o, lse

def _retention(q, k, v):
    B, S, H, dk = q.shape
    dv = v.shape[-1]
    half = dk // 2
    pos = jnp.arange(S, dtype=jnp.float32)
    inv_freq = ROPE_BASE ** (-jnp.arange(half, dtype=jnp.float32) / half)
    ang = pos[:, None] * inv_freq[None]
    cos = jnp.cos(ang)[None, :, None]
    sin = jnp.sin(ang)[None, :, None]

    def rot(t):
        t1, t2 = t[..., :half], t[..., half:]
        return jnp.concatenate([t1 * cos - t2 * sin, t1 * sin + t2 * cos], axis=-1).astype(t.dtype)

    q = rot(q)
    k = rot(k) * (dk ** -0.5)
    log_g = jnp.log(1.0 - 2.0 ** (-5.0 - jnp.arange(H, dtype=jnp.float32)))
    C = RET_CHUNK
    nC = S // C
    n = jnp.arange(C, dtype=jnp.float32)
    diff = n[:, None] - n[None, :]
    decay_mask = jnp.where(diff >= 0, jnp.exp(log_g[:, None, None] * jnp.maximum(diff, 0.0)), 0.0)
    q_dec = jnp.exp(log_g[:, None] * (n + 1.0))
    k_dec = jnp.exp(log_g[:, None] * (C - 1.0 - n))
    chunk_dec = jnp.exp(log_g * C)

    def chunks(t):
        return t.reshape(B, nC, C, H, t.shape[-1]).transpose(1, 0, 3, 2, 4)

    def step(state, xs):
        qc, kc, vc = xs
        sc = jnp.einsum('bhnd,bhmd->bhnm', qc, kc) * decay_mask
        o = (jnp.einsum('bhnm,bhmv->bhnv', sc, vc)
             + jnp.einsum('bhnd,bhdv->bhnv', qc * q_dec[..., None], state))
        state = (state * chunk_dec[:, None, None]
                 + jnp.einsum('bhmd,bhmv->bhdv', kc * k_dec[..., None], vc))
        return state.astype(jnp.float32), o.astype(jnp.float32)

    state0 = jnp.zeros((B, H, dk, dv), jnp.float32)
    _, ys = lax.scan(step, state0, (chunks(q), chunks(k), chunks(v)))
    o = ys.transpose(1, 0, 3, 2, 4).reshape(B, S, H, dv)
    mu = jnp.mean(o, axis=-1, keepdims=True)
    var = jnp.mean(jnp.square(o - mu), axis=-1, keepdims=True)
    return (o - mu) * lax.rsqrt(var + GN_EPS)

def _hybrid_mixer(x, rel_bias, w_in, b_in, w_attn_proj, w_ret_proj, w_out):
    B, S, _ = x.shape
    z = jnp.einsum('bsd,dc->bsc', x, w_in) + b_in
    q_a, k_a, v_a, q_r, k_r, v_r, g_r, gate_a, gate_b = jnp.split(z, SPLIT_POINTS, axis=-1)
    q_a = q_a.reshape(B, S, N_GROUPS, HEADS_PER_GROUP, HEAD_DIM)
    k_a = k_a.reshape(B, S, N_GROUPS, HEADS_PER_GROUP, HEAD_DIM)
    v_a = v_a.reshape(B, S, N_GROUPS, HEADS_PER_GROUP, HEAD_DIM)
    outs, lses = [], []
    for gi, (window, dilation) in enumerate(ATTN_GROUPS):
        o, lse = _dilated_window_attention(
            q_a[:, :, gi], k_a[:, :, gi], v_a[:, :, gi],
            rel_bias[:, gi * HEADS_PER_GROUP:(gi + 1) * HEADS_PER_GROUP], window, dilation)
        outs.append(o.astype(jnp.float32))
        lses.append(lse)
    wts = jax.nn.softmax(jnp.stack(lses, axis=0), axis=0)
    y_a = jnp.sum(wts[..., None] * jnp.stack(outs, axis=0), axis=0)
    y_a = y_a.astype(x.dtype).reshape(B, S, ATTN_OUT_WIDTH)
    y_r = _retention(q_r.reshape(B, S, RET_HEADS, RET_QK_DIM),
                     k_r.reshape(B, S, RET_HEADS, RET_QK_DIM),
                     v_r.reshape(B, S, RET_HEADS, RET_V_DIM))
    y_b = (jax.nn.silu(g_r) * y_r.reshape(B, S, RET_V_WIDTH)).astype(x.dtype)
    merged = (jax.nn.sigmoid(gate_a) * jnp.einsum('bsc,cd->bsd', y_a, w_attn_proj)
              + jax.nn.sigmoid(gate_b) * jnp.einsum('bsc,cd->bsd', y_b, w_ret_proj))
    return jnp.einsum('bsd,de->bse', merged, w_out)

def _swiglu(x, w_gate, w_up, w_down):
    h = jax.nn.silu(jnp.einsum('bsd,df->bsf', x, w_gate)) * jnp.einsum('bsd,df->bsf', x, w_up)
    return jnp.einsum('bsf,fd->bsd', h, w_down)

def second_inputs(seed: int = 0) -> dict:
    key = jax.random.key(seed)
    ks = jax.random.split(key, 14)
    f32 = jnp.float32

    def nrm(k, shape, scale):
        return jax.random.normal(k, shape, f32) * scale

    return {
        "x": nrm(ks[0], (BATCH, SEQ, D_MODEL), 1.0),
        "rel_bias": nrm(ks[1], (NUM_BUCKETS, N_ATTN_HEADS), 0.2),
        "w_in": nrm(ks[2], (DEPTH, D_MODEL, IN_COLS), D_MODEL ** -0.5),
        "b_in": nrm(ks[3], (DEPTH, IN_COLS), 0.02),
        "w_attn_proj": nrm(ks[4], (DEPTH, ATTN_OUT_WIDTH, D_MODEL), BETA * ATTN_OUT_WIDTH ** -0.5),
        "w_ret_proj": nrm(ks[5], (DEPTH, RET_V_WIDTH, D_MODEL), BETA * RET_V_WIDTH ** -0.5),
        "w_out": nrm(ks[6], (DEPTH, D_MODEL, D_MODEL), BETA * D_MODEL ** -0.5),
        "ln1_g": 1.0 + nrm(ks[7], (DEPTH, D_MODEL), 0.02),
        "ln1_b": nrm(ks[8], (DEPTH, D_MODEL), 0.02),
        "w_ffn_gate": nrm(ks[9], (DEPTH, D_MODEL, D_FF_2), D_MODEL ** -0.5),
        "w_ffn_up": nrm(ks[10], (DEPTH, D_MODEL, D_FF_2), D_MODEL ** -0.5),
        "w_ffn_down": nrm(ks[11], (DEPTH, D_FF_2, D_MODEL), BETA * D_FF_2 ** -0.5),
        "ln2_g": 1.0 + nrm(ks[12], (DEPTH, D_MODEL), 0.02),
        "ln2_b": nrm(ks[13], (DEPTH, D_MODEL), 0.02),
    }

def second_block(x, rel_bias, w_in, b_in, w_attn_proj, w_ret_proj, w_out, ln1_g, ln1_b,
              w_ffn_gate, w_ffn_up, w_ffn_down, ln2_g, ln2_b):
    for l in range(DEPTH):
        mix = _hybrid_mixer(x, rel_bias, w_in[l], b_in[l], w_attn_proj[l], w_ret_proj[l], w_out[l])
        x = _layer_norm(ALPHA * x + mix, ln1_g[l], ln1_b[l])
        ffn = _swiglu(x, w_ffn_gate[l], w_ffn_up[l], w_ffn_down[l])
        x = _layer_norm(ALPHA * x + ffn, ln2_g[l], ln2_b[l])
    return x


def setup_inputs(seed=0):
    out = dict(first_inputs(seed))
    for name, value in second_inputs(seed + 1).items():
        if name != "x":
            out[name + "_2"] = value
    return out


def reference(
    x, p, positions, w_in, b_forget, lambda_q1, lambda_k1, lambda_q2, lambda_k2, diff_subln,
    sinks, w_out, norm_pre_mix, norm_post_mix, norm_pre_mlp, norm_post_mlp, w_mlp_up,
    w_mlp_down, w_ple_proj, w_ple_gate, rel_bias_2, w_in_2, b_in_2, w_attn_proj_2, w_ret_proj_2,
    w_out_2, ln1_g_2, ln1_b_2, w_ffn_gate_2, w_ffn_up_2, w_ffn_down_2, ln2_g_2, ln2_b_2,
):
    x = first_block(
        x, p, positions, w_in, b_forget, lambda_q1, lambda_k1, lambda_q2, lambda_k2, diff_subln,
        sinks, w_out, norm_pre_mix, norm_post_mix, norm_pre_mlp, norm_post_mlp, w_mlp_up,
        w_mlp_down, w_ple_proj, w_ple_gate,
    )
    return second_block(
        x, rel_bias_2, w_in_2, b_in_2, w_attn_proj_2, w_ret_proj_2, w_out_2, ln1_g_2, ln1_b_2,
        w_ffn_gate_2, w_ffn_up_2, w_ffn_down_2, ln2_g_2, ln2_b_2,
    )


_drawn_inputs = setup_inputs


def setup_inputs(seed=0):
    import zlib

    import numpy as np

    out = dict(_drawn_inputs(seed))
    spreads = {}
    factors = {'lambda_q2': 5.467,
     'diff_subln': 2.851,
     'norm_pre_mlp': 2.765,
     'norm_post_mlp': 2.983,
     'rel_bias_2': 8.0,
     'b_in_2': 8.0,
     'sinks': 4.735}
    for name, (base, spread) in spreads.items():
        noise = np.random.default_rng([zlib.crc32(name.encode()), seed]).standard_normal(out[name].shape)
        drawn = base * np.exp(spread * noise) if base else spread * noise
        out[name] = __import__('jax').numpy.asarray(drawn.astype(out[name].dtype))
    for name, factor in factors.items():
        out[name] = (out[name] * factor).astype(out[name].dtype)
    return out
```

```python
import math
from contextlib import ExitStack

import numpy as np

import concourse.bass as bass
from concourse import mybir

F32 = mybir.dt.float32
F32R = mybir.dt.float32r
BF16 = mybir.dt.bfloat16
I32 = mybir.dt.int32
ALU = mybir.AluOpType
ACT = mybir.ActivationFunctionType
AX = mybir.AxisListType

P = 128
DM = 1024
S = 256
TILES = S // P
DEPTH = 2
KB = DM // P
COLS = 512
UK = 4
UNIT = UK * COLS
RAW = 4
PARTS = 2
HD = 64
EPS = 1e-6
LN_EPS = 1e-5
NEG = -1e30
TAKEN = -3e38
TOPK = 64
ALPHA = (2 * DEPTH) ** 0.25

A_Q, A_K, A_V, A_IQ, A_IK, A_IW = 0, 256, 512, 768, 1280, 1344
B_Q, B_K, B_V, B_F = 1352, 1608, 1864, 2120
C_Q, C_K, C_V = 2124, 2380, 2636
D_Q, D_K, D_V = 2892, 3148, 3276
D_IN = 3404
CH1 = 7
LAST1 = D_IN - 6 * COLS
D_FF = 4096
D_PLE = 256
IDX_HEADS = 8
MIX0 = A_IQ

ATTN_W = 1152
HG = 6
GROUPS = ((128, 1), (512, 4), (2048, 16))
RQ0 = 3 * ATTN_W
SEG1 = 7
LAST2 = RQ0 - 6 * COLS
IN2 = 11648
RH, RDV = 4, 512
YA_W = 384
D_FF2 = 2816
FJ = D_FF2 // 256

U_OUT, U_MLP, U_PLE, UNITS1 = 14, 18, 50, 56
V_RET, V_GATE, V_AP, V_RP, V_OUT, V_FFN, UNITS2 = 14, 30, 46, 48, 56, 60, 104

T_QK, T_JOB, T_MIX, T_N2, T_MLP, T_P, T_PX, TS1 = 4, 15, 30, 34, 38, 54, 56, 60
T2_QK, T2_JOB, T2_YA, T2_RET, T2_YB, T2_M, T2_FX, T2_FFN, TS2 = 4, 13, 31, 34, 42, 50, 54, 58, 80

JOBS1 = [("B", 0, 0), ("B", 1, 0), ("A", 0, 0), ("A", 1, 0), ("C", 0, 0), ("C", 0, 1),
         ("C", 1, 0), ("C", 1, 1), ("D", 0, 0), ("D", 1, 0)]
JOBS2 = [("E", m, h) for h in range(HG) for m in range(TILES)]
MIXCOL = {"A": 0, "B": 256, "C": 512, "D": 768}
SCALE = {"A": HD ** -0.5, "B": HD ** -0.5, "C": (HD // 2) ** -0.5, "D": HD ** -0.5, "E": HD ** -0.5}


def job_banks(jobs, q):
    return sum(m + 1 for _, m, _ in jobs[:q])


def split_no(blk, t):
    if blk == 0:
        return t if t <= T_QK else t - (T_MIX - T_QK)
    if t <= T2_QK:
        return t
    return t - (T2_YA - T2_QK) - (0 if t <= T2_RET else T2_YB - T2_RET)


class Tally:

    def __init__(self, sem, per, credit=0, step=1):
        self.sem, self.per, self.credit, self.step = sem, per, credit, step

    def at(self, blk, layer, k):
        base = self.credit + (DEPTH * self.per[0] if blk else 0)
        return layer * (self.per[blk] * self.step) + (k + base) * self.step


def constants():
    i = np.arange(P)
    c = {}
    ident = np.eye(P, dtype=np.float32)
    tri = (np.arange(S)[:, None] <= np.arange(S)[None, :]).astype(np.float32)
    causal = np.where(np.arange(S)[None, :] <= np.arange(S)[:, None], 0.0, NEG).astype(np.float32)
    tile_rows = lambda a: np.ascontiguousarray(a.reshape(TILES, P, -1).transpose(1, 0, 2))
    c["c_ident"] = ident
    c["c_flip"] = np.ascontiguousarray(ident[::-1])
    c["c_tri"] = tile_rows(tri)
    c["c_causal"] = tile_rows(causal)
    c["c_masks"] = np.stack([np.where(i[None] <= i[:, None], 0.0, NEG),
                             np.where(i[None] > i[:, None], 0.0, NEG)], 1).astype(np.float32)
    gam = np.log(1.0 - 2.0 ** (-5.0 - np.arange(RH)))
    diff = i[None, :] - i[:, None]
    diag = np.where(diff >= 0, np.exp(gam[:, None, None] * np.maximum(diff, 0)), 0.0)
    off = np.exp(gam[:, None, None] * (diff + P))
    c["c_decay"] = np.ascontiguousarray(
        (np.stack([diag, off], 1) / 16.0).transpose(2, 0, 1, 3)).astype(np.float32)
    inv = (np.float32(10000.0) ** (-np.arange(P, dtype=np.float32) / np.float32(P))).astype(np.float32)
    ang = (np.arange(S, dtype=np.float32)[:, None] * inv[None]).astype(np.float64)
    c["c_rot"] = np.ascontiguousarray(np.stack([tile_rows(np.cos(ang)), tile_rows(np.sin(ang))], 1)).astype(np.float32)
    f64 = (np.float32(10000.0) ** (-np.arange(32, dtype=np.float32) / np.float32(32))).astype(np.float32)
    f32 = (np.float32(10000.0) ** (-np.arange(16, dtype=np.float32) / np.float32(16))).astype(np.float32)
    c["c_freq"] = np.concatenate([f64, f64, f32, f32]).astype(np.float32)
    dist = 255 - np.arange(512)
    d = np.maximum(dist, 0)
    large = 16 + (np.log(np.maximum(d, 16) / 16) / np.log(2048 / 16) * 16).astype(np.int32)
    bucket = np.where(d < 16, d, np.minimum(large, 31))
    onehot = (np.arange(32)[:, None] == bucket[None]).astype(np.float32) * np.float32(HD ** 0.5)
    ok = np.concatenate([np.tile((dist >= 0) & (d <= w) & (d % s == 0), (HG, 1)) for w, s in GROUPS])
    c["c_onehot"] = onehot
    c["c_ok"] = np.stack([ok.astype(np.float32), np.where(ok, 0.0, NEG).astype(np.float32)], 1)
    lam0 = np.array([0.8 - 0.6 * math.exp(-0.3 * n) for n in range(DEPTH)])
    c["c_lam"] = np.concatenate([lam0, 1.0 - lam0]).astype(np.float32)
    return c


def program(nc, a, out):
    bias_rows = nc.dram_tensor("bias_rows", (18, 512), F32, kind="Internal").ap()

    with ExitStack() as ctx:
        def sb(name, shape, dt=F32):
            return ctx.enter_context(nc.sbuf_tensor(name, shape, dt))

        def psum(name, shape):
            return ctx.enter_context(nc.psum_tensor(name, shape, F32))

        def sem(name):
            return ctx.enter_context(nc.semaphore(name))

        raw = sb("raw", [P, RAW, UNIT])
        whi = sb("whi", [P, PARTS, UNIT], F32R)
        wlo = sb("wlo", [P, PARTS, UNIT], F32R)
        X = sb("X", [P, TILES, DM])
        XH = sb("XH", [P, KB, S], F32R)
        XL = sb("XL", [P, KB, S], F32R)
        MH = sb("MH", [P, UK, S], F32R)
        ML = sb("ML", [P, UK, S], F32R)
        YH = sb("YH", [P, KB, S], F32R)
        YL = sb("YL", [P, KB, S], F32R)
        gains = sb("gains", [P, 2, DM])
        arena = sb("arena", [P, 17100])

        def room(lo, *dims):
            n = int(np.prod(dims))
            ap = arena[:, lo:lo + n]
            if len(dims) == 1:
                return ap
            names = "abcd"[:len(dims)]
            kw = {names[i]: dims[i] for i in range(1, len(dims))}
            return ap.rearrange(f"p ({' '.join(names)}) -> p {' '.join(names)}", **kw)

        Z = room(0, TILES, D_IN)
        DUP = room(6808, TILES, 384)
        QT = room(7576, 21, S)
        PR = room(12952, 2, 4, S)
        PT = room(15000, 2, TILES, 512)
        RL = room(12952, IDX_HEADS, S)
        RT = room(15000, 1152)
        CO = room(6808, TILES, 4, HD)
        CS = room(7576, TILES, 4, HD)
        H = room(0, TILES, COLS)
        TMP = room(2048, TILES, COLS)
        PP = room(4096, TILES, DM)
        SG = room(8192, TILES, COLS)
        PB = room(9216, TILES, D_PLE)
        Z2 = room(0, TILES, RQ0)
        QT2 = room(6912, 18, S)
        PR2 = room(11520, 2, 3, S)
        PT2 = room(13056, 2, TILES, 384)
        BR = room(14592, 2, 3, S)
        QK = room(0, TILES, 2048)
        VR = room(4096, TILES, 2048)
        QTR = room(8192, 16, S)
        SCT = room(12288, 2, 384)
        RTR = room(13056, 2, TILES, 2, P)
        GZ = room(8192, TILES, COLS)
        SZ = room(9216, TILES, COLS)
        M = room(10240, TILES, DM)
        TMP2 = room(12288, TILES, COLS)
        H2 = room(0, TILES, 256)
        swap = sb("swap", [P, 2, COLS])
        BIN = swap[:]
        tri = swap[:, 0].rearrange("p (m s) -> p m s", m=TILES)
        causal = swap[:, 1].rearrange("p (m s) -> p m s", m=TILES)

        ident = sb("ident", [P, P])
        flip = sb("flip", [P, P])
        identb = sb("identb", [P, P], BF16)
        maskb = sb("maskb", [P, 2, P], BF16)
        amask = sb("amask", [P, TILES, S], BF16)
        decay = sb("decay", [P, RH, 2, P])
        rot = sb("rot", [P, 2, TILES, P])
        cosd = sb("cosd", [P, TILES, 96])
        sind = sb("sind", [P, TILES, 96])
        freq = sb("freq", [P, 96])
        posi = sb("posi", [P, TILES], I32)
        posf = sb("posf", [P, TILES])
        small = sb("small", [P, 424])
        bforget, sink = small[:, 0:8], small[:, 8:16]
        subln, lamv, lamc = small[:, 16:144], small[:, 144:400], small[:, 400:404]
        lsum, lam = small[:, 404:408], small[:, 408:410]
        cur = sb("cur", [P, 90])
        pre = sb("pre", [P, 2, DEPTH, KB])
        prec = sb("prec", [P, 2, KB])
        stat = sb("stat", [P, 3, 5, 8])
        mx, nm, ls = (sb(n, [P, 12, 4]) for n in ("mx", "nm", "ls"))
        rl, es, ds_ = (sb(n, [P, 12, 4]) for n in ("rl", "es", "ds_"))
        IW = sb("IW", [P, TILES, IDX_HEADS])
        SCO = sb("SCO", [P, S])
        m8 = sb("m8", [P, 8])
        LF = sb("LF", [P, 5, TILES, 4])
        bns = sb("bns", [P, 4, 6])
        bna = sb("bna", [P, 4, 2])

        G = psum("G", [P, 4, 512])
        T = psum("T", [P, 2, 512])
        A = psum("A", [P, 2, 512])

        s_raw = [Tally(sem(f"s_raw{n}"), (UNITS1 // RAW, UNITS2 // RAW + more), step=16)
                 for n, more in enumerate((1, 1, FJ - 1, FJ - 1))]
        s_hi = Tally(sem("s_hi"), (UNITS1, UNITS2))
        s_lo = Tally(sem("s_lo"), (UNITS1, UNITS2), credit=RAW)
        s_used = Tally(sem("s_used"), (UNITS1, UNITS2), credit=PARTS)
        s_evac = Tally(sem("s_evac"), (CH1, 29), credit=2)
        s_t = Tally(sem("s_t"), (TS1, TS2))
        s_thi = Tally(sem("s_thi"), (TS1 - 26, TS2 - 35))
        s_tfree = Tally(sem("s_tfree"), (TS1, TS2), credit=2)
        s_x = Tally(sem("s_x"), (3, 2), credit=1)
        s_ss = Tally(sem("s_ss"), (4, 0))
        s_ms = Tally(sem("s_ms"), (5, 4))
        s_sd = Tally(sem("s_sd"), (5, 4))
        s_rs = Tally(sem("s_rs"), (2, 0))
        s_cur = Tally(sem("s_cur"), (1, 0))
        s_dup = Tally(sem("s_dup"), (4, 0))
        s_lf = Tally(sem("s_lf"), (3, 0))
        s_lg = Tally(sem("s_lg"), (2, 0))
        s_dot = Tally(sem("s_dot"), (2, 0))
        s_rl = Tally(sem("s_rl"), (2, 0))
        s_rlf = Tally(sem("s_rlf"), (2, 0), credit=1)
        s_am = Tally(sem("s_am"), (2, 0))
        s_log = Tally(sem("s_log"), (len(JOBS1), len(JOBS2)))
        s_nm = Tally(sem("s_nm"), (len(JOBS1), len(JOBS2)))
        s_exp = Tally(sem("s_exp"), (len(JOBS1), len(JOBS2)), credit=2)
        s_pv = Tally(sem("s_pv"), (len(JOBS1), len(JOBS2)))
        s_o = Tally(sem("s_o"), (len(JOBS1), len(JOBS2)), credit=2)
        s_mix = Tally(sem("s_mix"), (1, 0))
        s_act = Tally(sem("s_act"), (8, FJ))
        s_h = Tally(sem("s_h"), (8, FJ))
        s_gain = Tally(sem("s_gain"), (2, 4), step=16)
        s_p = Tally(sem("s_p"), (1, 0), step=16)
        s_pp = Tally(sem("s_pp"), (2, 0))
        s_sg = Tally(sem("s_sg"), (2, 0))
        s_sgf = Tally(sem("s_sgf"), (2, 0), credit=1)
        s_bin = [Tally(sem(f"s_bin{n}"), (0, n0), step=16) for n, n0 in ((0, 12), (1, 11))]
        s_br = [Tally(sem(f"s_br{n}"), (0, 6), step=16) for n in (0, 1)]
        s_rot = Tally(sem("s_rot"), (0, 1))
        s_sc = Tally(sem("s_sc"), (0, RH))
        s_sd2 = Tally(sem("s_sd2"), (0, RH))
        s_ro = Tally(sem("s_ro"), (0, RH))
        s_yr = Tally(sem("s_yr"), (0, RH // 2), credit=1)
        s_sz = Tally(sem("s_sz"), (0, 8))
        s_m = Tally(sem("s_m"), (0, 1))
        s_yb = Tally(sem("s_yb"), (0, 4))
        s_xin = sem("s_xin")
        s_const = sem("s_const")
        s_tab = sem("s_tab")
        s_sin = sem("s_sin")
        s_bmm = sem("s_bmm")
        s_bvec = sem("s_bvec")
        s_brow = sem("s_brow")
        s_le = sem("s_le")
        s_out = sem("s_out")

        block = ctx.enter_context(nc.Block())
        N_CONST = 22

        @block.sync
        def _(sp):
            def unit(blk, L, u, src, kb, cols, slot):
                sp.wait_ge(s_lo.sem, s_lo.at(blk, L, u - RAW + 1))
                dst = raw[:, slot, 0:kb * cols].rearrange("p (k n) -> p k n", n=cols)
                return sp.dma_start(dst, src).then_inc(s_raw[slot].sem, 16)

            def rows(w, L, r0, kb, c0, cols):
                return w[bass.ds(L, 1), r0:r0 + kb * P, :][:, :, bass.ds(c0, cols)].rearrange(
                    "l (k p) n -> p (l k) n", p=P)

            n_const = 0
            sp.dma_start(X[:], a["x"].rearrange("b (m p) d -> p (b m) d", p=P)).then_inc(s_xin, 16)

            def const(dst, src):
                sp.dma_start(dst, src).then_inc(s_const, 16)

            with nc.allow_non_contiguous_dma(reason="small parameters"):
                const(ident[:], a["c_ident"])
                const(flip[:], a["c_flip"])
                const(tri, a["c_tri"])
                const(causal, a["c_causal"])
                const(decay[:], a["c_decay"])
                const(rot[:], a["c_rot"])
                const(freq[:], a["c_freq"].partition_broadcast(P))
                const(posi[:], a["positions"].rearrange("b (m p) -> p (b m)", p=P))
                const(room(0, 2, P), a["c_masks"])
                const(arena[0:32, 256:274], a["rel_bias_2"])
                const(arena[0:32, 512:1024], a["c_onehot"])
                const(arena[0:18, 1024:2048].rearrange("p (a b) -> p a b", a=2), a["c_ok"])
                const(bforget, a["b_forget"].rearrange("l n -> (l n)").partition_broadcast(P))
                const(sink, a["sinks"].rearrange("l n -> (l n)").partition_broadcast(P))
                const(subln, a["diff_subln"].rearrange("l n -> (l n)").partition_broadcast(P))
                for n, name in enumerate(("lambda_q1", "lambda_k1", "lambda_q2", "lambda_k2")):
                    const(lamv[:, n * 64:n * 64 + 64], a[name].rearrange("l n -> (l n)").partition_broadcast(P))
                const(lamc, a["c_lam"].partition_broadcast(P))
                for n, name in enumerate(("norm_pre_mix", "norm_pre_mlp")):
                    sp.dma_start(pre[:, n], a[name].rearrange("l (k p) -> p l k", p=P)).then_inc(s_const, 16)
            sp.wait_ge(s_bvec, 1)
            sp.dma_start(bias_rows, arena[0:18, 2048:2560]).then_inc(s_brow, 16)

            with sp.Fori(0, DEPTH) as L:
                w = a["w_in"]
                with sp.Fori(0, 3) as i:
                    for c in range(2):
                        for k in range(2):
                            u = 2 * c + k
                            unit(0, L, 4 * i + u, rows(w, L, 512 * k, UK, i * 1024 + c * COLS, COLS), UK, COLS, u)
                for k in range(2):
                    unit(0, L, 12 + k, rows(w, L, 512 * k, UK, 6 * COLS, LAST1), UK, LAST1, k)
                sp.wait_ge(s_x.sem, s_x.at(0, L, 0))
                for n, name in enumerate(("norm_post_mix", "norm_post_mlp")):
                    sp.dma_start(gains[:, n:n + 1, :], a[name][bass.ds(L, 1), :].partition_broadcast(P)).then_inc(
                        s_gain.sem, 16)
                w = a["w_out"]
                for n in range(4):
                    u = U_OUT + n
                    unit(0, L, u, rows(w, L, 512 * (n % 2), UK, n // 2 * COLS, COLS), UK, COLS, u % RAW)
                up, down = a["w_mlp_up"], a["w_mlp_down"]
                for k in range(2):
                    unit(0, L, U_MLP + k, rows(up, L, 512 * k, UK, 0, COLS), UK, COLS, (U_MLP + k) % RAW)
                with sp.Fori(0, 7) as i:
                    for k in range(2):
                        unit(0, L, 4 * i + U_MLP + 2 + k, rows(up, L, 512 * k, UK, i * COLS + COLS, COLS),
                             UK, COLS, (U_MLP + 2 + k) % RAW)
                    for n in range(2):
                        src = down[bass.ds(L, 1)][:, bass.ds(i * COLS, COLS), n * COLS:(n + 1) * COLS].rearrange(
                            "l (k p) n -> p (l k) n", p=P)
                        unit(0, L, 4 * i + U_MLP + 4 + n, src, UK, COLS, (U_MLP + 4 + n) % RAW)
                sp.wait_ge(s_x.sem, s_x.at(0, L, 1))
                sp.dma_start(PB[:], a["p"][bass.ds(L, 1)].rearrange("l b (m p) d -> p (l b m) d", p=P)).then_inc(
                    s_p.sem, 16)
                for n in range(2):
                    unit(0, L, U_MLP + 30 + n, rows(down, L, 7 * COLS, UK, n * COLS, COLS), UK, COLS, (U_MLP + 30 + n) % RAW)
                for n in range(2):
                    unit(0, L, U_PLE + n, rows(a["w_ple_proj"], L, 0, 2, n * COLS, COLS), 2, COLS, (U_PLE + n) % RAW)
                for n in range(4):
                    u = U_PLE + 2 + n
                    unit(0, L, u, rows(a["w_ple_gate"], L, 512 * (n % 2), UK, n // 2 * COLS, COLS), UK, COLS, u % RAW)

            sp.wait_ge(s_mix.sem, s_mix.at(0, DEPTH, 0))
            with sp.Fori(0, DEPTH) as L:
                w = a["w_in_2"]

                def bias_in(c, c0, cols, slot):
                    sp.wait_ge(s_evac.sem, s_evac.at(1, L, c - 1))
                    src = a["b_in_2"][bass.ds(L, 1), :][:, bass.ds(c0, cols)].partition_broadcast(P)
                    sp.dma_start(BIN[:, slot:slot + 1, 0:cols], src).then_inc(s_bin[slot].sem, 16)

                def w_in_chunks(i, u0, c0, col0, chunks=2):
                    for c in range(chunks):
                        for k in range(2):
                            u = 2 * c + k
                            unit(1, L, 4 * i + u0 + u, rows(w, L, 512 * k, UK, i * 1024 + (col0 + c * COLS), COLS),
                                 UK, COLS, (u0 + u) % RAW)
                        bias_in(2 * i + c0 + c, i * 1024 + (col0 + c * COLS), COLS, (c0 + c) % 2)

                with sp.Fori(0, 3) as i:
                    w_in_chunks(i, 0, 0, 0)
                for k in range(2):
                    unit(1, L, 12 + k, rows(w, L, 512 * k, UK, 6 * COLS, LAST2), UK, LAST2, k)
                bias_in(6, 6 * COLS, LAST2, 0)
                sp.wait_ge(s_x.sem, s_x.at(1, L, 0))
                for n, name in enumerate(("ln1_g_2", "ln1_b_2")):
                    sp.dma_start(gains[:, n:n + 1, :], a[name][bass.ds(L, 1), :].partition_broadcast(P)).then_inc(
                        s_gain.sem, 16)
                w_in_chunks(0, V_RET, 7, RQ0, 1)
                sp.wait_ge(s_brow, 16)
                sp.wait_ge(s_t.sem, s_t.at(1, L, T2_QK))
                for q, (_, m, h) in enumerate(JOBS2):
                    if q >= 2:
                        sp.wait_ge(s_log.sem, s_log.at(1, L, q - 1))
                    n = (m + 1) * P
                    src = bass.AP(bias_rows.tensor, h * 512 + (1 - m) * P, [[1, P], [HG * 512, 3], [1, n]])
                    sp.dma_start(BR[:, q % 2, :, 0:n], src).then_inc(s_br[q % 2].sem, 16)
                with sp.Fori(0, 3) as i:
                    w_in_chunks(i, V_RET + 2, 8, RQ0 + COLS)
                w_in_chunks(0, V_RET + 14, 14, RQ0 + 7 * COLS, 1)
                with sp.Fori(0, 4) as i:
                    w_in_chunks(i, V_GATE, 15, RQ0 + 8 * COLS)
                for n in range(2):
                    unit(1, L, V_AP + n, rows(a["w_attn_proj_2"], L, 0, 3, n * COLS, COLS), 3, COLS, (V_AP + n) % RAW)
                for n in range(8):
                    u = V_RP + n
                    unit(1, L, u, rows(a["w_ret_proj_2"], L, 512 * (n % 4), UK, n // 4 * COLS, COLS), UK, COLS, u % RAW)
                for n in range(4):
                    u = V_OUT + n
                    unit(1, L, u, rows(a["w_out_2"], L, 512 * (n % 2), UK, n // 2 * COLS, COLS), UK, COLS, u % RAW)

                gate, up, down = a["w_ffn_gate_2"], a["w_ffn_up_2"], a["w_ffn_down_2"]

                def gate_up(j, u, k, slot):
                    sp.wait_ge(s_lo.sem, s_lo.at(1, L, u - RAW + 1))
                    dst = raw[:, slot].rearrange("p (k g n) -> p k g n", k=UK, g=2)
                    for g, wt in enumerate((gate, up)):
                        src = wt[bass.ds(L, 1), 512 * k:512 * k + 512, :][:, :, bass.ds(j * 256, 256)].rearrange(
                            "l (k p) n -> p (l k) n", p=P)
                        sp.dma_start(dst[:, :, g, :], src).then_inc(s_raw[slot].sem, 16)

                for k in range(2):
                    gate_up(0, V_FFN + k, k, (V_FFN + k) % RAW)
                with sp.Fori(0, FJ - 1) as i:
                    for k in range(2):
                        gate_up(i + 1, 4 * i + V_FFN + 2 + k, k, (V_FFN + 2 + k) % RAW)
                    for n in range(2):
                        src = down[bass.ds(L, 1)][:, bass.ds(i * 256, 256), n * COLS:(n + 1) * COLS].rearrange(
                            "l (k p) n -> p (l k) n", p=P)
                        unit(1, L, 4 * i + V_FFN + 4 + n, src, 2, COLS, (V_FFN + 4 + n) % RAW)
                for n in range(2):
                    unit(1, L, V_FFN + 42 + n, rows(down, L, (FJ - 1) * 256, 2, n * COLS, COLS), 2, COLS,
                         (V_FFN + 42 + n) % RAW)
                sp.wait_ge(s_x.sem, s_x.at(1, L, 1))
                for n, name in enumerate(("ln2_g_2", "ln2_b_2")):
                    sp.dma_start(gains[:, n:n + 1, :], a[name][bass.ds(L, 1), :].partition_broadcast(P)).then_inc(
                        s_gain.sem, 16)
            sp.wait_ge(s_x.sem, s_x.at(1, DEPTH, 0))
            sp.dma_start(out.rearrange("b (m p) d -> p (b m) d", p=P), X[:]).then_inc(s_out, 16)
            sp.wait_ge(s_out, 16)

        def landed(blk, L, i, c):
            o, slot = i + c // RAW, c % RAW
            k = o + 1
            if blk and c >= V_FFN:
                if slot < 2:
                    k = o + 2
                elif c >= UNITS2 - 2:
                    k = o + FJ
                else:
                    k = o * 2 - (2 * (V_FFN // RAW) - 17)
            return s_raw[slot].at(blk, L, k)

        def size(blk, c):
            if blk == 0:
                return UK * LAST1 if c in (12, 13) else 2 * COLS if c in (50, 51) else UNIT
            if c in (12, 13):
                return UK * LAST2
            if c in (V_AP, V_AP + 1):
                return 3 * COLS
            small_unit = c >= UNITS2 - 2 or (c >= V_FFN + 4 and c % RAW < 2)
            return 2 * COLS if small_unit else UNIT

        def logit_set(q):
            g = G[:, 2 * (q % 2):2 * (q % 2) + 2, :]
            return g.rearrange("p b (u s) -> p (b u) s", s=S)

        def logit(q, u):
            return G[:, 2 * (q % 2) + u % 2, u // 2 * S:(u // 2 + 1) * S]

        def pair(n):
            return A[:, :, :] if n == 2 else G[:, 2 * n:2 * n + 2, :]

        @block.tensor
        def _(pe):
            def unit(blk, L, i, c, hx, lx, k0, kb, cols, dst, first, last):
                hi = whi[:, c % PARTS, 0:kb * cols].rearrange("p (k n) -> p k n", n=cols)
                lo = wlo[:, c % PARTS, 0:kb * cols].rearrange("p (k n) -> p k n", n=cols)
                pe.wait_ge(s_hi.sem, s_hi.at(blk, L, 4 * i + c + 1))
                for k in range(kb):
                    for m in range(TILES):
                        rows = slice(m * P, (m + 1) * P)
                        nc.tensor.matmul(dst(m), hx[:, k0 + k, rows], hi[:, k, :], start=first and k == 0, stop=False)
                        nc.tensor.matmul(dst(m), lx[:, k0 + k, rows], hi[:, k, :], start=False, stop=False)
                pe.wait_ge(s_lo.sem, s_lo.at(blk, L, 4 * i + c + 1))
                for k in range(kb):
                    for m in range(TILES):
                        mm = nc.tensor.matmul(dst(m), hx[:, k0 + k, m * P:(m + 1) * P], lo[:, k, :],
                                              start=False, stop=last and k == kb - 1)
                mm.then_inc(s_used.sem, 1)

            def bank_pair(n, cols=COLS):
                return lambda m: pair(n)[:, m, 0:cols]

            def chunk(blk, L, i, c, group, cols=COLS, hx=XH, lx=XL):
                for k in range(2):
                    unit(blk, L, i, c + k, hx, lx, UK * k, UK, cols, bank_pair(group, cols), k == 0, k == 1)

            def transposes(blk, L, i, t, blocks):
                pe.wait_ge(s_tfree.sem, s_tfree.at(blk, L, 2 * i + t - 1))
                for n, src in enumerate(blocks):
                    tr = nc.tensor.transpose(T[:, t % 2, n * P:(n + 1) * P], src, ident[:])
                tr.then_inc(s_t.sem, 1)

            def both(src, blocks):
                return [src[:, m, b * P:(b + 1) * P] for b in blocks for m in range(TILES)]

            def turn(blk, L, i, t, src, nblocks, per=2):
                for b in range(0, nblocks, per):
                    transposes(blk, L, i, t + b // per, both(src, range(b, min(b + per, nblocks))))

            def job_outputs(blk, L, q, jobs, t0):
                kind, m, x = jobs[q]
                pe.wait_ge(s_tfree.sem, s_tfree.at(blk, L, t0 + job_banks(jobs, q + 1)))
                pe.wait_ge(s_o.sem, s_o.at(blk, L, q - 1))
                for u in range(3 if kind == "E" else 4):
                    for kt in range(m + 1):
                        if kind == "E":
                            v = Z2[:, kt, 2 * ATTN_W + (u * HG + x) * HD:][:, 0:HD]
                            mm = nc.tensor.matmul(A[:, q % 2, 0:HD], PT2[:, q % 2, kt, u * P:(u + 1) * P], v,
                                                  start=(u == 0 and kt == 0), stop=(u == 2 and kt == m))
                        else:
                            col = {"A": A_V + u * HD, "B": B_V + u * HD, "D": D_V + u // 2 * HD,
                                   "C": C_V + (2 * (u // 2) + x) * HD}[kind]
                            mm = nc.tensor.matmul(A[:, q % 2, u * HD:(u + 1) * HD], PT[:, q % 2, kt, u * P:(u + 1) * P],
                                                  Z[:, kt, col:col + HD], start=kt == 0, stop=kt == m)
                mm.then_inc(s_pv.sem, 1)

            def job_turn(blk, L, q, jobs, t0, probs):
                kind, m, _ = jobs[q]
                pe.wait_ge(s_exp.sem, s_exp.at(blk, L, q + 1))
                for kt in range(m + 1):
                    t = t0 + job_banks(jobs, q) + kt
                    transposes(blk, L, 0, t, [probs[:, q % 2, u, kt * P:(kt + 1) * P]
                                              for u in range(3 if kind == "E" else 4)])

            pe.wait_ge(s_const, 16 * N_CONST)
            nc.tensor.matmul(T[0:18, 0, :], arena[0:32, 256:274], arena[0:32, 512:1024], start=True, stop=True).then_inc(s_bmm, 1)
            pe.sem_inc(s_used.sem, s_used.credit)
            pe.wait_ge(s_bvec, 1)

            def logits1(L, q):
                kind, m, x = JOBS1[q]
                n = (m + 1) * P
                rows = slice(m * P, (m + 1) * P)
                pe.wait_ge(s_exp.sem, s_exp.at(0, L, q - 1))
                for u in range(4):
                    dst = logit(q, u)
                    if kind == "C":
                        qb, kb = 13 + u // 2, 15 + u // 2
                        part = slice(32 * (2 * x + u % 2), 32 * (2 * x + u % 2) + 32)
                    else:
                        qb, kb = {"A": (9 + u // 2, 11 + u // 2), "B": (u // 2, 2 + u // 2),
                                  "D": (17 + u // 2, 19 + u // 2)}[kind]
                        part = slice(HD * (u % 2), HD * (u % 2) + HD)
                    nc.tensor.matmul(dst[:, 0:n], QT[part, qb, rows], QT[part, kb, 0:n], start=True, stop=False)
                    if kind == "A":
                        mm = nc.tensor.matmul(dst[:, 0:n], identb[:], amask[:, m, 0:n], start=False, stop=True)
                        continue
                    if kind == "B":
                        for kt in range(m + 1):
                            nc.tensor.matmul(dst[:, 0:n], LF[:, 4, kt, u:u + 1].to_broadcast([P, P]),
                                             tri[:, kt, 0:n], start=False, stop=False)
                    if kind == "D" and m == 1:
                        nc.tensor.matmul(dst[:, 0:P], identb[:], maskb[:, 1], start=False, stop=False)
                    mm = nc.tensor.matmul(dst[:, m * P:n], identb[:], maskb[:, 0], start=False, stop=True)
                mm.then_inc(s_log.sem, 1)

            def logits2(L, q):
                _, m, h = JOBS2[q]
                n = (m + 1) * P
                part = slice(HD * (h % 2), HD * (h % 2) + HD)
                pe.wait_ge(s_exp.sem, s_exp.at(1, L, q - 1))
                pe.wait_ge(s_br[q % 2].sem, s_br[q % 2].at(1, L, q // 2 + 1))
                dst = logit_set(q)
                for g in range(3):
                    b = 3 * g + h // 2
                    nc.tensor.matmul(dst[:, g, 0:n], QT2[part, b, m * P:(m + 1) * P], QT2[part, 9 + b, 0:n],
                                     start=True, stop=False)
                    mm = nc.tensor.matmul(dst[:, g, 0:n], flip[:], BR[:, q % 2, g, 0:n], start=False, stop=True)
                mm.then_inc(s_log.sem, 1)

            def run_jobs(blk, L, jobs, t0, logits, probs):
                for q in range(len(jobs) + 2):
                    if q < len(jobs):
                        logits(L, q)
                    if 1 <= q <= len(jobs):
                        job_turn(blk, L, q - 1, jobs, t0, probs)
                    if q >= 2:
                        job_outputs(blk, L, q - 2, jobs, t0)

            with pe.Fori(0, DEPTH) as L:
                pe.wait_ge(s_x.sem, s_x.at(0, L, 0))
                turn(0, L, 0, 0, X, KB)
                with pe.Fori(0, 3) as i:
                    pe.wait_ge(s_tfree.sem, s_tfree.at(0, L, T_QK))
                    for c in range(2):
                        pe.wait_ge(s_evac.sem, s_evac.at(0, L, 2 * i + c - 1))
                        chunk(0, L, i, 2 * c, c)
                pe.wait_ge(s_evac.sem, s_evac.at(0, L, 5))
                chunk(0, L, 0, 12, 0, LAST1)

                pe.wait_ge(s_evac.sem, s_evac.at(0, L, CH1))
                pe.wait_ge(s_dup.sem, s_dup.at(0, L, 4))
                zb = lambda col: [Z[:, m, col:col + P] for m in range(TILES)]
                db = lambda col: [DUP[:, m, col:col + P] for m in range(TILES)]
                blocks = [zb(c) for c in (B_Q, B_Q + P, B_K, B_K + P)] + [zb(A_IQ + n * P) for n in range(4)] + [db(0)]
                blocks += [zb(c) for c in (A_Q, A_Q + P, A_K, A_K + P, C_Q, C_Q + P, C_K, C_K + P, D_Q, D_Q + P)]
                blocks += [db(P), db(2 * P)]
                for b in range(0, 21, 2):
                    transposes(0, L, 0, T_QK + b // 2, sum(blocks[b:b + 2], []))
                pe.wait_ge(s_tfree.sem, s_tfree.at(0, L, T_JOB))
                for m in range(TILES):
                    n = (m + 1) * P
                    if m:
                        pe.wait_ge(s_rl.sem, s_rl.at(0, L, 1))
                    for h in range(IDX_HEADS):
                        part = slice(HD * (h % 2), HD * (h % 2) + HD)
                        mm = nc.tensor.matmul(G[:, h % 4, h // 4 * S:h // 4 * S + n], QT[part, 4 + h // 2, m * P:n],
                                              QT[part, 8, 0:n], start=True, stop=True)
                    mm.then_inc(s_dot.sem, 1)
                pe.wait_ge(s_rl.sem, s_rl.at(0, L, 2))
                pe.wait_ge(s_lf.sem, s_lf.at(0, L, 3))
                pe.wait_ge(s_am.sem, s_am.at(0, L, 2))
                run_jobs(0, L, JOBS1, T_JOB, logits1, PR)

                pe.wait_ge(s_mix.sem, s_mix.at(0, L, 1))
                turn(0, L, 0, T_MIX, Z[:, :, MIX0:MIX0 + DM], KB)
                pe.wait_ge(s_tfree.sem, s_tfree.at(0, L, T_N2))
                chunk(0, L, 0, U_OUT, 1)
                chunk(0, L, 0, U_OUT + 2, 0)

                pe.wait_ge(s_x.sem, s_x.at(0, L, 1))
                turn(0, L, 0, T_N2, X, KB)
                pe.wait_ge(s_tfree.sem, s_tfree.at(0, L, T_MLP))

                def inner_turn(i, j):
                    pe.wait_ge(s_h.sem, s_h.at(0, L, i + j + 1))
                    turn(0, L, i, T_MLP + 2 * j, H, UK)

                def down(i, c, first, last, t):
                    pe.wait_ge(s_tfree.sem, s_tfree.at(0, L, 2 * i + t))
                    for n in range(2):
                        unit(0, L, i, c + n, MH, ML, 0, UK, COLS, bank_pair(1 + n), first, last)

                chunk(0, L, 0, U_MLP, 0)
                inner_turn(0, 0)
                chunk(0, L, 0, U_MLP + 2, 0)
                down(0, U_MLP + 4, True, False, T_MLP + 2)
                inner_turn(0, 1)
                with pe.Fori(0, 6) as i:
                    chunk(0, L, i, U_MLP + 6, 0)
                    down(i, U_MLP + 8, False, False, T_MLP + 4)
                    inner_turn(i, 2)
                down(0, U_MLP + 30, False, True, T_MLP + 16)

                pe.wait_ge(s_p.sem, s_p.at(0, L, 1))
                turn(0, L, 0, T_P, PB, 2, per=1)
                pe.wait_ge(s_tfree.sem, s_tfree.at(0, L, T_PX))
                unit(0, L, 0, U_PLE, YH, YL, 0, 2, COLS, bank_pair(0), True, True)
                pe.wait_ge(s_x.sem, s_x.at(0, L, 2))
                unit(0, L, 0, U_PLE + 1, YH, YL, 0, 2, COLS, bank_pair(1), True, True)
                turn(0, L, 0, T_PX, X, KB)
                pe.wait_ge(s_tfree.sem, s_tfree.at(0, L, TS1))
                for n in range(2):
                    pe.wait_ge(s_pp.sem, s_pp.at(0, L, n + 1))
                    chunk(0, L, 0, U_PLE + 2 + 2 * n, n)

            with pe.Fori(0, DEPTH) as L:
                pe.wait_ge(s_x.sem, s_x.at(1, L, 0))
                turn(1, L, 0, 0, X, KB)
                def w_in_chunk(i, c, u):
                    pe.wait_ge(s_evac.sem, s_evac.at(1, L, 2 * i + c - 1))
                    chunk(1, L, i, u, c % 2)

                with pe.Fori(0, 3) as i:
                    pe.wait_ge(s_tfree.sem, s_tfree.at(1, L, T2_QK))
                    for c in range(2):
                        w_in_chunk(i, c, 2 * c)
                pe.wait_ge(s_evac.sem, s_evac.at(1, L, 5))
                chunk(1, L, 0, 12, 0, LAST2)

                pe.wait_ge(s_evac.sem, s_evac.at(1, L, SEG1))
                turn(1, L, 0, T2_QK, Z2, 18)
                pe.wait_ge(s_tfree.sem, s_tfree.at(1, L, T2_JOB))
                run_jobs(1, L, JOBS2, T2_JOB, logits2, PR2)
                pe.wait_ge(s_o.sem, s_o.at(1, L, len(JOBS2)))
                turn(1, L, 0, T2_YA, Z2, 3, per=1)

                with pe.Fori(0, 4) as i:
                    for c in range(2):
                        w_in_chunk(i, SEG1 + c, V_RET + 2 * c)
                pe.wait_ge(s_rot.sem, s_rot.at(1, L, 4))
                turn(1, L, 0, T2_RET, QK, 16)
                pe.wait_ge(s_tfree.sem, s_tfree.at(1, L, T2_YB))
                pe.wait_ge(s_evac.sem, s_evac.at(1, L, 15))

                def scores(h):
                    for kt in range(TILES):
                        for b in range(2):
                            o = A[:, h % 2, 0:S] if kt == 0 else A[:, h % 2, S:S + P]
                            mm = nc.tensor.matmul(o, QTR[:, 8 + 2 * h + b, kt * P:(kt + 1) * P],
                                                  QTR[:, 2 * h + b, kt * P:S], start=b == 0, stop=b == 1)
                    mm.then_inc(s_sc.sem, 1)

                def outputs(h):
                    pe.wait_ge(s_sd2.sem, s_sd2.at(1, L, h + 1))
                    v = lambda kt: VR[:, kt, h * RDV:(h + 1) * RDV]
                    g = 2 * (h % 2)
                    nc.tensor.matmul(G[:, g], SCT[:, h % 2, 0:P], v(0), start=True, stop=True)
                    nc.tensor.matmul(G[:, g + 1], SCT[:, h % 2, P:S], v(0), start=True, stop=False)
                    nc.tensor.matmul(G[:, g + 1], SCT[:, h % 2, S:S + P], v(1), start=False, stop=True).then_inc(s_ro.sem, 1)

                scores(0)
                scores(1)
                outputs(0)
                outputs(1)
                scores(2)
                scores(3)
                pe.wait_ge(s_yr.sem, s_yr.at(1, L, 1))
                outputs(2)
                outputs(3)

                with pe.Fori(0, 4) as i:
                    pe.wait_ge(s_yr.sem, s_yr.at(1, L, 2))
                    for c in range(2):
                        w_in_chunk(i, 15 + c, V_GATE + 2 * c)
                pe.wait_ge(s_yb.sem, s_yb.at(1, L, 4))
                for n in range(2):
                    for b in range(2):
                        transposes(1, L, 0, T2_YB + 2 * n + b, both(QK, (4 * n + 2 * b, 4 * n + 2 * b + 1)))
                    pe.wait_ge(s_evac.sem, s_evac.at(1, L, 22 + n))
                    unit(1, L, 0, V_AP + n, MH, ML, 0, 3, COLS, bank_pair(1 - n), True, True)
                for b in range(4, 8):
                    transposes(1, L, 0, T2_YB + b, both(QK, (2 * b, 2 * b + 1)))
                pe.wait_ge(s_tfree.sem, s_tfree.at(1, L, T2_M))
                for n in range(2):
                    pe.wait_ge(s_evac.sem, s_evac.at(1, L, 24 + n))
                    for k in range(4):
                        hx, lx = (XH, XL) if k < 2 else (YH, YL)
                        unit(1, L, 0, V_RP + 4 * n + k, hx, lx, UK * (k % 2), UK, COLS, bank_pair(1 - n), k == 0, k == 3)
                pe.wait_ge(s_m.sem, s_m.at(1, L, 1))
                turn(1, L, 0, T2_M, M, KB)
                pe.wait_ge(s_tfree.sem, s_tfree.at(1, L, T2_FX))
                chunk(1, L, 0, V_OUT, 1)
                chunk(1, L, 0, V_OUT + 2, 0)

                pe.wait_ge(s_x.sem, s_x.at(1, L, 1))
                turn(1, L, 0, T2_FX, X, KB)
                pe.wait_ge(s_tfree.sem, s_tfree.at(1, L, T2_FFN))

                def inner_turn2(i, j):
                    pe.wait_ge(s_h.sem, s_h.at(1, L, i + j + 1))
                    turn(1, L, i, T2_FFN + 2 * j, H2, 2, per=1)

                def down2(i, c, first, last, t):
                    pe.wait_ge(s_tfree.sem, s_tfree.at(1, L, 2 * i + t))
                    for n in range(2):
                        unit(1, L, i, c + n, MH, ML, 0, 2, COLS, bank_pair(1 + n), first, last)

                chunk(1, L, 0, V_FFN, 0)
                inner_turn2(0, 0)
                chunk(1, L, 0, V_FFN + 2, 0)
                down2(0, V_FFN + 4, True, False, T2_FFN + 2)
                inner_turn2(0, 1)
                with pe.Fori(0, FJ - 2) as i:
                    chunk(1, L, i, V_FFN + 6, 0)
                    down2(i, V_FFN + 8, False, False, T2_FFN + 4)
                    inner_turn2(i, 2)
                down2(0, V_FFN + 42, False, True, T2_FFN + 2 * FJ)

        @block.scalar
        def _(act):
            def act_(out_, in_, func, **kw):
                return nc.scalar.activation(out_, in_, func, **kw)

            def hi(blk, L, i, c):
                n, slot = size(blk, c), c % RAW
                act.wait_ge(s_raw[slot].sem, landed(blk, L, i, c))
                act.wait_ge(s_used.sem, s_used.at(blk, L, 4 * i + c - 1))
                act_(whi[:, c % PARTS, 0:n], raw[:, slot, 0:n], ACT.Copy).then_inc(s_hi.sem, 1)

            def his(blk, L, i, *cs):
                for c in cs:
                    hi(blk, L, i, c)

            def turn_hi(blk, L, i, t, n, dst, per=2, gain=None):
                for b in range(0, n, per):
                    tt = t + b // per
                    act.wait_ge(s_t.sem, s_t.at(blk, L, 2 * i + tt + 1))
                    k = min(per, n - b)
                    src = T[:, tt % 2, 0:k * S].rearrange("p (k s) -> p k s", s=S)
                    if gain is None:
                        ins = act_(dst[:, b:b + k, :], src, ACT.Copy)
                    else:
                        for kk in range(k):
                            ins = act_(dst[:, b + kk, :], src[:, kk, :], ACT.Copy, scale=gain[:, b + kk:b + kk + 1])
                    ins.then_inc(s_thi.sem, 1)

            def turn_copy(blk, L, t, n, dst):
                for b in range(0, n, 2):
                    tt = t + b // 2
                    act.wait_ge(s_t.sem, s_t.at(blk, L, tt + 1))
                    k = min(2, n - b)
                    act_(dst[:, b:b + k, :], T[:, tt % 2, 0:k * S].rearrange("p (k s) -> p k s", s=S),
                         ACT.Copy).then_inc(s_tfree.sem, 1)

            def root(blk, L, k, norm, n):
                act.wait_ge(s_ms.sem, s_ms.at(blk, L, k))
                act_(stat[:, 1, norm, 0:n], stat[:, 0, norm, 0:n], ACT.Sqrt).then_inc(s_sd.sem, 1)

            def exps(blk, L, q, jobs, probs):
                kind, m, _ = jobs[q]
                n = (m + 1) * P
                act.wait_ge(s_nm.sem, s_nm.at(blk, L, q + 1))
                src = logit_set(q)
                if kind == "E":
                    act_(probs[:, q % 2, :, 0:n], src[:, 0:3, 0:n], ACT.Exp, bias=nm[:, q, 0:1], scale=SCALE[kind],
                         accum_out=ls[:, q, 0:1]).then_inc(s_exp.sem, 1)
                    return
                if kind == "D":
                    act_(es[:, q, :], ds_[:, q, :], ACT.Exp)
                for u in range(4):
                    ins = act_(probs[:, q % 2, u, 0:n], logit(q, u)[:, 0:n], ACT.Exp, bias=nm[:, q, u:u + 1],
                               scale=SCALE[kind], accum_out=ls[:, q, u:u + 1])
                ins.then_inc(s_exp.sem, 1)

            act.sem_inc(s_exp.sem, s_exp.credit)
            act.wait_ge(s_tab, 1)
            act_(lsum, lsum, ACT.Exp).then_inc(s_le, 1)
            act.wait_ge(s_tab, 2)
            act_(cosd[:], cosd[:], ACT.Sin)
            act_(sind[:], sind[:], ACT.Sin).then_inc(s_sin, 1)
            act.wait_ge(s_brow, 16)

            with act.Fori(0, DEPTH) as L:
                his(0, L, 0, 0, 1)
                act.wait_ge(s_cur.sem, s_cur.at(0, L, 1))
                turn_hi(0, L, 0, 0, KB, XH, gain=prec[:, 0])
                act.wait_ge(s_x.sem, s_x.at(0, L, 0))
                for m in range(TILES):
                    ins = act_(room(12288, TILES, DM)[:, m], X[:, m, :], ACT.Square, accum_out=stat[:, 0, 0, m:m + 1])
                ins.then_inc(s_ss.sem, 1)
                root(0, L, 1, 0, 2)

                def project(i, c, cols=COLS):
                    act.wait_ge(s_used.sem, s_used.at(0, L, 4 * i + 2 * c + 2))
                    for m in range(TILES):
                        dst = Z[:, m, c * COLS:c * COLS + cols] if isinstance(i, int) else \
                            Z[:, m, bass.ds(i * 1024 + c * COLS, cols)]
                        ins = act_(dst, G[:, 2 * (c % 2) + m, 0:cols], ACT.Copy, scale=stat[:, 2, 0, m:m + 1])
                    ins.then_inc(s_evac.sem, 1)

                act.wait_ge(s_rs.sem, s_rs.at(0, L, 1))
                with act.Fori(0, 2) as i:
                    for c in range(2):
                        his(0, L, i, 2 * c + 2, 2 * c + 3)
                        project(i, c)
                for c in range(4, CH1):
                    his(0, L, 0, 2 * c + 2, 2 * c + 3)
                    project(0, c, COLS if c < 6 else LAST1)

                act.wait_ge(s_lf.sem, s_lf.at(0, L, 1))
                act_(LF[:, 1], LF[:, 1], ACT.Exp).then_inc(s_lg.sem, 1)
                act.wait_ge(s_lf.sem, s_lf.at(0, L, 2))
                act_(LF[:, 2], LF[:, 2], ACT.Ln).then_inc(s_lg.sem, 1)
                turn_copy(0, L, T_QK, 21, QT)
                for m in range(TILES):
                    n = (m + 1) * P
                    act.wait_ge(s_dot.sem, s_dot.at(0, L, m + 1))
                    act.wait_ge(s_rlf.sem, s_rlf.at(0, L, m))
                    for g in range(2):
                        ins = act_(RL[:, 4 * g:4 * g + 4, 0:n], G[:, :, g * S:g * S + n], ACT.Relu)
                    ins.then_inc(s_rl.sem, 1)
                for q in range(len(JOBS1)):
                    exps(0, L, q, JOBS1, PR)
                root(0, L, 2, 1, 8)

                turn_hi(0, L, 0, T_MIX, KB, XH)

                def squares(k, c, bank, used):
                    act.wait_ge(s_used.sem, s_used.at(0, L, used))
                    for m in range(TILES):
                        ins = act_(room(8192, 2, TILES, COLS)[:, c, m], pair(bank)[:, m, :], ACT.Square,
                                   accum_out=stat[:, 0, k, 2 * c + m:2 * c + m + 1])
                    return ins

                his(0, L, 0, U_OUT + 2, U_OUT + 3)
                squares(2, 0, 1, U_OUT + 2)
                his(0, L, 0, U_OUT + 4, U_OUT + 5)
                squares(2, 1, 0, U_OUT + 4).then_inc(s_ss.sem, 1)
                root(0, L, 3, 2, 2)

                turn_hi(0, L, 0, T_N2, KB, XH, gain=prec[:, 1])
                act.wait_ge(s_x.sem, s_x.at(0, L, 1))
                for m in range(TILES):
                    ins = act_(room(12288, TILES, DM)[:, m], X[:, m, :], ACT.Square, accum_out=stat[:, 0, 3, m:m + 1])
                ins.then_inc(s_ss.sem, 1)
                root(0, L, 4, 3, 2)
                act.wait_ge(s_rs.sem, s_rs.at(0, L, 2))

                def inner(i, j, used):
                    act.wait_ge(s_used.sem, s_used.at(0, L, 4 * i + used))
                    for m in range(TILES):
                        ins = act_(H[:, m, :], G[:, m, :], ACT.Relu, scale=stat[:, 2, 3, m:m + 1])
                    ins.then_inc(s_act.sem, 1)

                inner(0, 0, U_MLP + 2)
                his(0, L, 0, U_MLP + 2, U_MLP + 3)
                turn_hi(0, L, 0, T_MLP, UK, MH)
                with act.Fori(0, 7) as i:
                    his(0, L, i, U_MLP + 4, U_MLP + 5)
                    inner(i, 1, U_MLP + 4)
                    his(0, L, i, U_MLP + 6, U_MLP + 7)
                    turn_hi(0, L, i, T_MLP + 2, UK, MH)
                his(0, L, 0, U_PLE, U_PLE + 1)
                turn_hi(0, L, 0, T_P, 2, YH, per=1)
                squares(4, 0, 1, U_PLE - 1)
                squares(4, 1, 2, U_PLE).then_inc(s_ss.sem, 1)
                root(0, L, 5, 4, 2)

                his(0, L, 0, U_PLE + 2, U_PLE + 3)
                for n in range(2):
                    act.wait_ge(s_used.sem, s_used.at(0, L, U_PLE + 1 + n))
                    act_(PP[:, :, n * COLS:(n + 1) * COLS], pair(n), ACT.Copy).then_inc(s_pp.sem, 1)
                turn_hi(0, L, 0, T_PX, KB, XH)
                his(0, L, 0, U_PLE + 4, U_PLE + 5)
                for n in range(2):
                    act.wait_ge(s_used.sem, s_used.at(0, L, U_PLE + 4 + 2 * n))
                    act.wait_ge(s_sgf.sem, s_sgf.at(0, L, n))
                    act_(SG, pair(n), ACT.Sigmoid).then_inc(s_sg.sem, 1)

            with act.Fori(0, DEPTH) as L:
                his(1, L, 0, 0, 1)
                turn_hi(1, L, 0, 0, KB, XH)
                with act.Fori(0, 2) as i:
                    his(1, L, i, 2, 3, 4, 5)
                his(1, L, 0, 10, 11, 12, 13, 14, 15)
                turn_copy(1, L, T2_QK, 18, QT2)
                for q in range(len(JOBS2)):
                    exps(1, L, q, JOBS2, PR2)
                turn_hi(1, L, 0, T2_YA, 3, MH, per=1)
                with act.Fori(0, 4) as i:
                    his(1, L, i, V_RET + 2, V_RET + 3, V_RET + 4, V_RET + 5)
                turn_copy(1, L, T2_RET, 16, QTR)
                root(1, L, 1, 0, 4)
                root(1, L, 2, 1, 4)

                def gate(i, c, first, func, buf):
                    act.wait_ge(s_evac.sem, s_evac.at(1, L, 2 * i + c + 1))
                    act_(*buf, func).then_inc(s_sz.sem, 1)

                with act.Fori(0, 2) as i:
                    for c in range(2):
                        his(1, L, i, V_GATE + 2 + 2 * c, V_GATE + 3 + 2 * c)
                        gate(i, 15 + c, True, ACT.Silu, (SZ, GZ))
                for c in range(19, 23):
                    his(1, L, 0, 2 * c + 2, 2 * c + 3)
                    gt = VR[:, :, (c - 19) * COLS:(c - 18) * COLS]
                    gate(0, c, False, ACT.Sigmoid, (gt, gt))

                turn_hi(1, L, 0, T2_YB, 4, XH)
                hi(1, L, 0, V_RP)
                turn_hi(1, L, 0, T2_YB + 2, 4, XH[:, 4:8])
                hi(1, L, 0, V_RP + 1)
                turn_hi(1, L, 0, T2_YB + 4, 8, YH)
                his(1, L, 0, *range(V_RP + 2, V_OUT + 2))
                turn_hi(1, L, 0, T2_M, KB, XH)
                his(1, L, 0, *range(V_OUT + 2, V_FFN + 2))
                root(1, L, 3, 2, 2)

                turn_hi(1, L, 0, T2_FX, KB, XH)

                def inner2(i, j, used):
                    act.wait_ge(s_used.sem, s_used.at(1, L, 4 * i + used))
                    act_(H2, G[:, 0:2, 0:256], ACT.Silu).then_inc(s_act.sem, 1)

                inner2(0, 0, V_FFN + 2)
                his(1, L, 0, V_FFN + 2, V_FFN + 3)
                turn_hi(1, L, 0, T2_FFN, 2, MH, per=1)
                with act.Fori(0, FJ - 2) as i:
                    his(1, L, i, V_FFN + 4, V_FFN + 5)
                    inner2(i, 1, V_FFN + 4)
                    his(1, L, i, V_FFN + 6, V_FFN + 7)
                    turn_hi(1, L, i, T2_FFN + 2, 2, MH, per=1)
                e = 4 * (FJ - 2)
                his(1, L, 0, V_FFN + 4 + e, V_FFN + 5 + e)
                inner2(0, FJ - 1, V_FFN + 4 + e)
                his(1, L, 0, V_FFN + 6 + e, V_FFN + 7 + e)
                turn_hi(1, L, 0, T2_FFN + 2 * (FJ - 1), 2, MH, per=1)
                root(1, L, 4, 3, 2)

        @block.vector
        def _(dve):
            tt, ts, stt = nc.vector.tensor_tensor, nc.vector.tensor_scalar, nc.vector.scalar_tensor_tensor

            def lo(blk, L, i, c):
                n, slot = size(blk, c), c % RAW
                dve.wait_ge(s_hi.sem, s_hi.at(blk, L, 4 * i + c + 1))
                tt(wlo[:, c % PARTS, 0:n], raw[:, slot, 0:n], whi[:, c % PARTS, 0:n].bitcast(F32),
                   ALU.subtract).then_inc(s_lo.sem, 1)

            def los(blk, L, i, *cs):
                for c in cs:
                    lo(blk, L, i, c)

            def turn_lo(blk, L, i, t, n, hx, lx, per=2, gain=None):
                for b in range(0, n, per):
                    tt_ = t + b // per
                    dve.wait_ge(s_thi.sem, s_thi.at(blk, L, 2 * i + split_no(blk, tt_) + 1))
                    k = min(per, n - b)
                    src = T[:, tt_ % 2, 0:k * S].rearrange("p (k s) -> p k s", s=S)
                    if gain is None:
                        ins = tt(lx[:, b:b + k, :], src, hx[:, b:b + k, :].bitcast(F32), ALU.subtract)
                    else:
                        for kk in range(k):
                            ins = stt(out=lx[:, b + kk, :], in0=src[:, kk, :], scalar=gain[:, b + kk:b + kk + 1],
                                      in1=hx[:, b + kk, :].bitcast(F32), op0=ALU.mult, op1=ALU.subtract)
                    ins.then_inc(s_tfree.sem, 1)

            def mean(norm, n, width, halves=False):
                if halves:
                    tt(stat[:, 0, norm, 0:n], stat[:, 0, norm, 0:n], stat[:, 0, norm, n:2 * n], ALU.add)
                    dve.drain()
                return ts(stat[:, 0, norm, 0:n], stat[:, 0, norm, 0:n], 1.0 / width, EPS, ALU.mult, ALU.add)

            def invert(blk, L, k, norm, n):
                dve.wait_ge(s_sd.sem, s_sd.at(blk, L, k))
                return nc.vector.reciprocal(stat[:, 2, norm, 0:n], stat[:, 1, norm, 0:n])

            def prep(blk, L, q, jobs):
                kind, m, _ = jobs[q]
                n = (m + 1) * P
                dve.wait_ge(s_log.sem, s_log.at(blk, L, q + 1))
                if kind == "E":
                    nc.vector.tensor_reduce(mx[:, q, 0:1], logit_set(q)[:, 0:3, 0:n], AX.XY, ALU.max)
                    dve.drain()
                    ts(nm[:, q, 0:1], mx[:, q, 0:1], -SCALE[kind], None, ALU.mult).then_inc(s_nm.sem, 1)
                    return
                g = G[:, 2 * (q % 2):2 * (q % 2) + 2, :].rearrange("p b (h s) -> p h b s", s=S)
                nc.vector.tensor_reduce(mx[:, q, :].rearrange("p (h b) -> p h b", b=2), g[:, :, :, 0:n], AX.X, ALU.max)
                dve.drain()
                if kind == "D":
                    tt(mx[:, q, :], mx[:, q, :], cur[:, 8:12], ALU.max)
                    dve.drain()
                ins = ts(nm[:, q, :], mx[:, q, :], -SCALE[kind], None, ALU.mult)
                if kind == "D":
                    dve.drain()
                    ins = tt(ds_[:, q, :], cur[:, 4:8], nm[:, q, :], ALU.add)
                ins.then_inc(s_nm.sem, 1)

            def copy_turned(blk, L, q, jobs, t0, dst):
                kind, m, _ = jobs[q]
                w = (3 if kind == "E" else 4) * P
                for kt in range(m + 1):
                    t = t0 + job_banks(jobs, q) + kt
                    dve.wait_ge(s_t.sem, s_t.at(blk, L, t + 1))
                    nc.vector.tensor_copy(dst[:, q % 2, kt, 0:w], T[:, t % 2, 0:w]).then_inc(s_tfree.sem, 1)

            def outputs(blk, L, q, jobs):
                kind, m, x = jobs[q]
                dve.wait_ge(s_pv.sem, s_pv.at(blk, L, q + 1))
                if kind == "E":
                    nc.vector.reciprocal(rl[:, q, 0:1], ls[:, q, 0:1])
                    dve.drain()
                    ts(Z2[:, m, x * HD:(x + 1) * HD], A[:, q % 2, 0:HD], rl[:, q, 0:1], None,
                       ALU.mult).then_inc(s_o.sem, 1)
                    return
                if kind == "D":
                    tt(ls[:, q, :], ls[:, q, :], es[:, q, :], ALU.add)
                    dve.drain()
                nc.vector.reciprocal(rl[:, q, :], ls[:, q, :])
                dve.drain()
                src = A[:, q % 2, 0:4 * HD].rearrange("p (u d) -> p u d", d=HD)
                by = rl[:, q, :].unsqueeze(2).to_broadcast([P, 4, HD])
                if kind != "C":
                    dst = Z[:, m, MIX0 + MIXCOL[kind]:MIX0 + MIXCOL[kind] + 4 * HD].rearrange("p (u d) -> p u d", d=HD)
                    tt(dst, src, by, ALU.mult).then_inc(s_o.sem, 1)
                    return
                odd = rl[:, q, :].rearrange("p (h m) -> p h m", m=2)[:, :, 1]
                ts(odd, odd, cur[:, 12:13], -1.0, ALU.mult, ALU.mult)
                dve.drain()
                both = SCO[:].rearrange("p (u d) -> p u d", d=HD)
                tt(both, src, by, ALU.mult)
                dve.drain()
                two = SCO[:].rearrange("p (h m d) -> p h m d", m=2, d=HD)
                tt(CO[:, m, :, :].rearrange("p (h x) d -> p h x d", x=2)[:, :, x, :], two[:, :, 0, :], two[:, :, 1, :], ALU.add).then_inc(s_o.sem, 1)

            def run_jobs(blk, L, jobs, t0, dst):
                for q in range(len(jobs) + 2):
                    if q < len(jobs):
                        prep(blk, L, q, jobs)
                    if 1 <= q <= len(jobs):
                        copy_turned(blk, L, q - 1, jobs, t0, dst)
                    if q >= 2:
                        outputs(blk, L, q - 2, jobs)

            for t in (s_lo, s_tfree, s_evac, s_rlf, s_o, s_sgf, s_yr):
                dve.sem_inc(t.sem, t.credit)
            dve.wait_ge(s_xin, 16)
            dve.sem_inc(s_x.sem, 1)
            dve.wait_ge(s_const, 16 * N_CONST)
            for n in range(2):
                tt(lamv[:, n * 128:n * 128 + 64], lamv[:, n * 128:n * 128 + 64], lamv[:, n * 128 + 64:n * 128 + 128], ALU.mult)
            dve.drain()
            for n in range(2):
                ins = nc.vector.tensor_reduce(lsum[:, 2 * n:2 * n + 2], lamv[:, n * 128:n * 128 + 64].rearrange(
                    "p (l d) -> p l d", d=32), AX.X, ALU.add)
            ins.then_inc(s_tab, 1)
            nc.vector.tensor_copy(identb[:], ident[:])
            nc.vector.tensor_copy(maskb[:], room(0, 2, P))
            nc.vector.tensor_copy(posf[:], posi[:])
            dve.drain()
            turns, part = room(2600, TILES, 96), room(2800, TILES, 96)
            for m in range(TILES):
                ts(sind[:, m, :], freq[:], posf[:, m:m + 1], None, ALU.mult)
            dve.drain()
            magic = 12582912.0
            ts(turns, sind[:], 1.0 / (2 * math.pi), magic, ALU.mult, ALU.add)
            dve.drain()
            ts(turns, turns, magic, None, ALU.subtract)
            dve.drain()
            c1 = 6.28125
            c2 = float(np.float32(round((2 * math.pi - c1) * 2 ** 21) / 2 ** 21))
            for c in (c1, c2, 2 * math.pi - c1 - c2):
                stt(out=sind[:], in0=turns, scalar=-c, in1=sind[:], op0=ALU.mult, op1=ALU.add)
                dve.drain()
            ts(sind[:], sind[:], 3.1415925, -3.1415925, ALU.min, ALU.max)
            dve.drain()
            stt(out=part, in0=sind[:], scalar=-1.0, in1=sind[:], op0=ALU.mult, op1=ALU.max)
            dve.drain()
            ts(cosd[:], part, -1.0, math.pi / 2, ALU.mult, ALU.add).then_inc(s_tab, 1)
            dve.wait_ge(s_sin, 1)
            ts(sind[:, :, 0:32], sind[:, :, 0:32], -1.0, None, ALU.mult)
            ts(sind[:, :, 64:80], sind[:, :, 64:80], -1.0, None, ALU.mult)
            dve.wait_ge(s_le, 1)
            tt(lam, lsum[:, 0:2], lsum[:, 2:4], ALU.subtract)
            dve.drain()
            tt(lam, lam, lamc[:, 0:2], ALU.add)
            for n in range(DEPTH):
                ts(subln[:, n * HD:(n + 1) * HD], subln[:, n * HD:(n + 1) * HD], lamc[:, 2 + n:3 + n], None, ALU.mult)
            ok = arena[0:18, 1024:2048].rearrange("p (a b) -> p a b", a=2)
            rowsb = arena[0:18, 2048:2560]
            dve.wait_ge(s_bmm, 1)
            tt(rowsb, T[0:18, 0, :], ok[:, 0], ALU.mult)
            dve.drain()
            tt(rowsb, rowsb, ok[:, 1], ALU.add).then_inc(s_bvec, 1)

            def rope(col, heads, d, tab):
                h = d // 2
                x = Z[:, :, col:col + heads * d].rearrange("p m (h d) -> p m h d", d=d)
                u = RT[:, 0:heads * d].rearrange("p (h d) -> p h d", d=d)
                for m in range(TILES):
                    sin = lambda a_, b_: sind[:, m, tab + a_:tab + b_].unsqueeze(1).to_broadcast([P, heads, b_ - a_])
                    cos = cosd[:, m, tab:tab + d].unsqueeze(1).to_broadcast([P, heads, d])
                    tt(u[:, :, 0:h], x[:, m, :, h:d], sin(0, h), ALU.mult)
                    tt(u[:, :, h:d], x[:, m, :, 0:h], sin(h, d), ALU.mult)
                    dve.drain()
                    tt(x[:, m], x[:, m], cos, ALU.mult)
                    dve.drain()
                    ins = tt(x[:, m], x[:, m], u, ALU.add)
                    dve.drain()
                return ins

            def add_normed(L, norm, row, c, bank):
                for m in range(TILES):
                    stt(out=TMP[:, m, :], in0=pair(bank)[:, m, :], scalar=stat[:, 2, norm, m:m + 1],
                        in1=gains[:, row, c * COLS:(c + 1) * COLS], op0=ALU.mult, op1=ALU.mult)
                dve.drain()
                ins = tt(X[:, :, c * COLS:(c + 1) * COLS], X[:, :, c * COLS:(c + 1) * COLS], TMP, ALU.add)
                dve.drain()
                return ins

            with dve.Fori(0, DEPTH) as L:
                nc.vector.tensor_copy(cur[:, 0:4], bforget[:, bass.ds(L * 4, 4)])
                nc.vector.tensor_copy(cur[:, 4:8], sink[:, bass.ds(L * 4, 4)])
                nc.vector.tensor_copy(cur[:, 12:13], lam[:, bass.ds(L, 1)])
                nc.vector.tensor_copy(cur[:, 16:80], subln[:, bass.ds(L * HD, HD)])
                nc.vector.tensor_copy(prec[:], pre[:, :, bass.ds(L, 1), :].rearrange("p n l k -> p (n l) k"))
                dve.drain()
                ts(cur[:, 8:12], cur[:, 4:8], 1.0 / SCALE["D"], None, ALU.mult).then_inc(s_cur.sem, 1)

                turn_lo(0, L, 0, 0, KB, XH, XL, gain=prec[:, 0])
                los(0, L, 0, 0, 1)
                dve.wait_ge(s_ss.sem, s_ss.at(0, L, 1))
                mean(0, 2, DM).then_inc(s_ms.sem, 1)
                invert(0, L, 1, 0, 2).then_inc(s_rs.sem, 1)

                with dve.Fori(0, 2) as i:
                    los(0, L, i, 2, 3, 4, 5)
                los(0, L, 0, 10, 11)
                dve.wait_ge(s_evac.sem, s_evac.at(0, L, 3))
                rope(A_Q, 8, HD, 0)
                los(0, L, 0, 12, 13)
                rope(A_IQ, 9, HD, 0)
                nc.vector.tensor_copy(DUP[:, :, 0:HD], Z[:, :, A_IK:A_IK + HD])
                nc.vector.tensor_copy(DUP[:, :, HD:P], Z[:, :, A_IK:A_IK + HD])
                ts(IW[:], Z[:, :, A_IW:A_IW + IDX_HEADS], IDX_HEADS ** -0.5 * HD ** -0.5, None, ALU.mult)
                los(0, L, 0, 14, 15)
                dve.wait_ge(s_evac.sem, s_evac.at(0, L, 5))
                tt(LF[:, 0], Z[:, :, B_F:B_F + 4], cur[:, 0:4].unsqueeze(1).to_broadcast([P, TILES, 4]), ALU.add)
                dve.drain()
                stt(out=LF[:, 1], in0=LF[:, 0], scalar=-1.0, in1=LF[:, 0], op0=ALU.mult, op1=ALU.min).then_inc(s_lf.sem, 1)
                ts(LF[:, 3], LF[:, 0], 0.0, None, ALU.min)
                dve.wait_ge(s_evac.sem, s_evac.at(0, L, 6))
                rope(C_Q, 16, 32, 64)
                dve.wait_ge(s_evac.sem, s_evac.at(0, L, CH1))
                rope(D_Q, 6, HD, 0)
                for kv in range(2):
                    for r in range(2):
                        ins = nc.vector.tensor_copy(DUP[:, :, P + (2 * kv + r) * HD:P + (2 * kv + r + 1) * HD],
                                                    Z[:, :, D_K + kv * HD:D_K + (kv + 1) * HD])
                ins.then_inc(s_dup.sem, 4)
                dve.wait_ge(s_lg.sem, s_lg.at(0, L, 1))
                ts(LF[:, 2], LF[:, 1], 1.0, None, ALU.add).then_inc(s_lf.sem, 1)
                dve.wait_ge(s_lg.sem, s_lg.at(0, L, 2))
                tt(LF[:, 3], LF[:, 3], LF[:, 2], ALU.subtract)
                dve.drain()
                ts(LF[:, 4], LF[:, 3], -1.0 / SCALE["B"], None, ALU.mult).then_inc(s_lf.sem, 1)

                for m in range(TILES):
                    n = (m + 1) * P
                    sc = SCO[:, 0:n]
                    dve.drain()
                    dve.wait_ge(s_rl.sem, s_rl.at(0, L, m + 1))
                    ts(sc, RL[:, 0, 0:n], IW[:, m, 0:1], None, ALU.mult)
                    for h in range(1, IDX_HEADS):
                        dve.drain()
                        ins = stt(out=sc, in0=RL[:, h, 0:n], scalar=IW[:, m, h:h + 1], in1=sc, op0=ALU.mult, op1=ALU.add)
                    ins.then_inc(s_rlf.sem, 1)
                    dve.drain()
                    tt(sc, sc, causal[:, m, 0:n], ALU.add)
                    for _ in range(TOPK // 8):
                        dve.drain()
                        nc.vector.max(m8[:], sc)
                        dve.drain()
                        nc.vector.match_replace(out=sc, in_to_replace=m8[:], in_values=sc, imm_value=TAKEN)
                    dve.drain()
                    ts(sc, sc, TAKEN / 2, NEG, ALU.is_gt, ALU.mult)
                    dve.drain()
                    tt(amask[:, m, 0:n], sc, causal[:, m, 0:n], ALU.min).then_inc(s_am.sem, 1)

                run_jobs(0, L, JOBS1, T_JOB, PT)
                dve.drain()
                tt(CS, CO, CO, ALU.mult)
                dve.drain()
                nc.vector.tensor_reduce(stat[:, 0, 1, :], CS.rearrange("p m h d -> p (m h) d"), AX.X, ALU.add)
                dve.drain()
                mean(1, 8, HD).then_inc(s_ms.sem, 1)
                invert(0, L, 2, 1, 8)
                dve.drain()
                co = CO.rearrange("p m h d -> p (m h) d")
                tt(co, co, stat[:, 2, 1, :].unsqueeze(2).to_broadcast([P, 8, HD]), ALU.mult)
                dve.drain()
                c0 = MIX0 + MIXCOL["C"]
                for m in range(TILES):
                    ins = tt(Z[:, m, c0:c0 + 256].rearrange("p (h d) -> p h d", d=HD), CO[:, m],
                             cur[:, 16:80].unsqueeze(1).to_broadcast([P, 4, HD]), ALU.mult)
                ins.then_inc(s_mix.sem, 1)

                turn_lo(0, L, 0, T_MIX, KB, XH, XL)
                los(0, L, 0, U_OUT + 2, U_OUT + 3, U_OUT + 4, U_OUT + 5)
                dve.wait_ge(s_ss.sem, s_ss.at(0, L, 2))
                mean(2, 2, DM, halves=True).then_inc(s_ms.sem, 1)
                invert(0, L, 3, 2, 2)
                dve.drain()
                dve.wait_ge(s_gain.sem, s_gain.at(0, L, 2))
                add_normed(L, 2, 0, 0, 1)
                add_normed(L, 2, 0, 1, 0).then_inc(s_x.sem, 1)

                turn_lo(0, L, 0, T_N2, KB, XH, XL, gain=prec[:, 1])
                dve.wait_ge(s_ss.sem, s_ss.at(0, L, 3))
                mean(3, 2, DM).then_inc(s_ms.sem, 1)
                invert(0, L, 4, 3, 2).then_inc(s_rs.sem, 1)
                dve.drain()

                def inner(i, j):
                    dve.wait_ge(s_act.sem, s_act.at(0, L, i + j + 1))
                    for m in range(TILES):
                        ins = stt(out=H[:, m, :], in0=G[:, m, :], scalar=stat[:, 2, 3, m:m + 1], in1=H[:, m, :],
                                  op0=ALU.mult, op1=ALU.mult)
                    ins.then_inc(s_h.sem, 1)

                inner(0, 0)
                los(0, L, 0, U_MLP + 2, U_MLP + 3)
                turn_lo(0, L, 0, T_MLP, UK, MH, ML)
                with dve.Fori(0, 7) as i:
                    los(0, L, i, U_MLP + 4, U_MLP + 5)
                    inner(i, 1)
                    los(0, L, i, U_MLP + 6, U_MLP + 7)
                    turn_lo(0, L, i, T_MLP + 2, UK, MH, ML)
                los(0, L, 0, U_PLE, U_PLE + 1)
                turn_lo(0, L, 0, T_P, 2, YH, YL, per=1)
                dve.wait_ge(s_ss.sem, s_ss.at(0, L, 4))
                mean(4, 2, DM, halves=True).then_inc(s_ms.sem, 1)
                invert(0, L, 5, 4, 2)
                dve.drain()
                add_normed(L, 4, 1, 0, 1)
                add_normed(L, 4, 1, 1, 2).then_inc(s_x.sem, 1)

                los(0, L, 0, U_PLE + 2, U_PLE + 3)
                turn_lo(0, L, 0, T_PX, KB, XH, XL)
                los(0, L, 0, U_PLE + 4, U_PLE + 5)
                for n in range(2):
                    dve.wait_ge(s_sg.sem, s_sg.at(0, L, n + 1))
                    cols = slice(n * COLS, (n + 1) * COLS)
                    tt(TMP, SG, PP[:, :, cols], ALU.mult).then_inc(s_sgf.sem, 1)
                    dve.drain()
                    ins = tt(X[:, :, cols], X[:, :, cols], TMP, ALU.add)
                    dve.drain()
                ins.then_inc(s_x.sem, 1)

            with dve.Fori(0, DEPTH) as L:
                turn_lo(1, L, 0, 0, KB, XH, XL)
                los(1, L, 0, 0, 1)

                def project(i, c, dst, cols=COLS):
                    dve.wait_ge(s_used.sem, s_used.at(1, L, 4 * i + 2 * c + 2))
                    dve.wait_ge(s_bin[c % 2].sem, s_bin[c % 2].at(1, L, i + c // 2 + 1))
                    tt(dst, pair(c % 2)[:, :, 0:cols], BIN[:, c % 2, 0:cols].unsqueeze(1).to_broadcast([P, TILES, cols]),
                       ALU.add).then_inc(s_evac.sem, 1)

                with dve.Fori(0, 2) as i:
                    for c in range(2):
                        los(1, L, i, 2 * c + 2, 2 * c + 3)
                        project(i, c, Z2[:, :, bass.ds(i * 1024 + c * COLS, COLS)])
                for c in range(4, SEG1):
                    los(1, L, 0, 2 * c + 2, 2 * c + 3)
                    cols = COLS if c < 6 else LAST2
                    project(0, c, Z2[:, :, c * COLS:c * COLS + cols], cols)
                run_jobs(1, L, JOBS2, T2_JOB, PT2)
                turn_lo(1, L, 0, T2_YA, 3, MH, ML, per=1)

                def rotate(i, c):
                    x = QK[:, :, bass.ds(i * 1024 + c * COLS, COLS)].rearrange("p m (h e d) -> p m h e d", e=2, d=P)
                    x1, x2 = x[:, :, :, 0], x[:, :, :, 1]
                    cos, sin = (rot[:, n].unsqueeze(2).to_broadcast([P, TILES, 2, P]) for n in range(2))
                    u = RTR[:]
                    tt(u[:, 0], x2, sin, ALU.mult)
                    tt(u[:, 1], x1, sin, ALU.mult)
                    dve.drain()
                    tt(x1, x1, cos, ALU.mult)
                    tt(x2, x2, cos, ALU.mult)
                    dve.drain()
                    tt(x1, x1, u[:, 0], ALU.subtract)
                    ins = tt(x2, x2, u[:, 1], ALU.add)
                    return ins

                with dve.Fori(0, 2) as i:
                    for c in range(2):
                        los(1, L, i, V_RET + 2 + 2 * c, V_RET + 3 + 2 * c)
                        project(i, SEG1 + c, QK[:, :, bass.ds(i * 1024 + c * COLS, COLS)])
                        dve.drain()
                        rotate(i, c).then_inc(s_rot.sem, 1)
                with dve.Fori(0, 2) as i:
                    for c in range(2):
                        los(1, L, i, V_RET + 10 + 2 * c, V_RET + 11 + 2 * c)
                        project(i, SEG1 + 4 + c, VR[:, :, bass.ds(i * 1024 + c * COLS, COLS)])

                def decayed(h):
                    dve.wait_ge(s_sc.sem, s_sc.at(1, L, h + 1))
                    tt(SCT[:, h % 2, 0:S], A[:, h % 2, 0:S], decay[:, h].rearrange("p a b -> p (a b)"), ALU.mult)
                    tt(SCT[:, h % 2, S:S + P], A[:, h % 2, S:S + P], decay[:, h, 0], ALU.mult).then_inc(s_sd2.sem, 1)

                def moments(h):
                    dve.wait_ge(s_ro.sem, s_ro.at(1, L, h + 1))
                    for m in range(TILES):
                        nc.vector.bn_stats(bns[:, 2 * (h % 2) + m, :], G[:, 2 * (h % 2) + m, :])

                def normalise(r):
                    dve.drain()
                    for n in range(4):
                        nc.vector.bn_aggr(bna[:, n, :], bns[:, n, :])
                    dve.drain()
                    ts(stat[:, 0, r, 0:4], bna[:, :, 1], LN_EPS, None, ALU.add).then_inc(s_ms.sem, 1)
                    invert(1, L, r + 1, r, 4)
                    dve.drain()
                    for n in range(4):
                        h, m = 2 * r + n // 2, n % 2
                        ins = ts(QK[:, m, h * RDV:(h + 1) * RDV], G[:, n, :], bna[:, n, 0:1], stat[:, 2, r, n:n + 1],
                                 ALU.subtract, ALU.mult)
                    ins.then_inc(s_yr.sem, 1)

                decayed(0)
                decayed(1)
                moments(0)
                moments(1)
                decayed(2)
                decayed(3)
                normalise(0)
                moments(2)
                moments(3)
                normalise(1)

                with dve.Fori(0, 2) as i:
                    for c in range(2):
                        los(1, L, i, V_GATE + 2 + 2 * c, V_GATE + 3 + 2 * c)
                        project(i, 15 + c, GZ)
                        dve.wait_ge(s_sz.sem, s_sz.at(1, L, 2 * i + c + 1))
                        y = QK[:, :, bass.ds(i * 1024 + c * COLS, COLS)]
                        tt(y, y, SZ, ALU.mult).then_inc(s_yb.sem, 1)
                for c in range(19, 23):
                    los(1, L, 0, 2 * c + 2, 2 * c + 3)
                    project(0, c, VR[:, :, (c - 19) * COLS:(c - 18) * COLS])

                turn_lo(1, L, 0, T2_YB, 4, XH, XL)
                lo(1, L, 0, V_RP)
                dve.wait_ge(s_sz.sem, s_sz.at(1, L, 8))

                def gated(n, used, gate_col, dst):
                    dve.wait_ge(s_used.sem, s_used.at(1, L, used))
                    tt(dst, pair(1 - n), VR[:, :, gate_col + n * COLS:gate_col + (n + 1) * COLS],
                       ALU.mult).then_inc(s_evac.sem, 1)

                gated(0, V_AP + 1, 0, M[:, :, 0:COLS])
                turn_lo(1, L, 0, T2_YB + 2, 4, XH[:, 4:8], XL[:, 4:8])
                lo(1, L, 0, V_RP + 1)
                gated(1, V_AP + 2, 0, M[:, :, COLS:DM])
                turn_lo(1, L, 0, T2_YB + 4, 8, YH, YL)
                for n in range(2):
                    los(1, L, 0, *range(V_RP + 2 + 4 * n, V_RP + 6 + 4 * n))
                    gated(n, V_RP + 4 + 4 * n, DM, TMP2)
                    dve.drain()
                    mc = M[:, :, n * COLS:(n + 1) * COLS]
                    ins = tt(mc, mc, TMP2, ALU.add)
                    dve.drain()
                ins.then_inc(s_m.sem, 1)
                turn_lo(1, L, 0, T2_M, KB, XH, XL)

                def residual(c, bank):
                    xc = X[:, :, c * COLS:(c + 1) * COLS]
                    ins = stt(out=xc, in0=xc, scalar=ALPHA, in1=pair(bank), op0=ALU.mult, op1=ALU.add)
                    dve.drain()
                    for m in range(TILES):
                        nc.vector.bn_stats(bns[:, 2 * m + c, :], X[:, m, c * COLS:(c + 1) * COLS])
                    return ins

                def layer_norm(k, norm, gain):
                    dve.drain()
                    for m in range(TILES):
                        nc.vector.bn_aggr(bna[:, m, :], bns[:, 2 * m:2 * m + 2, :].rearrange("p a b -> p (a b)"))
                    dve.drain()
                    ts(stat[:, 0, norm, 0:2], bna[:, 0:2, 1], LN_EPS, None, ALU.add).then_inc(s_ms.sem, 1)
                    dve.wait_ge(s_gain.sem, s_gain.at(1, L, gain))
                    for m in range(TILES):
                        stt(out=X[:, m], in0=X[:, m], scalar=bna[:, m, 0:1], in1=gains[:, 0], op0=ALU.subtract, op1=ALU.mult)
                    invert(1, L, k, norm, 2)
                    dve.drain()
                    for m in range(TILES):
                        ins = stt(out=X[:, m], in0=X[:, m], scalar=stat[:, 2, norm, m:m + 1], in1=gains[:, 1],
                                  op0=ALU.mult, op1=ALU.add)
                    ins.then_inc(s_x.sem, 1)

                los(1, L, 0, V_OUT + 2, V_OUT + 3)
                dve.wait_ge(s_used.sem, s_used.at(1, L, V_OUT + 2))
                residual(0, 1).then_inc(s_evac.sem, 1)
                los(1, L, 0, V_OUT + 4, V_OUT + 5)
                dve.wait_ge(s_used.sem, s_used.at(1, L, V_OUT + 4))
                residual(1, 0).then_inc(s_evac.sem, 1)
                layer_norm(3, 2, 2)

                turn_lo(1, L, 0, T2_FX, KB, XH, XL)

                def inner2(i, j):
                    dve.wait_ge(s_act.sem, s_act.at(1, L, i + j + 1))
                    tt(H2, H2, G[:, 0:2, 256:512], ALU.mult).then_inc(s_h.sem, 1)

                inner2(0, 0)
                los(1, L, 0, V_FFN + 2, V_FFN + 3)
                turn_lo(1, L, 0, T2_FFN, 2, MH, ML, per=1)
                with dve.Fori(0, FJ - 2) as i:
                    los(1, L, i, V_FFN + 4, V_FFN + 5)
                    inner2(i, 1)
                    los(1, L, i, V_FFN + 6, V_FFN + 7)
                    turn_lo(1, L, i, T2_FFN + 2, 2, MH, ML, per=1)
                e = 4 * (FJ - 2)
                los(1, L, 0, V_FFN + 4 + e, V_FFN + 5 + e)
                inner2(0, FJ - 1)
                los(1, L, 0, V_FFN + 6 + e, V_FFN + 7 + e)
                turn_lo(1, L, 0, T2_FFN + 2 * (FJ - 1), 2, MH, ML, per=1)
                for c in range(2):
                    dve.wait_ge(s_used.sem, s_used.at(1, L, UNITS2 - 1 + c))
                    residual(c, 1 + c)
                layer_norm(4, 3, 4)


def kernel(**inputs):
    import concourse.bacc as bacc
    from concourse.bass_utils import run_bass_kernel_spmd

    nc = bacc.Bacc("TRN2", target_bir_lowering=False, num_devices=1)
    arrays = {f"in_{k}": np.ascontiguousarray(v) for k, v in {**inputs, **constants()}.items()}
    a = {k[3:]: nc.dram_tensor(k, v.shape, mybir.dt.from_np(v.dtype), kind="ExternalInput").ap()
         for k, v in arrays.items()}
    out = nc.dram_tensor("out", (1, S, DM), F32, kind="ExternalOutput").ap()
    program(nc, a, out)
    return run_bass_kernel_spmd(nc, [arrays], core_ids=[0]).results[0]["out"]
```

```python
import math
from contextlib import ExitStack

import numpy as np

import concourse.bass as bass
from concourse import mybir

F32 = mybir.dt.float32
F32R = mybir.dt.float32r
BF16 = mybir.dt.bfloat16
I32 = mybir.dt.int32
ALU = mybir.AluOpType
ACT = mybir.ActivationFunctionType
AX = mybir.AxisListType

P = 128
DM = 1024
S = 256
TILES = S // P
DEPTH = 2
KB = DM // P
COLS = 512
UK = 4
UNIT = UK * COLS
RAW = 4
PARTS = 2
HD = 64
EPS = 1e-6
LN_EPS = 1e-5
NEG = -1e30
TAKEN = -3e38
TOPK = 64
ALPHA = (2 * DEPTH) ** 0.25

A_Q, A_K, A_V, A_IQ, A_IK, A_IW = 0, 256, 512, 768, 1280, 1344
B_Q, B_K, B_V, B_F = 1352, 1608, 1864, 2120
C_Q, C_K, C_V = 2124, 2380, 2636
D_Q, D_K, D_V = 2892, 3148, 3276
D_IN = 3404
CH1 = 7
LAST1 = D_IN - 6 * COLS
D_FF = 4096
D_PLE = 256
IDX_HEADS = 8
MIX0 = A_IQ

ATTN_W = 1152
HG = 6
GROUPS = ((128, 1), (512, 4), (2048, 16))
RQ0 = 3 * ATTN_W
SEG1 = 7
LAST2 = RQ0 - 6 * COLS
IN2 = 11648
RH, RDV = 4, 512
YA_W = 384
D_FF2 = 2816
FJ = D_FF2 // 256

U_OUT, U_MLP, U_PLE, UNITS1 = 14, 18, 50, 56
V_RET, V_GATE, V_AP, V_RP, V_OUT, V_FFN, UNITS2 = 14, 30, 46, 48, 56, 60, 104

T_QK, T_JOB, T_MIX, T_N2, T_MLP, T_P, T_PX, TS1 = 4, 15, 30, 34, 38, 54, 56, 60
T2_QK, T2_JOB, T2_YA, T2_RET, T2_YB, T2_M, T2_FX, T2_FFN, TS2 = 4, 13, 31, 34, 42, 50, 54, 58, 80

JOBS1 = [("C", 0, 0), ("C", 0, 1), ("C", 1, 0), ("C", 1, 1), ("B", 0, 0), ("B", 1, 0),
         ("A", 0, 0), ("A", 1, 0), ("D", 0, 0), ("D", 1, 0)]
JOBS2 = [("E", m, h) for h in range(HG) for m in range(TILES)]
MIXCOL = {"A": 0, "B": 256, "C": 512, "D": 768}
SCALE = {"A": HD ** -0.5, "B": HD ** -0.5, "C": (HD // 2) ** -0.5, "D": HD ** -0.5, "E": HD ** -0.5}


def job_banks(jobs, q):
    return sum(m + 1 for _, m, _ in jobs[:q])


def split_no(blk, t):
    if blk == 0:
        return t if t <= T_QK else t - (T_MIX - T_QK)
    if t <= T2_QK:
        return t
    return t - (T2_YA - T2_QK) - (0 if t <= T2_RET else T2_YB - T2_RET)


class Tally:

    def __init__(self, sem, per, credit=0, step=1):
        self.sem, self.per, self.credit, self.step = sem, per, credit, step

    def at(self, blk, layer, k):
        base = self.credit + (DEPTH * self.per[0] if blk else 0)
        return layer * (self.per[blk] * self.step) + (k + base) * self.step


def constants():
    i = np.arange(P)
    c = {}
    ident = np.eye(P, dtype=np.float32)
    tri = (np.arange(S)[:, None] <= np.arange(S)[None, :]).astype(np.float32)
    causal = np.where(np.arange(S)[None, :] <= np.arange(S)[:, None], 0.0, NEG).astype(np.float32)
    tile_rows = lambda a: np.ascontiguousarray(a.reshape(TILES, P, -1).transpose(1, 0, 2))
    c["c_ident"] = ident
    c["c_flip"] = np.ascontiguousarray(ident[::-1])
    c["c_tri"] = tile_rows(tri)
    c["c_causal"] = tile_rows(causal)
    c["c_masks"] = np.stack([np.where(i[None] <= i[:, None], 0.0, NEG),
                             np.where(i[None] > i[:, None], 0.0, NEG)], 1).astype(np.float32)
    gam = np.log(1.0 - 2.0 ** (-5.0 - np.arange(RH)))
    diff = i[None, :] - i[:, None]
    diag = np.where(diff >= 0, np.exp(gam[:, None, None] * np.maximum(diff, 0)), 0.0)
    off = np.exp(gam[:, None, None] * (diff + P))
    c["c_decay"] = np.ascontiguousarray(
        (np.stack([diag, off], 1) / 16.0).transpose(2, 0, 1, 3)).astype(np.float32)
    inv = (np.float32(10000.0) ** (-np.arange(P, dtype=np.float32) / np.float32(P))).astype(np.float32)
    ang = (np.arange(S, dtype=np.float32)[:, None] * inv[None]).astype(np.float64)
    c["c_rot"] = np.ascontiguousarray(np.stack([tile_rows(np.cos(ang)), tile_rows(np.sin(ang))], 1)).astype(np.float32)
    f64 = (np.float32(10000.0) ** (-np.arange(32, dtype=np.float32) / np.float32(32))).astype(np.float32)
    f32 = (np.float32(10000.0) ** (-np.arange(16, dtype=np.float32) / np.float32(16))).astype(np.float32)
    c["c_freq"] = np.concatenate([f64, f64, f32, f32]).astype(np.float32)
    dist = 255 - np.arange(512)
    d = np.maximum(dist, 0)
    large = 16 + (np.log(np.maximum(d, 16) / 16) / np.log(2048 / 16) * 16).astype(np.int32)
    bucket = np.where(d < 16, d, np.minimum(large, 31))
    onehot = (np.arange(32)[:, None] == bucket[None]).astype(np.float32) * np.float32(HD ** 0.5)
    ok = np.concatenate([np.tile((dist >= 0) & (d <= w) & (d % s == 0), (HG, 1)) for w, s in GROUPS])
    c["c_onehot"] = onehot
    c["c_ok"] = np.stack([ok.astype(np.float32), np.where(ok, 0.0, NEG).astype(np.float32)], 1)
    lam0 = np.array([0.8 - 0.6 * math.exp(-0.3 * n) for n in range(DEPTH)])
    c["c_lam"] = np.concatenate([lam0, 1.0 - lam0]).astype(np.float32)
    return c


def program(nc, a, out):
    bias_rows = nc.dram_tensor("bias_rows", (18, 512), F32, kind="Internal").ap()

    with ExitStack() as ctx:
        def sb(name, shape, dt=F32):
            return ctx.enter_context(nc.sbuf_tensor(name, shape, dt))

        def psum(name, shape):
            return ctx.enter_context(nc.psum_tensor(name, shape, F32))

        def sem(name):
            return ctx.enter_context(nc.semaphore(name))

        raw = sb("raw", [P, RAW, UNIT])
        whi = sb("whi", [P, PARTS, UNIT], F32R)
        wlo = sb("wlo", [P, PARTS, UNIT], F32R)
        X = sb("X", [P, TILES, DM])
        XH = sb("XH", [P, KB, S], F32R)
        XL = sb("XL", [P, KB, S], F32R)
        MH = sb("MH", [P, UK, S], F32R)
        ML = sb("ML", [P, UK, S], F32R)
        YH = sb("YH", [P, KB, S], F32R)
        YL = sb("YL", [P, KB, S], F32R)
        gains = sb("gains", [P, 2, DM])
        arena = sb("arena", [P, 17100])

        def room(lo, *dims):
            n = int(np.prod(dims))
            ap = arena[:, lo:lo + n]
            if len(dims) == 1:
                return ap
            names = "abcd"[:len(dims)]
            kw = {names[i]: dims[i] for i in range(1, len(dims))}
            return ap.rearrange(f"p ({' '.join(names)}) -> p {' '.join(names)}", **kw)

        Z = room(0, TILES, D_IN)
        DUP = room(6808, TILES, 384)
        QT = room(7576, 21, S)
        PR = room(12952, 2, 4, S)
        PT = room(15000, 2, TILES, 512)
        RL = room(12952, IDX_HEADS, S)
        RT = room(15000, 1152)
        RTP = room(16152, 512)
        CO = room(6808, TILES, 4, HD)
        CS = room(7576, TILES, 4, HD)
        NG = room(10240, TILES, DM)
        H = room(0, TILES, COLS)
        TMP = room(2048, TILES, COLS)
        PP = room(4096, TILES, DM)
        SG = room(8192, TILES, COLS)
        PB = room(9216, TILES, D_PLE)
        Z2 = room(0, TILES, RQ0)
        QT2 = room(6912, 18, S)
        PR2 = room(11520, 2, 3, S)
        PT2 = room(13056, 2, TILES, 384)
        BR = room(14592, 2, 3, S)
        QK = room(0, TILES, 2048)
        VR = room(4096, TILES, 2048)
        QTR = room(8192, 16, S)
        SCT = room(12288, RH, 384)
        RTR = room(13056, 2, TILES, 2, P)
        GZ = room(8192, TILES, COLS)
        SZ = room(9216, TILES, COLS)
        M = room(10240, TILES, DM)
        TMP2 = room(12288, TILES, COLS)
        H2 = room(0, TILES, 256)
        swap = sb("swap", [P, 2, COLS])
        BIN = swap[:]
        tri = swap[:, 0].rearrange("p (m s) -> p m s", m=TILES)
        causal = swap[:, 1].rearrange("p (m s) -> p m s", m=TILES)

        ident = sb("ident", [P, P])
        flip = sb("flip", [P, P])
        identb = sb("identb", [P, P], BF16)
        maskb = sb("maskb", [P, 2, P], BF16)
        amask = sb("amask", [P, TILES, S], BF16)
        decay = sb("decay", [P, RH, 2, P])
        rot = sb("rot", [P, 2, TILES, P])
        cosd = sb("cosd", [P, TILES, 96])
        sind = sb("sind", [P, TILES, 96])
        freq = sb("freq", [P, 96])
        posi = sb("posi", [P, TILES], I32)
        posf = sb("posf", [P, TILES])
        small = sb("small", [P, 424])
        bforget, sink = small[:, 0:8], small[:, 8:16]
        subln, lamv, lamc = small[:, 16:144], small[:, 144:400], small[:, 400:404]
        lsum, lam = small[:, 404:408], small[:, 408:410]
        cur = sb("cur", [P, 90])
        pre = sb("pre", [P, 2, DEPTH, KB])
        prec = sb("prec", [P, 2, KB])
        stat = sb("stat", [P, 3, 5, 8])
        mx, nm, ls = (sb(n, [P, 12, 4]) for n in ("mx", "nm", "ls"))
        rl, es, ds_ = (sb(n, [P, 12, 4]) for n in ("rl", "es", "ds_"))
        IW = sb("IW", [P, TILES, IDX_HEADS])
        SCO = sb("SCO", [P, S])
        m8 = sb("m8", [P, 8])
        LF = sb("LF", [P, 5, TILES, 4])
        bns = sb("bns", [P, 4, 6])
        bna = sb("bna", [P, 4, 2])

        G = psum("G", [P, 4, 512])
        T = psum("T", [P, 2, 512])
        A = psum("A", [P, 2, 512])

        s_raw = [Tally(sem(f"s_raw{n}"), (UNITS1 // RAW, UNITS2 // RAW + more), step=16)
                 for n, more in enumerate((1, 1, FJ - 1, FJ - 1))]
        s_hi = Tally(sem("s_hi"), (UNITS1, UNITS2))
        s_lo = Tally(sem("s_lo"), (UNITS1, UNITS2), credit=RAW)
        s_used = Tally(sem("s_used"), (UNITS1, UNITS2), credit=PARTS)
        s_evac = Tally(sem("s_evac"), (CH1, 29), credit=2)
        s_t = Tally(sem("s_t"), (TS1, TS2))
        s_thi = Tally(sem("s_thi"), (TS1 - 26, TS2 - 35))
        s_tfree = Tally(sem("s_tfree"), (TS1, TS2), credit=2)
        s_x = Tally(sem("s_x"), (3, 2), credit=1)
        s_xh = Tally(sem("s_xh"), (3, 2), credit=1)
        s_ng = Tally(sem("s_ng"), (8, 0))
        s_sq = Tally(sem("s_sq"), (8, 0))
        s_ss = Tally(sem("s_ss"), (2, 0))
        s_ms = Tally(sem("s_ms"), (5, 6))
        s_sd = Tally(sem("s_sd"), (5, 6))
        s_rs = Tally(sem("s_rs"), (2, 0))
        s_cur = Tally(sem("s_cur"), (1, 0))
        s_rope = Tally(sem("s_rope"), (2, 0))
        s_prope = Tally(sem("s_prope"), (3, 0))
        s_lf = Tally(sem("s_lf"), (3, 0))
        s_lg = Tally(sem("s_lg"), (2, 0))
        s_dot = Tally(sem("s_dot"), (3, 0))
        s_rl = Tally(sem("s_rl"), (3, 0))
        s_rlf = Tally(sem("s_rlf"), (2, 0), credit=1)
        s_am = Tally(sem("s_am"), (2, 0))
        s_log = Tally(sem("s_log"), (len(JOBS1), len(JOBS2)))
        s_nm = Tally(sem("s_nm"), (len(JOBS1), len(JOBS2)))
        s_exp = Tally(sem("s_exp"), (len(JOBS1), len(JOBS2)), credit=2)
        s_pv = Tally(sem("s_pv"), (len(JOBS1), len(JOBS2)))
        s_o = Tally(sem("s_o"), (len(JOBS1), len(JOBS2)), credit=2)
        s_mix = Tally(sem("s_mix"), (1, 0))
        s_act = Tally(sem("s_act"), (8, FJ))
        s_h = Tally(sem("s_h"), (8, FJ))
        s_gain = Tally(sem("s_gain"), (2, 4), step=16)
        s_p = Tally(sem("s_p"), (1, 0), step=16)
        s_pp = Tally(sem("s_pp"), (2, 0))
        s_sg = Tally(sem("s_sg"), (2, 0))
        s_sgf = Tally(sem("s_sgf"), (2, 0), credit=1)
        s_bin = [Tally(sem(f"s_bin{n}"), (0, n0), step=16) for n, n0 in ((0, 12), (1, 11))]
        s_br = [Tally(sem(f"s_br{n}"), (0, 6), step=16) for n in (0, 1)]
        s_rot = Tally(sem("s_rot"), (0, 4))
        s_sc = Tally(sem("s_sc"), (0, RH))
        s_sd2 = Tally(sem("s_sd2"), (0, RH))
        s_ro = Tally(sem("s_ro"), (0, RH))
        s_yr = Tally(sem("s_yr"), (0, RH))
        s_sz = Tally(sem("s_sz"), (0, 8))
        s_m = Tally(sem("s_m"), (0, 2))
        s_yb = Tally(sem("s_yb"), (0, 4))
        s_xin = sem("s_xin")
        s_const = sem("s_const")
        s_tab = sem("s_tab")
        s_sin = sem("s_sin")
        s_bmm = sem("s_bmm")
        s_bvec = sem("s_bvec")
        s_brow = sem("s_brow")
        s_le = sem("s_le")
        s_out = sem("s_out")

        block = ctx.enter_context(nc.Block())
        N_CONST = 22

        @block.sync
        def _(sp):
            def unit(blk, L, u, src, kb, cols, slot):
                sp.wait_ge(s_lo.sem, s_lo.at(blk, L, u - RAW + 1))
                dst = raw[:, slot, 0:kb * cols].rearrange("p (k n) -> p k n", n=cols)
                return sp.dma_start(dst, src).then_inc(s_raw[slot].sem, 16)

            def rows(w, L, r0, kb, c0, cols):
                return w[bass.ds(L, 1), r0:r0 + kb * P, :][:, :, bass.ds(c0, cols)].rearrange(
                    "l (k p) n -> p (l k) n", p=P)

            n_const = 0
            sp.dma_start(X[:], a["x"].rearrange("b (m p) d -> p (b m) d", p=P)).then_inc(s_xin, 16)

            def const(dst, src):
                sp.dma_start(dst, src).then_inc(s_const, 16)

            with nc.allow_non_contiguous_dma(reason="small parameters"):
                const(ident[:], a["c_ident"])
                const(flip[:], a["c_flip"])
                const(tri, a["c_tri"])
                const(causal, a["c_causal"])
                const(decay[:], a["c_decay"])
                const(rot[:], a["c_rot"])
                const(freq[:], a["c_freq"].partition_broadcast(P))
                const(posi[:], a["positions"].rearrange("b (m p) -> p (b m)", p=P))
                const(room(0, 2, P), a["c_masks"])
                const(arena[0:32, 256:274], a["rel_bias_2"])
                const(arena[0:32, 512:1024], a["c_onehot"])
                const(arena[0:18, 1024:2048].rearrange("p (a b) -> p a b", a=2), a["c_ok"])
                const(bforget, a["b_forget"].rearrange("l n -> (l n)").partition_broadcast(P))
                const(sink, a["sinks"].rearrange("l n -> (l n)").partition_broadcast(P))
                const(subln, a["diff_subln"].rearrange("l n -> (l n)").partition_broadcast(P))
                for n, name in enumerate(("lambda_q1", "lambda_k1", "lambda_q2", "lambda_k2")):
                    const(lamv[:, n * 64:n * 64 + 64], a[name].rearrange("l n -> (l n)").partition_broadcast(P))
                const(lamc, a["c_lam"].partition_broadcast(P))
                for n, name in enumerate(("norm_pre_mix", "norm_pre_mlp")):
                    sp.dma_start(pre[:, n], a[name].rearrange("l (k p) -> p l k", p=P)).then_inc(s_const, 16)
            sp.wait_ge(s_bvec, 1)
            sp.dma_start(bias_rows, arena[0:18, 2048:2560]).then_inc(s_brow, 16)

            with sp.Fori(0, DEPTH) as L:
                w = a["w_in"]
                with sp.Fori(0, 3) as i:
                    for c in range(2):
                        for k in range(2):
                            u = 2 * c + k
                            unit(0, L, 4 * i + u, rows(w, L, 512 * k, UK, i * 1024 + c * COLS, COLS), UK, COLS, u)
                for k in range(2):
                    unit(0, L, 12 + k, rows(w, L, 512 * k, UK, 6 * COLS, LAST1), UK, LAST1, k)
                sp.wait_ge(s_x.sem, s_x.at(0, L, 0))
                for n, name in enumerate(("norm_post_mix", "norm_post_mlp")):
                    sp.dma_start(gains[:, n:n + 1, :], a[name][bass.ds(L, 1), :].partition_broadcast(P)).then_inc(
                        s_gain.sem, 16)
                w = a["w_out"]
                for n in range(4):
                    u = U_OUT + n
                    unit(0, L, u, rows(w, L, 512 * (n // 2), UK, n % 2 * COLS, COLS), UK, COLS, u % RAW)
                up, down = a["w_mlp_up"], a["w_mlp_down"]
                for k in range(2):
                    unit(0, L, U_MLP + k, rows(up, L, 512 * k, UK, 0, COLS), UK, COLS, (U_MLP + k) % RAW)
                with sp.Fori(0, 7) as i:
                    for k in range(2):
                        unit(0, L, 4 * i + U_MLP + 2 + k, rows(up, L, 512 * k, UK, i * COLS + COLS, COLS),
                             UK, COLS, (U_MLP + 2 + k) % RAW)
                    for n in range(2):
                        src = down[bass.ds(L, 1)][:, bass.ds(i * COLS, COLS), n * COLS:(n + 1) * COLS].rearrange(
                            "l (k p) n -> p (l k) n", p=P)
                        unit(0, L, 4 * i + U_MLP + 4 + n, src, UK, COLS, (U_MLP + 4 + n) % RAW)
                sp.wait_ge(s_x.sem, s_x.at(0, L, 1))
                sp.dma_start(PB[:], a["p"][bass.ds(L, 1)].rearrange("l b (m p) d -> p (l b m) d", p=P)).then_inc(
                    s_p.sem, 16)
                for n in range(2):
                    unit(0, L, U_MLP + 30 + n, rows(down, L, 7 * COLS, UK, n * COLS, COLS), UK, COLS, (U_MLP + 30 + n) % RAW)
                for n in range(2):
                    unit(0, L, U_PLE + n, rows(a["w_ple_proj"], L, 0, 2, n * COLS, COLS), 2, COLS, (U_PLE + n) % RAW)
                for n in range(4):
                    u = U_PLE + 2 + n
                    unit(0, L, u, rows(a["w_ple_gate"], L, 512 * (n % 2), UK, n // 2 * COLS, COLS), UK, COLS, u % RAW)

            sp.wait_ge(s_mix.sem, s_mix.at(0, DEPTH, 0))
            with sp.Fori(0, DEPTH) as L:
                w = a["w_in_2"]

                def bias_in(c, c0, cols, slot):
                    sp.wait_ge(s_evac.sem, s_evac.at(1, L, c - 1))
                    src = a["b_in_2"][bass.ds(L, 1), :][:, bass.ds(c0, cols)].partition_broadcast(P)
                    sp.dma_start(BIN[:, slot:slot + 1, 0:cols], src).then_inc(s_bin[slot].sem, 16)

                def w_in_chunks(i, u0, c0, col0, chunks=2):
                    for c in range(chunks):
                        for k in range(2):
                            u = 2 * c + k
                            unit(1, L, 4 * i + u0 + u, rows(w, L, 512 * k, UK, i * 1024 + (col0 + c * COLS), COLS),
                                 UK, COLS, (u0 + u) % RAW)
                        bias_in(2 * i + c0 + c, i * 1024 + (col0 + c * COLS), COLS, (c0 + c) % 2)

                with sp.Fori(0, 3) as i:
                    w_in_chunks(i, 0, 0, 0)
                for k in range(2):
                    unit(1, L, 12 + k, rows(w, L, 512 * k, UK, 6 * COLS, LAST2), UK, LAST2, k)
                bias_in(6, 6 * COLS, LAST2, 0)
                sp.wait_ge(s_x.sem, s_x.at(1, L, 0))
                for n, name in enumerate(("ln1_g_2", "ln1_b_2")):
                    sp.dma_start(gains[:, n:n + 1, :], a[name][bass.ds(L, 1), :].partition_broadcast(P)).then_inc(
                        s_gain.sem, 16)
                w_in_chunks(0, V_RET, 7, RQ0, 1)
                sp.wait_ge(s_brow, 16)
                sp.wait_ge(s_t.sem, s_t.at(1, L, T2_QK))
                for q, (_, m, h) in enumerate(JOBS2):
                    if q >= 2:
                        sp.wait_ge(s_log.sem, s_log.at(1, L, q - 1))
                    n = (m + 1) * P
                    src = bass.AP(bias_rows.tensor, h * 512 + (1 - m) * P, [[1, P], [HG * 512, 3], [1, n]])
                    sp.dma_start(BR[:, q % 2, :, 0:n], src).then_inc(s_br[q % 2].sem, 16)
                with sp.Fori(0, 3) as i:
                    w_in_chunks(i, V_RET + 2, 8, RQ0 + COLS)
                w_in_chunks(0, V_RET + 14, 14, RQ0 + 7 * COLS, 1)
                with sp.Fori(0, 4) as i:
                    w_in_chunks(i, V_GATE, 15, RQ0 + 8 * COLS)
                for n in range(2):
                    unit(1, L, V_AP + n, rows(a["w_attn_proj_2"], L, 0, 3, n * COLS, COLS), 3, COLS, (V_AP + n) % RAW)
                for n in range(8):
                    u = V_RP + n
                    unit(1, L, u, rows(a["w_ret_proj_2"], L, 512 * (n % 4), UK, n // 4 * COLS, COLS), UK, COLS, u % RAW)
                for n in range(4):
                    u = V_OUT + n
                    unit(1, L, u, rows(a["w_out_2"], L, 512 * (n // 2), UK, n % 2 * COLS, COLS), UK, COLS, u % RAW)

                gate, up, down = a["w_ffn_gate_2"], a["w_ffn_up_2"], a["w_ffn_down_2"]

                def gate_up(j, u, k, slot):
                    sp.wait_ge(s_lo.sem, s_lo.at(1, L, u - RAW + 1))
                    dst = raw[:, slot].rearrange("p (k g n) -> p k g n", k=UK, g=2)
                    for g, wt in enumerate((gate, up)):
                        src = wt[bass.ds(L, 1), 512 * k:512 * k + 512, :][:, :, bass.ds(j * 256, 256)].rearrange(
                            "l (k p) n -> p (l k) n", p=P)
                        sp.dma_start(dst[:, :, g, :], src).then_inc(s_raw[slot].sem, 16)

                for k in range(2):
                    gate_up(0, V_FFN + k, k, (V_FFN + k) % RAW)
                with sp.Fori(0, FJ - 1) as i:
                    for k in range(2):
                        gate_up(i + 1, 4 * i + V_FFN + 2 + k, k, (V_FFN + 2 + k) % RAW)
                    for n in range(2):
                        src = down[bass.ds(L, 1)][:, bass.ds(i * 256, 256), n * COLS:(n + 1) * COLS].rearrange(
                            "l (k p) n -> p (l k) n", p=P)
                        unit(1, L, 4 * i + V_FFN + 4 + n, src, 2, COLS, (V_FFN + 4 + n) % RAW)
                for n in range(2):
                    unit(1, L, V_FFN + 42 + n, rows(down, L, (FJ - 1) * 256, 2, n * COLS, COLS), 2, COLS,
                         (V_FFN + 42 + n) % RAW)
                sp.wait_ge(s_x.sem, s_x.at(1, L, 1))
                for n, name in enumerate(("ln2_g_2", "ln2_b_2")):
                    sp.dma_start(gains[:, n:n + 1, :], a[name][bass.ds(L, 1), :].partition_broadcast(P)).then_inc(
                        s_gain.sem, 16)
            sp.wait_ge(s_x.sem, s_x.at(1, DEPTH, 0))
            sp.dma_start(out.rearrange("b (m p) d -> p (b m) d", p=P), X[:]).then_inc(s_out, 16)
            sp.wait_ge(s_out, 16)

        def landed(blk, L, i, c):
            o, slot = i + c // RAW, c % RAW
            k = o + 1
            if blk and c >= V_FFN:
                if slot < 2:
                    k = o + 2
                elif c >= UNITS2 - 2:
                    k = o + FJ
                else:
                    k = o * 2 - (2 * (V_FFN // RAW) - 17)
            return s_raw[slot].at(blk, L, k)

        def size(blk, c):
            if blk == 0:
                return UK * LAST1 if c in (12, 13) else 2 * COLS if c in (50, 51) else UNIT
            if c in (12, 13):
                return UK * LAST2
            if c in (V_AP, V_AP + 1):
                return 3 * COLS
            small_unit = c >= UNITS2 - 2 or (c >= V_FFN + 4 and c % RAW < 2)
            return 2 * COLS if small_unit else UNIT

        def logit_set(q):
            g = G[:, 2 * (q % 2):2 * (q % 2) + 2, :]
            return g.rearrange("p b (u s) -> p (b u) s", s=S)

        def logit(q, u):
            return G[:, 2 * (q % 2) + u % 2, u // 2 * S:(u // 2 + 1) * S]

        def rope(eng, engine, scratch, col, heads, d, tab):
            h = d // 2
            x = Z[:, :, col:col + heads * d].rearrange("p m (h d) -> p m h d", d=d)
            u = scratch[:, 0:TILES * heads * d].rearrange("p (m h d) -> p m h d", m=TILES, d=d)
            sin = lambda a_, b_: sind[:, :, tab + a_:tab + b_].unsqueeze(2).to_broadcast([P, TILES, heads, b_ - a_])
            cos = cosd[:, :, tab:tab + d].unsqueeze(2).to_broadcast([P, TILES, heads, d])
            engine.tensor_tensor(u[:, :, :, 0:h], x[:, :, :, h:d], sin(0, h), ALU.mult)
            engine.tensor_tensor(u[:, :, :, h:d], x[:, :, :, 0:h], sin(h, d), ALU.mult)
            eng.drain()
            engine.tensor_tensor(x, x, cos, ALU.mult)
            eng.drain()
            return engine.tensor_tensor(x, x, u, ALU.add)

        def pair(n):
            return A[:, :, :] if n == 2 else G[:, 2 * n:2 * n + 2, :]

        @block.tensor
        def _(pe):
            def unit(blk, L, i, c, hx, lx, k0, kb, cols, dst, first, last):
                hi = whi[:, c % PARTS, 0:kb * cols].rearrange("p (k n) -> p k n", n=cols)
                lo = wlo[:, c % PARTS, 0:kb * cols].rearrange("p (k n) -> p k n", n=cols)
                pe.wait_ge(s_hi.sem, s_hi.at(blk, L, 4 * i + c + 1))
                for k in range(kb):
                    for m in range(TILES):
                        rows = slice(m * P, (m + 1) * P)
                        nc.tensor.matmul(dst(m), hx[:, k0 + k, rows], hi[:, k, :], start=first and k == 0, stop=False)
                        nc.tensor.matmul(dst(m), lx[:, k0 + k, rows], hi[:, k, :], start=False, stop=False)
                pe.wait_ge(s_lo.sem, s_lo.at(blk, L, 4 * i + c + 1))
                for k in range(kb):
                    for m in range(TILES):
                        mm = nc.tensor.matmul(dst(m), hx[:, k0 + k, m * P:(m + 1) * P], lo[:, k, :],
                                              start=False, stop=last and k == kb - 1)
                mm.then_inc(s_used.sem, 1)

            def bank_pair(n, cols=COLS):
                return lambda m: pair(n)[:, m, 0:cols]

            def chunk(blk, L, i, c, group, cols=COLS, hx=XH, lx=XL):
                for k in range(2):
                    unit(blk, L, i, c + k, hx, lx, UK * k, UK, cols, bank_pair(group, cols), k == 0, k == 1)

            def transposes(blk, L, i, t, blocks):
                pe.wait_ge(s_tfree.sem, s_tfree.at(blk, L, 2 * i + t - 1))
                for n, src in enumerate(blocks):
                    tr = nc.tensor.transpose(T[:, t % 2, n * P:(n + 1) * P], src, ident[:])
                tr.then_inc(s_t.sem, 1)

            def both(src, blocks):
                return [src[:, m, b * P:(b + 1) * P] for b in blocks for m in range(TILES)]

            def turn_x(blk, L, t, src, xh, x):
                pe.wait_ge(xh[0].sem, xh[0].at(blk, L, xh[1]))
                turn(blk, L, 0, t, src, UK)
                pe.wait_ge(x[0].sem, x[0].at(blk, L, x[1]))
                turn(blk, L, 0, t + 2, src[:, :, UK * P:DM], UK)

            def first_chunk(blk, L, c, t, group=0):
                for k in range(2):
                    pe.wait_ge(s_tfree.sem, s_tfree.at(blk, L, t + 2 + 2 * k))
                    unit(blk, L, 0, c + k, XH, XL, UK * k, UK, COLS, bank_pair(group), k == 0, k == 1)

            def turn(blk, L, i, t, src, nblocks, per=2):
                for b in range(0, nblocks, per):
                    transposes(blk, L, i, t + b // per, both(src, range(b, min(b + per, nblocks))))

            def job_outputs(blk, L, q, jobs, t0):
                kind, m, x = jobs[q]
                pe.wait_ge(s_tfree.sem, s_tfree.at(blk, L, t0 + job_banks(jobs, q + 1)))
                pe.wait_ge(s_o.sem, s_o.at(blk, L, q - 1))
                for u in range(3 if kind == "E" else 4):
                    for kt in range(m + 1):
                        if kind == "E":
                            v = Z2[:, kt, 2 * ATTN_W + (u * HG + x) * HD:][:, 0:HD]
                            mm = nc.tensor.matmul(A[:, q % 2, 0:HD], PT2[:, q % 2, kt, u * P:(u + 1) * P], v,
                                                  start=(u == 0 and kt == 0), stop=(u == 2 and kt == m))
                        else:
                            col = {"A": A_V + u * HD, "B": B_V + u * HD, "D": D_V + u // 2 * HD,
                                   "C": C_V + (2 * (u // 2) + x) * HD}[kind]
                            mm = nc.tensor.matmul(A[:, q % 2, u * HD:(u + 1) * HD], PT[:, q % 2, kt, u * P:(u + 1) * P],
                                                  Z[:, kt, col:col + HD], start=kt == 0, stop=kt == m)
                mm.then_inc(s_pv.sem, 1)

            def job_turn(blk, L, q, jobs, t0, probs):
                kind, m, _ = jobs[q]
                pe.wait_ge(s_exp.sem, s_exp.at(blk, L, q + 1))
                for kt in range(m + 1):
                    t = t0 + job_banks(jobs, q) + kt
                    transposes(blk, L, 0, t, [probs[:, q % 2, u, kt * P:(kt + 1) * P]
                                              for u in range(3 if kind == "E" else 4)])

            pe.wait_ge(s_const, 16 * N_CONST)
            nc.tensor.matmul(T[0:18, 0, :], arena[0:32, 256:274], arena[0:32, 512:1024], start=True, stop=True).then_inc(s_bmm, 1)
            pe.sem_inc(s_used.sem, s_used.credit)
            pe.wait_ge(s_bvec, 1)

            def logits1(L, q):
                kind, m, x = JOBS1[q]
                n = (m + 1) * P
                rows = slice(m * P, (m + 1) * P)
                if kind == "A":
                    pe.wait_ge(s_am.sem, s_am.at(0, L, m + 1))
                if kind == "B":
                    pe.wait_ge(s_lf.sem, s_lf.at(0, L, 3))
                pe.wait_ge(s_exp.sem, s_exp.at(0, L, q - 1))
                for u in range(4):
                    dst = logit(q, u)
                    if kind == "C":
                        qb, kb = 13 + u // 2, 15 + u // 2
                        part = slice(32 * (2 * x + u % 2), 32 * (2 * x + u % 2) + 32)
                    else:
                        qb, kb = {"A": (5 + u // 2, 7 + u // 2), "B": (9 + u // 2, 11 + u // 2),
                                  "D": (17 + u // 2, 19 + u // 2)}[kind]
                        part = slice(HD * (u % 2), HD * (u % 2) + HD)
                    nc.tensor.matmul(dst[:, 0:n], QT[part, qb, rows], QT[part, kb, 0:n], start=True, stop=False)
                    if kind == "A":
                        mm = nc.tensor.matmul(dst[:, 0:n], identb[:], amask[:, m, 0:n], start=False, stop=True)
                        continue
                    if kind == "B":
                        for kt in range(m + 1):
                            nc.tensor.matmul(dst[:, kt * P:n], LF[:, 4, kt, u:u + 1].to_broadcast([P, P]),
                                             tri[:, kt, kt * P:n], start=False, stop=False)
                    if kind == "D" and m == 1:
                        nc.tensor.matmul(dst[:, 0:P], identb[:], maskb[:, 1], start=False, stop=False)
                    mm = nc.tensor.matmul(dst[:, m * P:n], identb[:], maskb[:, 0], start=False, stop=True)
                mm.then_inc(s_log.sem, 1)

            def logits2(L, q):
                _, m, h = JOBS2[q]
                n = (m + 1) * P
                part = slice(HD * (h % 2), HD * (h % 2) + HD)
                pe.wait_ge(s_exp.sem, s_exp.at(1, L, q - 1))
                pe.wait_ge(s_br[q % 2].sem, s_br[q % 2].at(1, L, q // 2 + 1))
                dst = logit_set(q)
                for g in range(3):
                    b = 3 * g + h // 2
                    nc.tensor.matmul(dst[:, g, 0:n], QT2[part, b, m * P:(m + 1) * P], QT2[part, 9 + b, 0:n],
                                     start=True, stop=False)
                    mm = nc.tensor.matmul(dst[:, g, 0:n], flip[:], BR[:, q % 2, g, 0:n], start=False, stop=True)
                mm.then_inc(s_log.sem, 1)

            def run_jobs(blk, L, jobs, t0, logits, probs, after_first=None):
                for q in range(len(jobs) + 2):
                    if q == 1 and after_first:
                        after_first()
                    if q < len(jobs):
                        logits(L, q)
                    if 1 <= q <= len(jobs):
                        job_turn(blk, L, q - 1, jobs, t0, probs)
                    if q >= 2:
                        job_outputs(blk, L, q - 2, jobs, t0)

            with pe.Fori(0, DEPTH) as L:
                turn_x(0, L, 0, X, (s_xh, 0), (s_x, 0))
                first_chunk(0, L, 0, 0)
                for c in range(1, 4):
                    pe.wait_ge(s_evac.sem, s_evac.at(0, L, c - 1))
                    chunk(0, L, 0, 2 * c, c % 2)

                zb = lambda col: [Z[:, m, col:col + P] for m in range(TILES)]
                db = lambda col: [DUP[:, m, col:col + P] for m in range(TILES)]

                def turn_qk(t, *blocks):
                    for b in range(0, len(blocks), 2):
                        transposes(0, L, 0, T_QK + t + b // 2, sum(blocks[b:b + 2], []))

                def dots(m, heads, n_dot):
                    n = (m + 1) * P
                    for h in heads:
                        part = slice(HD * (h % 2), HD * (h % 2) + HD)
                        j = (h - heads[0]) // 2
                        mm = nc.tensor.matmul(A[:, h % 2, j * n:(j + 1) * n], QT[part, h // 2, m * P:n],
                                              QT[part, 4, 0:n], start=True, stop=True)
                    mm.then_inc(s_dot.sem, 1)

                def w_in_unit(c, k, cols=COLS):
                    unit(0, L, 0, 2 * c + k, XH, XL, UK * k, UK, cols, bank_pair(c % 2, cols), k == 0, k == 1)

                pe.wait_ge(s_rope.sem, s_rope.at(0, L, 1))
                turn_qk(0, *[zb(A_IQ + n * P) for n in range(4)], db(0))
                pe.wait_ge(s_evac.sem, s_evac.at(0, L, 3))
                w_in_unit(4, 0)
                pe.wait_ge(s_tfree.sem, s_tfree.at(0, L, T_QK + 3))
                dots(0, range(IDX_HEADS), 1)
                w_in_unit(4, 1)
                pe.wait_ge(s_rl.sem, s_rl.at(0, L, 1))
                dots(1, range(4), 2)
                pe.wait_ge(s_prope.sem, s_prope.at(0, L, 1))
                turn_qk(3, zb(A_Q), zb(A_Q + P), zb(A_K), zb(A_K + P))
                pe.wait_ge(s_evac.sem, s_evac.at(0, L, 4))
                w_in_unit(5, 0)
                pe.wait_ge(s_rl.sem, s_rl.at(0, L, 2))
                dots(1, range(4, 8), 3)
                w_in_unit(5, 1)
                turn_qk(5, zb(B_Q), zb(B_Q + P), zb(B_K), zb(B_K + P))
                pe.wait_ge(s_evac.sem, s_evac.at(0, L, 5))
                w_in_unit(6, 0, LAST1)
                w_in_unit(6, 1, LAST1)
                pe.wait_ge(s_prope.sem, s_prope.at(0, L, 2))
                turn_qk(7, zb(C_Q), zb(C_Q + P), zb(C_K), zb(C_K + P))

                def turn_d():
                    pe.wait_ge(s_rope.sem, s_rope.at(0, L, 2))
                    pe.wait_ge(s_prope.sem, s_prope.at(0, L, 3))
                    turn_qk(9, zb(D_Q), zb(D_Q + P), db(P), db(2 * P))

                pe.wait_ge(s_evac.sem, s_evac.at(0, L, CH1))
                pe.wait_ge(s_tfree.sem, s_tfree.at(0, L, T_JOB - 2))
                pe.wait_ge(s_rl.sem, s_rl.at(0, L, 3))
                run_jobs(0, L, JOBS1, T_JOB, logits1, PR, turn_d)

                pe.wait_ge(s_o.sem, s_o.at(0, L, len(JOBS1)))
                turn(0, L, 0, T_MIX, Z[:, :, MIX0:MIX0 + DM], UK)
                pe.wait_ge(s_tfree.sem, s_tfree.at(0, L, T_MIX + 2))
                unit(0, L, 0, U_OUT, XH, XL, 0, UK, COLS, bank_pair(1), True, False)
                pe.wait_ge(s_mix.sem, s_mix.at(0, L, 1))
                turn(0, L, 0, T_MIX + 2, Z[:, :, MIX0 + UK * P:MIX0 + DM], UK)
                unit(0, L, 0, U_OUT + 1, XH, XL, 0, UK, COLS, bank_pair(0), True, False)
                pe.wait_ge(s_tfree.sem, s_tfree.at(0, L, T_N2))
                for n in range(2):
                    unit(0, L, 0, U_OUT + 2 + n, XH, XL, UK, UK, COLS, bank_pair(1 - n), False, True)

                turn_x(0, L, T_N2, X, (s_xh, 1), (s_x, 1))

                def inner_turn(i, j):
                    pe.wait_ge(s_h.sem, s_h.at(0, L, i + j + 1))
                    turn(0, L, i, T_MLP + 2 * j, H, UK)

                def down(i, c, first, last, t):
                    pe.wait_ge(s_tfree.sem, s_tfree.at(0, L, 2 * i + t))
                    for n in range(2):
                        unit(0, L, i, c + n, MH, ML, 0, UK, COLS, bank_pair(1 + n), first, last)

                first_chunk(0, L, U_MLP, T_N2)
                inner_turn(0, 0)
                chunk(0, L, 0, U_MLP + 2, 0)
                down(0, U_MLP + 4, True, False, T_MLP + 2)
                inner_turn(0, 1)
                with pe.Fori(0, 6) as i:
                    chunk(0, L, i, U_MLP + 6, 0)
                    down(i, U_MLP + 8, False, False, T_MLP + 4)
                    inner_turn(i, 2)
                pe.wait_ge(s_p.sem, s_p.at(0, L, 1))
                turn(0, L, 0, T_P, PB, 2, per=1)
                down(0, U_MLP + 30, False, True, T_MLP + 16)

                pe.wait_ge(s_tfree.sem, s_tfree.at(0, L, T_PX))
                unit(0, L, 0, U_PLE, YH, YL, 0, 2, COLS, bank_pair(0), True, True)
                pe.wait_ge(s_sq.sem, s_sq.at(0, L, 6))
                pe.wait_ge(s_ng.sem, s_ng.at(0, L, 6))
                unit(0, L, 0, U_PLE + 1, YH, YL, 0, 2, COLS, bank_pair(1), True, True)
                turn_x(0, L, T_PX, X, (s_xh, 2), (s_x, 2))
                pe.wait_ge(s_pp.sem, s_pp.at(0, L, 1))
                first_chunk(0, L, U_PLE + 2, T_PX)
                pe.wait_ge(s_pp.sem, s_pp.at(0, L, 2))
                chunk(0, L, 0, U_PLE + 4, 1)

            with pe.Fori(0, DEPTH) as L:
                turn_x(1, L, 0, X, (s_xh, 0), (s_x, 0))

                def w_in_chunk(i, c, u):
                    pe.wait_ge(s_evac.sem, s_evac.at(1, L, 2 * i + c - 1))
                    chunk(1, L, i, u, c % 2)

                first_chunk(1, L, 0, 0)
                with pe.Fori(0, 2) as i:
                    for c in range(1, 3):
                        w_in_chunk(i, c, 2 * c)
                w_in_chunk(0, 5, 10)
                pe.wait_ge(s_evac.sem, s_evac.at(1, L, 5))
                chunk(1, L, 0, 12, 0, LAST2)

                pe.wait_ge(s_evac.sem, s_evac.at(1, L, SEG1))
                turn(1, L, 0, T2_QK, Z2, 18)
                pe.wait_ge(s_tfree.sem, s_tfree.at(1, L, T2_JOB))
                run_jobs(1, L, JOBS2, T2_JOB, logits2, PR2)
                pe.wait_ge(s_o.sem, s_o.at(1, L, len(JOBS2)))
                turn(1, L, 0, T2_YA, Z2, 3, per=1)

                def scores(h):
                    for kt in range(TILES):
                        for b in range(2):
                            o = A[:, h % 2, 0:S] if kt == 0 else A[:, h % 2, S:S + P]
                            mm = nc.tensor.matmul(o, QTR[:, 8 + 2 * h + b, kt * P:(kt + 1) * P],
                                                  QTR[:, 2 * h + b, kt * P:S], start=b == 0, stop=b == 1)
                    mm.then_inc(s_sc.sem, 1)

                def outputs(h):
                    v = lambda kt: VR[:, kt, h * RDV:(h + 1) * RDV]
                    nc.tensor.matmul(A[:, 0], SCT[:, h, 0:P], v(0), start=True, stop=True)
                    nc.tensor.matmul(A[:, 1], SCT[:, h, P:S], v(0), start=True, stop=False)
                    nc.tensor.matmul(A[:, 1], SCT[:, h, S:S + P], v(1), start=False, stop=True).then_inc(s_ro.sem, 1)

                with pe.Fori(0, 2) as i:
                    for c in range(2):
                        w_in_chunk(i, SEG1 + c, V_RET + 2 * c)
                w_in_chunk(0, 11, V_RET + 8)
                pe.wait_ge(s_rot.sem, s_rot.at(1, L, 4))
                turn(1, L, 0, T2_RET, QK, 16)
                w_in_chunk(0, 12, V_RET + 10)
                pe.wait_ge(s_tfree.sem, s_tfree.at(1, L, T2_YB))
                scores(0)
                scores(1)
                w_in_chunk(0, 13, V_RET + 12)
                pe.wait_ge(s_sd2.sem, s_sd2.at(1, L, 2))
                scores(2)
                scores(3)
                w_in_chunk(0, 14, V_RET + 14)

                for h in range(RH):
                    c = 15 + h
                    pe.wait_ge(s_evac.sem, s_evac.at(1, L, c - 1))
                    unit(1, L, 0, V_GATE + 2 * h, XH, XL, 0, UK, COLS, bank_pair(c % 2), True, False)
                    if h:
                        pe.wait_ge(s_yr.sem, s_yr.at(1, L, h))
                    else:
                        pe.wait_ge(s_sd2.sem, s_sd2.at(1, L, RH))
                        pe.wait_ge(s_evac.sem, s_evac.at(1, L, 15))
                    outputs(h)
                    unit(1, L, 0, V_GATE + 2 * h + 1, XH, XL, UK, UK, COLS, bank_pair(c % 2), False, True)
                w_in_chunk(0, 19, V_GATE + 8)
                w_in_chunk(0, 20, V_GATE + 10)
                pe.wait_ge(s_yb.sem, s_yb.at(1, L, 4))
                turn(1, L, 0, T2_YB, QK[:, :, DM:], KB)
                w_in_chunk(0, 21, V_GATE + 12)
                w_in_chunk(0, 22, V_GATE + 14)
                for n in range(2):
                    turn(1, L, 0, T2_YB + 4 + 2 * n, QK[:, :, n * COLS:(n + 1) * COLS], UK)
                    pe.wait_ge(s_evac.sem, s_evac.at(1, L, 22 + n))
                    unit(1, L, 0, V_AP + n, MH, ML, 0, 3, COLS, bank_pair(1 - n), True, True)
                pe.wait_ge(s_tfree.sem, s_tfree.at(1, L, T2_M))
                for n in range(2):
                    pe.wait_ge(s_evac.sem, s_evac.at(1, L, 24 + n))
                    for k in range(4):
                        if n == 1 and k == 2:
                            pe.wait_ge(s_m.sem, s_m.at(1, L, 1))
                            turn(1, L, 0, T2_M, M, UK)
                        hx, lx = (XH, XL) if k < 2 else (YH, YL)
                        unit(1, L, 0, V_RP + 4 * n + k, hx, lx, UK * (k % 2), UK, COLS, bank_pair(1 - n), k == 0, k == 3)
                pe.wait_ge(s_tfree.sem, s_tfree.at(1, L, T2_M + 2))
                unit(1, L, 0, V_OUT, XH, XL, 0, UK, COLS, bank_pair(1), True, False)
                pe.wait_ge(s_m.sem, s_m.at(1, L, 2))
                turn(1, L, 0, T2_M + 2, M[:, :, COLS:DM], UK)
                unit(1, L, 0, V_OUT + 1, XH, XL, 0, UK, COLS, bank_pair(0), True, False)
                pe.wait_ge(s_tfree.sem, s_tfree.at(1, L, T2_FX))
                for n in range(2):
                    unit(1, L, 0, V_OUT + 2 + n, XH, XL, UK, UK, COLS, bank_pair(1 - n), False, True)

                turn_x(1, L, T2_FX, X, (s_xh, 1), (s_x, 1))

                def inner_turn2(i, j):
                    pe.wait_ge(s_h.sem, s_h.at(1, L, i + j + 1))
                    turn(1, L, i, T2_FFN + 2 * j, H2, 2, per=1)

                def down2(i, c, first, last, t):
                    pe.wait_ge(s_tfree.sem, s_tfree.at(1, L, 2 * i + t))
                    for n in range(2):
                        unit(1, L, i, c + n, MH, ML, 0, 2, COLS, bank_pair(1 + n), first, last)

                first_chunk(1, L, V_FFN, T2_FX)
                inner_turn2(0, 0)
                chunk(1, L, 0, V_FFN + 2, 0)
                down2(0, V_FFN + 4, True, False, T2_FFN + 2)
                inner_turn2(0, 1)
                with pe.Fori(0, FJ - 2) as i:
                    chunk(1, L, i, V_FFN + 6, 0)
                    down2(i, V_FFN + 8, False, False, T2_FFN + 4)
                    inner_turn2(i, 2)
                down2(0, V_FFN + 42, False, True, T2_FFN + 2 * FJ)

        @block.scalar
        def _(act):
            def act_(out_, in_, func, **kw):
                return nc.scalar.activation(out_, in_, func, **kw)

            def hi(blk, L, i, c):
                n, slot = size(blk, c), c % RAW
                act.wait_ge(s_raw[slot].sem, landed(blk, L, i, c))
                act.wait_ge(s_used.sem, s_used.at(blk, L, 4 * i + c - 1))
                act_(whi[:, c % PARTS, 0:n], raw[:, slot, 0:n], ACT.Copy).then_inc(s_hi.sem, 1)

            def his(blk, L, i, *cs):
                for c in cs:
                    hi(blk, L, i, c)

            def turn_hi(blk, L, i, t, n, dst, per=2, gain=None):
                for b in range(0, n, per):
                    tt = t + b // per
                    act.wait_ge(s_t.sem, s_t.at(blk, L, 2 * i + tt + 1))
                    k = min(per, n - b)
                    src = T[:, tt % 2, 0:k * S].rearrange("p (k s) -> p k s", s=S)
                    if gain is None:
                        ins = act_(dst[:, b:b + k, :], src, ACT.Copy)
                    else:
                        for kk in range(k):
                            ins = act_(dst[:, b + kk, :], src[:, kk, :], ACT.Copy, scale=gain[:, b + kk:b + kk + 1])
                    ins.then_inc(s_thi.sem, 1)

            def turn_copy(blk, L, t, n, dst):
                for b in range(0, n, 2):
                    tt = t + b // 2
                    act.wait_ge(s_t.sem, s_t.at(blk, L, tt + 1))
                    k = min(2, n - b)
                    act_(dst[:, b:b + k, :], T[:, tt % 2, 0:k * S].rearrange("p (k s) -> p k s", s=S),
                         ACT.Copy).then_inc(s_tfree.sem, 1)

            def root(blk, L, k, norm, n):
                act.wait_ge(s_ms.sem, s_ms.at(blk, L, k))
                act_(stat[:, 1, norm, 0:n], stat[:, 0, norm, 0:n], ACT.Sqrt).then_inc(s_sd.sem, 1)

            def exps(blk, L, q, jobs, probs):
                kind, m, _ = jobs[q]
                n = (m + 1) * P
                act.wait_ge(s_nm.sem, s_nm.at(blk, L, q + 1))
                src = logit_set(q)
                if kind == "E":
                    act_(probs[:, q % 2, :, 0:n], src[:, 0:3, 0:n], ACT.Exp, bias=nm[:, q, 0:1], scale=SCALE[kind],
                         accum_out=ls[:, q, 0:1]).then_inc(s_exp.sem, 1)
                    return
                if kind == "D":
                    act_(es[:, q, :], ds_[:, q, :], ACT.Exp)
                for u in range(4):
                    ins = act_(probs[:, q % 2, u, 0:n], logit(q, u)[:, 0:n], ACT.Exp, bias=nm[:, q, u:u + 1],
                               scale=SCALE[kind], accum_out=ls[:, q, u:u + 1])
                ins.then_inc(s_exp.sem, 1)

            act.sem_inc(s_exp.sem, s_exp.credit)
            act.wait_ge(s_tab, 1)
            act_(lsum, lsum, ACT.Exp).then_inc(s_le, 1)
            act.wait_ge(s_tab, 2)
            act_(cosd[:], cosd[:], ACT.Sin)
            act_(sind[:], sind[:], ACT.Sin).then_inc(s_sin, 1)
            act.wait_ge(s_brow, 16)

            with act.Fori(0, DEPTH) as L:
                his(0, L, 0, 0, 1)
                act.wait_ge(s_cur.sem, s_cur.at(0, L, 1))
                turn_hi(0, L, 0, 0, KB, XH, gain=prec[:, 0])
                act.wait_ge(s_x.sem, s_x.at(0, L, 0))
                for m in range(TILES):
                    ins = act_(room(12288, TILES, DM)[:, m], X[:, m, :], ACT.Square, accum_out=stat[:, 0, 0, m:m + 1])
                ins.then_inc(s_ss.sem, 1)
                root(0, L, 1, 0, 2)

                def project(i, c, cols=COLS):
                    act.wait_ge(s_used.sem, s_used.at(0, L, 4 * i + 2 * c + 2))
                    for m in range(TILES):
                        dst = Z[:, m, c * COLS:c * COLS + cols] if isinstance(i, int) else \
                            Z[:, m, bass.ds(i * 1024 + c * COLS, cols)]
                        ins = act_(dst, G[:, 2 * (c % 2) + m, 0:cols], ACT.Copy, scale=stat[:, 2, 0, m:m + 1])
                    ins.then_inc(s_evac.sem, 1)

                act.wait_ge(s_rs.sem, s_rs.at(0, L, 1))
                with act.Fori(0, 2) as i:
                    for c in range(2):
                        his(0, L, i, 2 * c + 2, 2 * c + 3)
                        project(i, c)

                def relus(n_dot, m, heads):
                    n, nj = (m + 1) * P, len(heads) // 2
                    act.wait_ge(s_dot.sem, s_dot.at(0, L, n_dot))
                    act.wait_ge(s_rlf.sem, s_rlf.at(0, L, m))
                    dst = RL[:, heads[0]:heads[0] + len(heads), 0:n].rearrange("p (j b) s -> p b j s", b=2)
                    act_(dst, A[:, :, 0:nj * n].rearrange("p b (j s) -> p b j s", s=n), ACT.Relu).then_inc(s_rl.sem, 1)

                turn_copy(0, L, T_QK, 5, QT)
                hi(0, L, 0, 10)
                relus(1, 0, range(IDX_HEADS))
                hi(0, L, 0, 11)
                project(0, 4)
                relus(2, 1, range(4))
                turn_copy(0, L, T_QK + 3, 4, QT[:, 5:9])
                hi(0, L, 0, 12)
                relus(3, 1, range(4, 8))
                hi(0, L, 0, 13)
                project(0, 5)
                act.wait_ge(s_lf.sem, s_lf.at(0, L, 1))
                act_(LF[:, 1], LF[:, 1], ACT.Exp).then_inc(s_lg.sem, 1)
                turn_copy(0, L, T_QK + 5, 4, QT[:, 9:13])
                project(0, 6, LAST1)
                act.wait_ge(s_lf.sem, s_lf.at(0, L, 2))
                act_(LF[:, 2], LF[:, 2], ACT.Ln).then_inc(s_lg.sem, 1)
                turn_copy(0, L, T_QK + 7, 4, QT[:, 13:17])
                turn_copy(0, L, T_QK + 9, 4, QT[:, 17:21])
                his(0, L, 0, 14, 15)
                for q in range(len(JOBS1)):
                    exps(0, L, q, JOBS1, PR)
                turn_hi(0, L, 0, T_MIX, UK, XH)
                root(0, L, 2, 1, 8)
                hi(0, L, 0, U_OUT + 2)
                turn_hi(0, L, 0, T_MIX + 2, UK, XH[:, UK:KB])

                def squares(k, c, bank, used):
                    act.wait_ge(s_used.sem, s_used.at(0, L, used))
                    for m in range(TILES):
                        if m == 1:
                            act.wait_ge(s_ng.sem, s_ng.at(0, L, 2 * (k - 2 + c) + 1))
                        act_(room(8192, 2, TILES, COLS)[:, c, m], pair(bank)[:, m, :], ACT.Square,
                             accum_out=stat[:, 0, k, 2 * c + m:2 * c + m + 1]).then_inc(s_sq.sem, 1)

                his(0, L, 0, U_OUT + 3, U_OUT + 4)
                squares(2, 0, 1, U_OUT + 3)
                squares(2, 1, 0, U_OUT + 4)
                root(0, L, 3, 2, 2)

                turn_hi(0, L, 0, T_N2, KB, XH, gain=prec[:, 1])
                hi(0, L, 0, U_OUT + 5)
                act.wait_ge(s_x.sem, s_x.at(0, L, 1))
                for m in range(TILES):
                    ins = act_(room(12288, TILES, DM)[:, m], X[:, m, :], ACT.Square, accum_out=stat[:, 0, 3, m:m + 1])
                ins.then_inc(s_ss.sem, 1)
                root(0, L, 4, 3, 2)
                act.wait_ge(s_rs.sem, s_rs.at(0, L, 2))

                def inner(i, j, used):
                    act.wait_ge(s_used.sem, s_used.at(0, L, 4 * i + used))
                    for m in range(TILES):
                        ins = act_(H[:, m, :], G[:, m, :], ACT.Relu, scale=stat[:, 2, 3, m:m + 1])
                    ins.then_inc(s_act.sem, 1)

                inner(0, 0, U_MLP + 2)
                his(0, L, 0, U_MLP + 2, U_MLP + 3)
                turn_hi(0, L, 0, T_MLP, UK, MH)
                with act.Fori(0, 7) as i:
                    his(0, L, i, U_MLP + 4, U_MLP + 5)
                    inner(i, 1, U_MLP + 4)
                    his(0, L, i, U_MLP + 6, U_MLP + 7)
                    turn_hi(0, L, i, T_MLP + 2, UK, MH)
                turn_hi(0, L, 0, T_P, 2, YH, per=1)
                his(0, L, 0, U_PLE)
                squares(4, 0, 1, U_PLE - 1)
                squares(4, 1, 2, U_PLE)
                root(0, L, 5, 4, 2)

                his(0, L, 0, U_PLE + 1, U_PLE + 2)
                for n in range(2):
                    act.wait_ge(s_used.sem, s_used.at(0, L, U_PLE + 1 + n))
                    act_(PP[:, :, n * COLS:(n + 1) * COLS], pair(n), ACT.Copy).then_inc(s_pp.sem, 1)
                turn_hi(0, L, 0, T_PX, KB, XH)
                his(0, L, 0, U_PLE + 3, U_PLE + 4, U_PLE + 5)
                for n in range(2):
                    act.wait_ge(s_used.sem, s_used.at(0, L, U_PLE + 4 + 2 * n))
                    act.wait_ge(s_sgf.sem, s_sgf.at(0, L, n))
                    act_(SG, pair(n), ACT.Sigmoid).then_inc(s_sg.sem, 1)

            with act.Fori(0, DEPTH) as L:
                his(1, L, 0, 0, 1)
                turn_hi(1, L, 0, 0, KB, XH)
                with act.Fori(0, 2) as i:
                    his(1, L, i, 2, 3, 4, 5)
                his(1, L, 0, 10, 11, 12, 13, 14, 15)
                turn_copy(1, L, T2_QK, 18, QT2)
                for q in range(len(JOBS2)):
                    exps(1, L, q, JOBS2, PR2)
                turn_hi(1, L, 0, T2_YA, 3, MH, per=1)
                with act.Fori(0, 2) as i:
                    his(1, L, i, V_RET + 2, V_RET + 3, V_RET + 4, V_RET + 5)
                hi(1, L, 0, V_RET + 10)
                turn_copy(1, L, T2_RET, 16, QTR)
                his(1, L, 0, *range(V_RET + 11, V_GATE + 2))

                def gate(c, func, dst, src):
                    act.wait_ge(s_evac.sem, s_evac.at(1, L, c + 1))
                    act_(dst, src, func).then_inc(s_sz.sem, 1)

                for h in range(RH):
                    hi(1, L, 0, V_GATE + 2 * h + 2)
                    root(1, L, h + 1, h % 2, 2)
                    hi(1, L, 0, V_GATE + 2 * h + 3)
                    gate(15 + h, ACT.Silu, SZ, GZ)
                for c in range(19, 23):
                    his(1, L, 0, 2 * c + 2, 2 * c + 3)
                    if c == 20:
                        turn_hi(1, L, 0, T2_YB, KB, YH)
                    gt = VR[:, :, (c - 19) * COLS:(c - 18) * COLS]
                    gate(c, ACT.Sigmoid, gt, gt)

                turn_hi(1, L, 0, T2_YB + 4, 4, XH)
                hi(1, L, 0, V_RP)
                turn_hi(1, L, 0, T2_YB + 6, 4, XH[:, 4:8])
                his(1, L, 0, *range(V_RP + 1, V_RP + 8))
                turn_hi(1, L, 0, T2_M, 4, XH)
                his(1, L, 0, V_OUT, V_OUT + 1, V_OUT + 2)
                turn_hi(1, L, 0, T2_M + 2, 4, XH[:, 4:8])
                his(1, L, 0, V_OUT + 3, V_FFN)
                root(1, L, 5, 2, 2)

                turn_hi(1, L, 0, T2_FX, KB, XH)
                hi(1, L, 0, V_FFN + 1)

                def inner2(i, j, used):
                    act.wait_ge(s_used.sem, s_used.at(1, L, 4 * i + used))
                    act_(H2, G[:, 0:2, 0:256], ACT.Silu).then_inc(s_act.sem, 1)

                inner2(0, 0, V_FFN + 2)
                his(1, L, 0, V_FFN + 2, V_FFN + 3)
                turn_hi(1, L, 0, T2_FFN, 2, MH, per=1)
                with act.Fori(0, FJ - 2) as i:
                    his(1, L, i, V_FFN + 4, V_FFN + 5)
                    inner2(i, 1, V_FFN + 4)
                    his(1, L, i, V_FFN + 6, V_FFN + 7)
                    turn_hi(1, L, i, T2_FFN + 2, 2, MH, per=1)
                e = 4 * (FJ - 2)
                his(1, L, 0, V_FFN + 4 + e, V_FFN + 5 + e)
                inner2(0, FJ - 1, V_FFN + 4 + e)
                his(1, L, 0, V_FFN + 6 + e, V_FFN + 7 + e)
                turn_hi(1, L, 0, T2_FFN + 2 * (FJ - 1), 2, MH, per=1)
                root(1, L, 6, 3, 2)

        @block.gpsimd
        def _(pool):
            with pool.Fori(0, DEPTH) as L:
                pool.wait_ge(s_evac.sem, s_evac.at(0, L, 1))
                rope(pool, nc.gpsimd, RTP, A_Q, 4, HD, 0)
                pool.drain()
                rope(pool, nc.gpsimd, RTP, A_K, 4, HD, 0).then_inc(s_prope.sem, 1)
                pool.drain()
                pool.wait_ge(s_evac.sem, s_evac.at(0, L, 5))
                rope(pool, nc.gpsimd, RTP, C_Q, 8, 32, 64)
                pool.drain()
                pool.wait_ge(s_evac.sem, s_evac.at(0, L, 6))
                rope(pool, nc.gpsimd, RTP, C_K, 8, 32, 64).then_inc(s_prope.sem, 1)
                pool.drain()
                pool.wait_ge(s_evac.sem, s_evac.at(0, L, CH1))
                rope(pool, nc.gpsimd, RTP, D_K, 2, HD, 0)
                pool.drain()
                for kv in range(2):
                    for r in range(2):
                        ins = nc.gpsimd.tensor_copy(DUP[:, :, P + (2 * kv + r) * HD:P + (2 * kv + r + 1) * HD],
                                                    Z[:, :, D_K + kv * HD:D_K + (kv + 1) * HD])
                ins.then_inc(s_prope.sem, 1)

        @block.vector
        def _(dve):
            tt, ts, stt = nc.vector.tensor_tensor, nc.vector.tensor_scalar, nc.vector.scalar_tensor_tensor

            def lo(blk, L, i, c):
                n, slot = size(blk, c), c % RAW
                dve.wait_ge(s_hi.sem, s_hi.at(blk, L, 4 * i + c + 1))
                tt(wlo[:, c % PARTS, 0:n], raw[:, slot, 0:n], whi[:, c % PARTS, 0:n].bitcast(F32),
                   ALU.subtract).then_inc(s_lo.sem, 1)

            def los(blk, L, i, *cs):
                for c in cs:
                    lo(blk, L, i, c)

            def turn_lo(blk, L, i, t, n, hx, lx, per=2, gain=None):
                for b in range(0, n, per):
                    tt_ = t + b // per
                    dve.wait_ge(s_thi.sem, s_thi.at(blk, L, 2 * i + split_no(blk, tt_) + 1))
                    k = min(per, n - b)
                    src = T[:, tt_ % 2, 0:k * S].rearrange("p (k s) -> p k s", s=S)
                    if gain is None:
                        ins = tt(lx[:, b:b + k, :], src, hx[:, b:b + k, :].bitcast(F32), ALU.subtract)
                    else:
                        for kk in range(k):
                            ins = stt(out=lx[:, b + kk, :], in0=src[:, kk, :], scalar=gain[:, b + kk:b + kk + 1],
                                      in1=hx[:, b + kk, :].bitcast(F32), op0=ALU.mult, op1=ALU.subtract)
                    ins.then_inc(s_tfree.sem, 1)

            def mean(norm, n, width, halves=False):
                if halves:
                    tt(stat[:, 0, norm, 0:n], stat[:, 0, norm, 0:n], stat[:, 0, norm, n:2 * n], ALU.add)
                    dve.drain()
                return ts(stat[:, 0, norm, 0:n], stat[:, 0, norm, 0:n], 1.0 / width, EPS, ALU.mult, ALU.add)

            def invert(blk, L, k, norm, n):
                dve.wait_ge(s_sd.sem, s_sd.at(blk, L, k))
                return nc.vector.reciprocal(stat[:, 2, norm, 0:n], stat[:, 1, norm, 0:n])

            def prep(blk, L, q, jobs):
                kind, m, _ = jobs[q]
                n = (m + 1) * P
                dve.wait_ge(s_log.sem, s_log.at(blk, L, q + 1))
                if kind == "E":
                    nc.vector.tensor_reduce(mx[:, q, 0:1], logit_set(q)[:, 0:3, 0:n], AX.XY, ALU.max)
                    dve.drain()
                    ts(nm[:, q, 0:1], mx[:, q, 0:1], -SCALE[kind], None, ALU.mult).then_inc(s_nm.sem, 1)
                    return
                g = G[:, 2 * (q % 2):2 * (q % 2) + 2, :].rearrange("p b (h s) -> p h b s", s=S)
                nc.vector.tensor_reduce(mx[:, q, :].rearrange("p (h b) -> p h b", b=2), g[:, :, :, 0:n], AX.X, ALU.max)
                dve.drain()
                if kind == "D":
                    tt(mx[:, q, :], mx[:, q, :], cur[:, 8:12], ALU.max)
                    dve.drain()
                ins = ts(nm[:, q, :], mx[:, q, :], -SCALE[kind], None, ALU.mult)
                if kind == "D":
                    dve.drain()
                    ins = tt(ds_[:, q, :], cur[:, 4:8], nm[:, q, :], ALU.add)
                ins.then_inc(s_nm.sem, 1)

            def copy_turned(blk, L, q, jobs, t0, dst):
                kind, m, _ = jobs[q]
                w = (3 if kind == "E" else 4) * P
                for kt in range(m + 1):
                    t = t0 + job_banks(jobs, q) + kt
                    dve.wait_ge(s_t.sem, s_t.at(blk, L, t + 1))
                    nc.vector.tensor_copy(dst[:, q % 2, kt, 0:w], T[:, t % 2, 0:w]).then_inc(s_tfree.sem, 1)

            def outputs(blk, L, q, jobs):
                kind, m, x = jobs[q]
                dve.wait_ge(s_pv.sem, s_pv.at(blk, L, q + 1))
                if kind == "E":
                    nc.vector.reciprocal(rl[:, q, 0:1], ls[:, q, 0:1])
                    dve.drain()
                    ts(Z2[:, m, x * HD:(x + 1) * HD], A[:, q % 2, 0:HD], rl[:, q, 0:1], None,
                       ALU.mult).then_inc(s_o.sem, 1)
                    return
                if kind == "D":
                    tt(ls[:, q, :], ls[:, q, :], es[:, q, :], ALU.add)
                    dve.drain()
                nc.vector.reciprocal(rl[:, q, :], ls[:, q, :])
                dve.drain()
                src = A[:, q % 2, 0:4 * HD].rearrange("p (u d) -> p u d", d=HD)
                by = rl[:, q, :].unsqueeze(2).to_broadcast([P, 4, HD])
                if kind != "C":
                    dst = Z[:, m, MIX0 + MIXCOL[kind]:MIX0 + MIXCOL[kind] + 4 * HD].rearrange("p (u d) -> p u d", d=HD)
                    tt(dst, src, by, ALU.mult).then_inc(s_o.sem, 1)
                    return
                odd = rl[:, q, :].rearrange("p (h m) -> p h m", m=2)[:, :, 1]
                ts(odd, odd, cur[:, 12:13], -1.0, ALU.mult, ALU.mult)
                dve.drain()
                both = SCO[:].rearrange("p (u d) -> p u d", d=HD)
                tt(both, src, by, ALU.mult)
                dve.drain()
                two = SCO[:].rearrange("p (h m d) -> p h m d", m=2, d=HD)
                tt(CO[:, m, :, :].rearrange("p (h x) d -> p h x d", x=2)[:, :, x, :], two[:, :, 0, :], two[:, :, 1, :], ALU.add).then_inc(s_o.sem, 1)

            def run_jobs(blk, L, jobs, t0, dst, beside=None):
                for q in range(len(jobs) + 2):
                    if q < len(jobs):
                        prep(blk, L, q, jobs)
                        if beside:
                            beside(q)
                    if 1 <= q <= len(jobs):
                        copy_turned(blk, L, q - 1, jobs, t0, dst)
                    if q >= 2:
                        outputs(blk, L, q - 2, jobs)

            for t in (s_lo, s_tfree, s_evac, s_rlf, s_o, s_sgf):
                dve.sem_inc(t.sem, t.credit)
            dve.wait_ge(s_xin, 16)
            dve.sem_inc(s_xh.sem, 1)
            dve.sem_inc(s_x.sem, 1)
            dve.wait_ge(s_const, 16 * N_CONST)
            for n in range(2):
                tt(lamv[:, n * 128:n * 128 + 64], lamv[:, n * 128:n * 128 + 64], lamv[:, n * 128 + 64:n * 128 + 128], ALU.mult)
            dve.drain()
            for n in range(2):
                ins = nc.vector.tensor_reduce(lsum[:, 2 * n:2 * n + 2], lamv[:, n * 128:n * 128 + 64].rearrange(
                    "p (l d) -> p l d", d=32), AX.X, ALU.add)
            ins.then_inc(s_tab, 1)
            nc.vector.tensor_copy(identb[:], ident[:])
            nc.vector.tensor_copy(maskb[:], room(0, 2, P))
            nc.vector.tensor_copy(posf[:], posi[:])
            dve.drain()
            turns, part = room(2600, TILES, 96), room(2800, TILES, 96)
            for m in range(TILES):
                ts(sind[:, m, :], freq[:], posf[:, m:m + 1], None, ALU.mult)
            dve.drain()
            magic = 12582912.0
            ts(turns, sind[:], 1.0 / (2 * math.pi), magic, ALU.mult, ALU.add)
            dve.drain()
            ts(turns, turns, magic, None, ALU.subtract)
            dve.drain()
            c1 = 6.28125
            c2 = float(np.float32(round((2 * math.pi - c1) * 2 ** 21) / 2 ** 21))
            for c in (c1, c2, 2 * math.pi - c1 - c2):
                stt(out=sind[:], in0=turns, scalar=-c, in1=sind[:], op0=ALU.mult, op1=ALU.add)
                dve.drain()
            ts(sind[:], sind[:], 3.1415925, -3.1415925, ALU.min, ALU.max)
            dve.drain()
            stt(out=part, in0=sind[:], scalar=-1.0, in1=sind[:], op0=ALU.mult, op1=ALU.max)
            dve.drain()
            ts(cosd[:], part, -1.0, math.pi / 2, ALU.mult, ALU.add).then_inc(s_tab, 1)
            dve.wait_ge(s_sin, 1)
            ts(sind[:, :, 0:32], sind[:, :, 0:32], -1.0, None, ALU.mult)
            ts(sind[:, :, 64:80], sind[:, :, 64:80], -1.0, None, ALU.mult)
            dve.wait_ge(s_le, 1)
            tt(lam, lsum[:, 0:2], lsum[:, 2:4], ALU.subtract)
            dve.drain()
            tt(lam, lam, lamc[:, 0:2], ALU.add)
            for n in range(DEPTH):
                ts(subln[:, n * HD:(n + 1) * HD], subln[:, n * HD:(n + 1) * HD], lamc[:, 2 + n:3 + n], None, ALU.mult)
            ok = arena[0:18, 1024:2048].rearrange("p (a b) -> p a b", a=2)
            rowsb = arena[0:18, 2048:2560]
            dve.wait_ge(s_bmm, 1)
            tt(rowsb, T[0:18, 0, :], ok[:, 0], ALU.mult)
            dve.drain()
            tt(rowsb, rowsb, ok[:, 1], ALU.add).then_inc(s_bvec, 1)

            def times_gain(L, used, norm, row, c, bank):
                dve.wait_ge(s_used.sem, s_used.at(0, L, used))
                cols = slice(c * COLS, (c + 1) * COLS)
                for m in (1, 0):
                    if m == 0:
                        dve.wait_ge(s_sq.sem, s_sq.at(0, L, 2 * (norm - 2 + c) + 1))
                    tt(NG[:, m, cols], pair(bank)[:, m, :], gains[:, row, cols], ALU.mult).then_inc(s_ng.sem, 1)

            def add_normed(norm):
                dve.drain()
                for c, done in enumerate((s_xh, s_x)):
                    for m in range(TILES):
                        xc = X[:, m, c * COLS:(c + 1) * COLS]
                        ins = stt(out=xc, in0=NG[:, m, c * COLS:(c + 1) * COLS], scalar=stat[:, 2, norm, m:m + 1],
                                  in1=xc, op0=ALU.mult, op1=ALU.add)
                    ins.then_inc(done.sem, 1)

            with dve.Fori(0, DEPTH) as L:
                nc.vector.tensor_copy(cur[:, 0:4], bforget[:, bass.ds(L * 4, 4)])
                nc.vector.tensor_copy(cur[:, 4:8], sink[:, bass.ds(L * 4, 4)])
                nc.vector.tensor_copy(cur[:, 12:13], lam[:, bass.ds(L, 1)])
                nc.vector.tensor_copy(cur[:, 16:80], subln[:, bass.ds(L * HD, HD)])
                nc.vector.tensor_copy(prec[:], pre[:, :, bass.ds(L, 1), :].rearrange("p n l k -> p (n l) k"))
                dve.drain()
                ts(cur[:, 8:12], cur[:, 4:8], 1.0 / SCALE["D"], None, ALU.mult).then_inc(s_cur.sem, 1)

                turn_lo(0, L, 0, 0, KB, XH, XL, gain=prec[:, 0])
                los(0, L, 0, 0, 1)
                dve.wait_ge(s_ss.sem, s_ss.at(0, L, 1))
                mean(0, 2, DM).then_inc(s_ms.sem, 1)
                invert(0, L, 1, 0, 2).then_inc(s_rs.sem, 1)

                los(0, L, 0, *range(2, 8))
                dve.wait_ge(s_evac.sem, s_evac.at(0, L, 3))
                rope(dve, nc.vector, RT, A_IQ, 9, HD, 0)
                ts(IW[:], Z[:, :, A_IW:A_IW + IDX_HEADS], IDX_HEADS ** -0.5 * HD ** -0.5, None, ALU.mult)
                dve.drain()
                for r in range(2):
                    ins = nc.vector.tensor_copy(DUP[:, :, r * HD:(r + 1) * HD], Z[:, :, A_IK:A_IK + HD])
                ins.then_inc(s_rope.sem, 1)
                los(0, L, 0, 8, 9, 10)

                def scores(m):
                    n = (m + 1) * P
                    sc = SCO[:, 0:n]
                    dve.drain()
                    dve.wait_ge(s_rl.sem, s_rl.at(0, L, 1 + 2 * m))
                    ts(sc, RL[:, 0, 0:n], IW[:, m, 0:1], None, ALU.mult)
                    for h in range(1, IDX_HEADS):
                        dve.drain()
                        ins = stt(out=sc, in0=RL[:, h, 0:n], scalar=IW[:, m, h:h + 1], in1=sc, op0=ALU.mult, op1=ALU.add)
                    ins.then_inc(s_rlf.sem, 1)
                    dve.drain()
                    tt(sc, sc, causal[:, m, 0:n], ALU.add)

                def pick(m, keys):
                    sc = SCO[:, 0:(m + 1) * P]
                    for _ in range(keys // 8):
                        dve.drain()
                        nc.vector.max(m8[:], sc)
                        dve.drain()
                        nc.vector.match_replace(out=sc, in_to_replace=m8[:], in_values=sc, imm_value=TAKEN)

                def mask(m):
                    n = (m + 1) * P
                    sc = SCO[:, 0:n]
                    dve.drain()
                    ts(sc, sc, TAKEN / 2, NEG, ALU.is_gt, ALU.mult)
                    dve.drain()
                    tt(amask[:, m, 0:n], sc, causal[:, m, 0:n], ALU.min).then_inc(s_am.sem, 1)

                scores(0)
                pick(0, TOPK // 2)
                lo(0, L, 0, 11)
                pick(0, TOPK // 2)
                mask(0)
                dve.wait_ge(s_evac.sem, s_evac.at(0, L, 5))
                tt(LF[:, 0], Z[:, :, B_F:B_F + 4], cur[:, 0:4].unsqueeze(1).to_broadcast([P, TILES, 4]), ALU.add)
                dve.drain()
                stt(out=LF[:, 1], in0=LF[:, 0], scalar=-1.0, in1=LF[:, 0], op0=ALU.mult, op1=ALU.min).then_inc(s_lf.sem, 1)
                ts(LF[:, 3], LF[:, 0], 0.0, None, ALU.min)
                lo(0, L, 0, 12)
                scores(1)
                pick(1, TOPK // 4)
                lo(0, L, 0, 13)
                pick(1, TOPK // 4)
                dve.wait_ge(s_lg.sem, s_lg.at(0, L, 1))
                ts(LF[:, 2], LF[:, 1], 1.0, None, ALU.add).then_inc(s_lf.sem, 1)
                dve.wait_ge(s_evac.sem, s_evac.at(0, L, CH1))
                rope(dve, nc.vector, RT, D_Q, 4, HD, 0).then_inc(s_rope.sem, 1)

                def beside(q):
                    if q == 0:
                        dve.wait_ge(s_lg.sem, s_lg.at(0, L, 2))
                        tt(LF[:, 3], LF[:, 3], LF[:, 2], ALU.subtract)
                        dve.drain()
                        ts(LF[:, 4], LF[:, 3], -1.0 / SCALE["B"], None, ALU.mult).then_inc(s_lf.sem, 1)
                    elif q < 3:
                        pick(1, TOPK // 4)
                        if q == 2:
                            mask(1)
                    elif q < 5:
                        lo(0, L, 0, 11 + q)

                run_jobs(0, L, JOBS1, T_JOB, PT, beside)
                turn_lo(0, L, 0, T_MIX, UK, XH, XL)
                dve.drain()
                tt(CS, CO, CO, ALU.mult)
                dve.drain()
                nc.vector.tensor_reduce(stat[:, 0, 1, :], CS.rearrange("p m h d -> p (m h) d"), AX.X, ALU.add)
                dve.drain()
                mean(1, 8, HD).then_inc(s_ms.sem, 1)
                invert(0, L, 2, 1, 8)
                dve.drain()
                co = CO.rearrange("p m h d -> p (m h) d")
                tt(co, co, stat[:, 2, 1, :].unsqueeze(2).to_broadcast([P, 8, HD]), ALU.mult)
                dve.drain()
                c0 = MIX0 + MIXCOL["C"]
                for m in range(TILES):
                    ins = tt(Z[:, m, c0:c0 + 256].rearrange("p (h d) -> p h d", d=HD), CO[:, m],
                             cur[:, 16:80].unsqueeze(1).to_broadcast([P, 4, HD]), ALU.mult)
                ins.then_inc(s_mix.sem, 1)

                lo(0, L, 0, U_OUT + 2)
                turn_lo(0, L, 0, T_MIX + 2, UK, XH[:, UK:KB], XL[:, UK:KB])
                los(0, L, 0, U_OUT + 3, U_OUT + 4)
                dve.wait_ge(s_gain.sem, s_gain.at(0, L, 2))
                times_gain(L, U_OUT + 3, 2, 0, 0, 1)
                times_gain(L, U_OUT + 4, 2, 0, 1, 0)
                dve.drain()
                dve.wait_ge(s_sq.sem, s_sq.at(0, L, 4))
                mean(2, 2, DM, halves=True).then_inc(s_ms.sem, 1)
                invert(0, L, 3, 2, 2)
                add_normed(2)

                turn_lo(0, L, 0, T_N2, KB, XH, XL, gain=prec[:, 1])
                lo(0, L, 0, U_OUT + 5)
                dve.wait_ge(s_ss.sem, s_ss.at(0, L, 2))
                mean(3, 2, DM).then_inc(s_ms.sem, 1)
                invert(0, L, 4, 3, 2).then_inc(s_rs.sem, 1)
                dve.drain()

                def inner(i, j):
                    dve.wait_ge(s_act.sem, s_act.at(0, L, i + j + 1))
                    for m in range(TILES):
                        ins = stt(out=H[:, m, :], in0=G[:, m, :], scalar=stat[:, 2, 3, m:m + 1], in1=H[:, m, :],
                                  op0=ALU.mult, op1=ALU.mult)
                    ins.then_inc(s_h.sem, 1)

                inner(0, 0)
                los(0, L, 0, U_MLP + 2, U_MLP + 3)
                turn_lo(0, L, 0, T_MLP, UK, MH, ML)
                with dve.Fori(0, 7) as i:
                    los(0, L, i, U_MLP + 4, U_MLP + 5)
                    inner(i, 1)
                    los(0, L, i, U_MLP + 6, U_MLP + 7)
                    turn_lo(0, L, i, T_MLP + 2, UK, MH, ML)
                turn_lo(0, L, 0, T_P, 2, YH, YL, per=1)
                lo(0, L, 0, U_PLE)
                times_gain(L, U_PLE - 1, 4, 1, 0, 1)
                times_gain(L, U_PLE, 4, 1, 1, 2)
                dve.drain()
                dve.wait_ge(s_sq.sem, s_sq.at(0, L, 8))
                mean(4, 2, DM, halves=True).then_inc(s_ms.sem, 1)
                lo(0, L, 0, U_PLE + 1)
                invert(0, L, 5, 4, 2)
                add_normed(4)

                turn_lo(0, L, 0, T_PX, KB, XH, XL)
                los(0, L, 0, U_PLE + 2, U_PLE + 3, U_PLE + 4, U_PLE + 5)
                for n, done in enumerate((s_xh, s_x)):
                    dve.wait_ge(s_sg.sem, s_sg.at(0, L, n + 1))
                    cols = slice(n * COLS, (n + 1) * COLS)
                    tt(TMP, SG, PP[:, :, cols], ALU.mult).then_inc(s_sgf.sem, 1)
                    dve.drain()
                    tt(X[:, :, cols], X[:, :, cols], TMP, ALU.add).then_inc(done.sem, 1)
                    dve.drain()

            with dve.Fori(0, DEPTH) as L:
                turn_lo(1, L, 0, 0, KB, XH, XL)
                los(1, L, 0, 0, 1)

                def project(i, c, dst, cols=COLS):
                    dve.wait_ge(s_used.sem, s_used.at(1, L, 4 * i + 2 * c + 2))
                    dve.wait_ge(s_bin[c % 2].sem, s_bin[c % 2].at(1, L, i + c // 2 + 1))
                    tt(dst, pair(c % 2)[:, :, 0:cols], BIN[:, c % 2, 0:cols].unsqueeze(1).to_broadcast([P, TILES, cols]),
                       ALU.add).then_inc(s_evac.sem, 1)

                with dve.Fori(0, 2) as i:
                    for c in range(2):
                        los(1, L, i, 2 * c + 2, 2 * c + 3)
                        project(i, c, Z2[:, :, bass.ds(i * 1024 + c * COLS, COLS)])
                for c in range(4, SEG1):
                    los(1, L, 0, 2 * c + 2, 2 * c + 3)
                    cols = COLS if c < 6 else LAST2
                    project(0, c, Z2[:, :, c * COLS:c * COLS + cols], cols)
                run_jobs(1, L, JOBS2, T2_JOB, PT2)
                turn_lo(1, L, 0, T2_YA, 3, MH, ML, per=1)

                def rotate(i, c):
                    x = QK[:, :, bass.ds(i * 1024 + c * COLS, COLS)].rearrange("p m (h e d) -> p m h e d", e=2, d=P)
                    x1, x2 = x[:, :, :, 0], x[:, :, :, 1]
                    cos, sin = (rot[:, n].unsqueeze(2).to_broadcast([P, TILES, 2, P]) for n in range(2))
                    u = RTR[:]
                    tt(u[:, 0], x2, sin, ALU.mult)
                    tt(u[:, 1], x1, sin, ALU.mult)
                    dve.drain()
                    tt(x1, x1, cos, ALU.mult)
                    tt(x2, x2, cos, ALU.mult)
                    dve.drain()
                    tt(x1, x1, u[:, 0], ALU.subtract)
                    ins = tt(x2, x2, u[:, 1], ALU.add)
                    return ins

                with dve.Fori(0, 2) as i:
                    for c in range(2):
                        los(1, L, i, V_RET + 2 + 2 * c, V_RET + 3 + 2 * c)
                        project(i, SEG1 + c, QK[:, :, bass.ds(i * 1024 + c * COLS, COLS)])
                        dve.drain()
                        rotate(i, c).then_inc(s_rot.sem, 1)
                def decayed(h):
                    dve.wait_ge(s_sc.sem, s_sc.at(1, L, h + 1))
                    tt(SCT[:, h, 0:S], A[:, h % 2, 0:S], decay[:, h].rearrange("p a b -> p (a b)"), ALU.mult)
                    tt(SCT[:, h, S:S + P], A[:, h % 2, S:S + P], decay[:, h, 0], ALU.mult).then_inc(s_sd2.sem, 1)

                for c in range(11, 15):
                    los(1, L, 0, 2 * c + 2, 2 * c + 3)
                    project(0, c, VR[:, :, (c - 11) * COLS:(c - 10) * COLS])
                    if c in (12, 13):
                        decayed(2 * (c - 12))
                        decayed(2 * (c - 12) + 1)

                def normalise(h):
                    dve.wait_ge(s_ro.sem, s_ro.at(1, L, h + 1))
                    for m in range(TILES):
                        nc.vector.bn_stats(bns[:, 2 * (h % 2) + m, :], A[:, m, :])
                    dve.drain()
                    for m in range(TILES):
                        nc.vector.bn_aggr(bna[:, 2 * (h % 2) + m, :], bns[:, 2 * (h % 2) + m, :])
                    dve.drain()
                    b = bna[:, 2 * (h % 2):2 * (h % 2) + 2, :]
                    ts(stat[:, 0, h % 2, 0:2], b[:, :, 1], LN_EPS, None, ALU.add).then_inc(s_ms.sem, 1)
                    invert(1, L, h + 1, h % 2, 2)
                    dve.drain()
                    for m in range(TILES):
                        ins = ts(QK[:, m, h * RDV:(h + 1) * RDV], A[:, m, :], b[:, m, 0:1], stat[:, 2, h % 2, m:m + 1],
                                 ALU.subtract, ALU.mult)
                    ins.then_inc(s_yr.sem, 1)

                for h in range(RH):
                    lo(1, L, 0, V_GATE + 2 * h + 2)
                    normalise(h)
                    lo(1, L, 0, V_GATE + 2 * h + 3)
                    project(0, 15 + h, GZ)
                    dve.wait_ge(s_sz.sem, s_sz.at(1, L, h + 1))
                    y = QK[:, :, h * RDV:(h + 1) * RDV]
                    tt(y, y, SZ, ALU.mult).then_inc(s_yb.sem, 1)
                for c in range(19, 23):
                    los(1, L, 0, 2 * c + 2, 2 * c + 3)
                    project(0, c, VR[:, :, (c - 19) * COLS:(c - 18) * COLS])
                    if c == 20:
                        turn_lo(1, L, 0, T2_YB, KB, YH, YL)

                turn_lo(1, L, 0, T2_YB + 4, 4, XH, XL)
                lo(1, L, 0, V_RP)
                dve.wait_ge(s_sz.sem, s_sz.at(1, L, 8))

                def gated(n, used, gate_col, dst):
                    dve.wait_ge(s_used.sem, s_used.at(1, L, used))
                    tt(dst, pair(1 - n), VR[:, :, gate_col + n * COLS:gate_col + (n + 1) * COLS],
                       ALU.mult).then_inc(s_evac.sem, 1)

                gated(0, V_AP + 1, 0, M[:, :, 0:COLS])
                turn_lo(1, L, 0, T2_YB + 6, 4, XH[:, 4:8], XL[:, 4:8])
                lo(1, L, 0, V_RP + 1)
                gated(1, V_AP + 2, 0, M[:, :, COLS:DM])
                for n in range(2):
                    los(1, L, 0, *(range(V_RP + 2, V_RP + 6) if n == 0 else [V_OUT]))
                    gated(n, V_RP + 4 + 4 * n, DM, TMP2)
                    dve.drain()
                    mc = M[:, :, n * COLS:(n + 1) * COLS]
                    tt(mc, mc, TMP2, ALU.add).then_inc(s_m.sem, 1)
                    dve.drain()
                    if n == 0:
                        los(1, L, 0, V_RP + 6, V_RP + 7)
                        turn_lo(1, L, 0, T2_M, 4, XH, XL)
                lo(1, L, 0, V_OUT + 1)
                lo(1, L, 0, V_OUT + 2)
                turn_lo(1, L, 0, T2_M + 2, 4, XH[:, 4:8], XL[:, 4:8])

                def residual(c, bank):
                    xc = X[:, :, c * COLS:(c + 1) * COLS]
                    ins = stt(out=xc, in0=xc, scalar=ALPHA, in1=pair(bank), op0=ALU.mult, op1=ALU.add)
                    dve.drain()
                    for m in range(TILES):
                        nc.vector.bn_stats(bns[:, 2 * m + c, :], X[:, m, c * COLS:(c + 1) * COLS])
                    return ins

                def layer_norm(k, norm, gain):
                    dve.drain()
                    for m in range(TILES):
                        nc.vector.bn_aggr(bna[:, m, :], bns[:, 2 * m:2 * m + 2, :].rearrange("p a b -> p (a b)"))
                    dve.drain()
                    ts(stat[:, 0, norm, 0:2], bna[:, 0:2, 1], LN_EPS, None, ALU.add).then_inc(s_ms.sem, 1)
                    dve.wait_ge(s_gain.sem, s_gain.at(1, L, gain))
                    for c, done in enumerate((s_xh, s_x)):
                        cols = slice(c * COLS, (c + 1) * COLS)
                        for m in range(TILES):
                            xc = X[:, m, cols]
                            stt(out=xc, in0=xc, scalar=bna[:, m, 0:1], in1=gains[:, 0, cols], op0=ALU.subtract,
                                op1=ALU.mult)
                        if c == 0:
                            invert(1, L, k, norm, 2)
                        dve.drain()
                        for m in range(TILES):
                            xc = X[:, m, cols]
                            ins = stt(out=xc, in0=xc, scalar=stat[:, 2, norm, m:m + 1], in1=gains[:, 1, cols],
                                      op0=ALU.mult, op1=ALU.add)
                        ins.then_inc(done.sem, 1)

                lo(1, L, 0, V_OUT + 3)
                dve.wait_ge(s_used.sem, s_used.at(1, L, V_OUT + 3))
                residual(0, 1).then_inc(s_evac.sem, 1)
                lo(1, L, 0, V_FFN)
                dve.wait_ge(s_used.sem, s_used.at(1, L, V_OUT + 4))
                residual(1, 0).then_inc(s_evac.sem, 1)
                layer_norm(5, 2, 2)

                turn_lo(1, L, 0, T2_FX, KB, XH, XL)
                lo(1, L, 0, V_FFN + 1)

                def inner2(i, j):
                    dve.wait_ge(s_act.sem, s_act.at(1, L, i + j + 1))
                    tt(H2, H2, G[:, 0:2, 256:512], ALU.mult).then_inc(s_h.sem, 1)

                inner2(0, 0)
                los(1, L, 0, V_FFN + 2, V_FFN + 3)
                turn_lo(1, L, 0, T2_FFN, 2, MH, ML, per=1)
                with dve.Fori(0, FJ - 2) as i:
                    los(1, L, i, V_FFN + 4, V_FFN + 5)
                    inner2(i, 1)
                    los(1, L, i, V_FFN + 6, V_FFN + 7)
                    turn_lo(1, L, i, T2_FFN + 2, 2, MH, ML, per=1)
                e = 4 * (FJ - 2)
                los(1, L, 0, V_FFN + 4 + e, V_FFN + 5 + e)
                inner2(0, FJ - 1)
                los(1, L, 0, V_FFN + 6 + e, V_FFN + 7 + e)
                turn_lo(1, L, 0, T2_FFN + 2 * (FJ - 1), 2, MH, ML, per=1)
                for c in range(2):
                    dve.wait_ge(s_used.sem, s_used.at(1, L, UNITS2 - 1 + c))
                    residual(c, 1 + c)
                layer_norm(6, 3, 4)


def kernel(**inputs):
    import concourse.bacc as bacc
    from concourse.bass_utils import run_bass_kernel_spmd

    nc = bacc.Bacc("TRN2", target_bir_lowering=False, num_devices=1)
    arrays = {f"in_{k}": np.ascontiguousarray(v) for k, v in {**inputs, **constants()}.items()}
    a = {k[3:]: nc.dram_tensor(k, v.shape, mybir.dt.from_np(v.dtype), kind="ExternalInput").ap()
         for k, v in arrays.items()}
    out = nc.dram_tensor("out", (1, S, DM), F32, kind="ExternalOutput").ap()
    program(nc, a, out)
    return run_bass_kernel_spmd(nc, [arrays], core_ids=[0]).results[0]["out"]
```

```python
import math
from contextlib import ExitStack

import numpy as np

import concourse.bass as bass
from concourse import mybir

F32 = mybir.dt.float32
F32R = mybir.dt.float32r
BF16 = mybir.dt.bfloat16
I32 = mybir.dt.int32
ALU = mybir.AluOpType
ACT = mybir.ActivationFunctionType
AX = mybir.AxisListType

P = 128
DM = 1024
S = 256
TILES = S // P
DEPTH = 2
KB = DM // P
COLS = 512
UK = 4
UNIT = UK * COLS
RAW = 4
PARTS = 2
HD = 64
EPS = 1e-6
LN_EPS = 1e-5
NEG = -1e30
TAKEN = -3e38
TOPK = 64
ALPHA = (2 * DEPTH) ** 0.25

A_Q, A_K, A_V, A_IQ, A_IK, A_IW = 0, 256, 512, 768, 1280, 1344
B_Q, B_K, B_V, B_F = 1352, 1608, 1864, 2120
C_Q, C_K, C_V = 2124, 2380, 2636
D_Q, D_K, D_V = 2892, 3148, 3276
D_IN = 3404
CH1 = 7
LAST1 = D_IN - 6 * COLS
D_FF = 4096
D_PLE = 256
IDX_HEADS = 8
MIX0 = A_IQ

ATTN_W = 1152
HG = 6
GROUPS = ((128, 1), (512, 4), (2048, 16))
RQ0 = 3 * ATTN_W
SEG1 = 7
LAST2 = RQ0 - 6 * COLS
IN2 = 11648
RH, RDV = 4, 512
YA_W = 384
D_FF2 = 2816
FJ = D_FF2 // 256

U_OUT, U_MLP, U_PLE0, U_DN7, U_PLE1, UNITS1 = 14, 18, 48, 49, 51, 56
V_RET, V_GATE, V_AP, V_RP, V_OUT, V_FFN, UNITS2 = 14, 30, 46, 48, 56, 60, 104

T_QK, T_JOB, T_MIX, T_N2, T_P, T_MLP, T_PX, TS1 = 4, 11, 30, 34, 38, 40, 56, 60
T2_QK, T2_JOB, T2_YA, T2_RET, T2_YB, T2_M, T2_FX, T2_FFN, TS2 = 4, 13, 31, 34, 42, 50, 54, 58, 80

JOBS1 = [("B", 0, 0), ("A", 0, 0), ("B", 1, 0), ("C", 0, 0), ("C", 1, 0), ("C", 0, 1), ("C", 1, 1),
         ("A", 1, 0), ("D", 0, 0), ("D", 1, 0)]
Q_TURN_C, Q_TURN_D = 1, 5
JOBS2 = [("E", m, h) for h in range(HG) for m in range(TILES)]
MIXCOL = {"A": 0, "B": 256, "C": 512, "D": 768}
SCALE = {"A": HD ** -0.5, "B": HD ** -0.5, "C": (HD // 2) ** -0.5, "D": HD ** -0.5, "E": HD ** -0.5}


def job_banks(jobs, q):
    between = 2 * (q >= Q_TURN_C) + 2 * (q >= Q_TURN_D) if jobs is JOBS1 else 0
    return sum(m + 1 for _, m, _ in jobs[:q]) + between


def job_end(jobs, q):
    return job_banks(jobs, q) + jobs[q][1] + 1


def split_no(blk, t):
    if blk == 0:
        return t if t <= T_QK else t - (T_MIX - T_QK)
    if t <= T2_QK:
        return t
    return t - (T2_YA - T2_QK) - (0 if t <= T2_RET else T2_YB - T2_RET)


class Tally:

    def __init__(self, sem, per, credit=0, step=1):
        self.sem, self.per, self.credit, self.step = sem, per, credit, step

    def at(self, blk, layer, k):
        base = self.credit + (DEPTH * self.per[0] if blk else 0)
        return layer * (self.per[blk] * self.step) + (k + base) * self.step


def constants():
    i = np.arange(P)
    c = {}
    ident = np.eye(P, dtype=np.float32)
    tri = (np.arange(S)[:, None] <= np.arange(S)[None, :]).astype(np.float32)
    causal = np.where(np.arange(S)[None, :] <= np.arange(S)[:, None], 0.0, NEG).astype(np.float32)
    tile_rows = lambda a: np.ascontiguousarray(a.reshape(TILES, P, -1).transpose(1, 0, 2))
    c["c_ident"] = ident
    c["c_flip"] = np.ascontiguousarray(ident[::-1])
    c["c_tri"] = tile_rows(tri)
    c["c_causal"] = tile_rows(causal)
    c["c_masks"] = np.stack([np.where(i[None] <= i[:, None], 0.0, NEG),
                             np.where(i[None] > i[:, None], 0.0, NEG)], 1).astype(np.float32)
    gam = np.log(1.0 - 2.0 ** (-5.0 - np.arange(RH)))
    diff = i[None, :] - i[:, None]
    diag = np.where(diff >= 0, np.exp(gam[:, None, None] * np.maximum(diff, 0)), 0.0)
    off = np.exp(gam[:, None, None] * (diff + P))
    c["c_decay"] = np.ascontiguousarray(
        (np.stack([diag, off], 1) / 16.0).transpose(2, 0, 1, 3)).astype(np.float32)
    inv = (np.float32(10000.0) ** (-np.arange(P, dtype=np.float32) / np.float32(P))).astype(np.float32)
    ang = (np.arange(S, dtype=np.float32)[:, None] * inv[None]).astype(np.float64)
    c["c_rot"] = np.ascontiguousarray(np.stack([tile_rows(np.cos(ang)), tile_rows(np.sin(ang))], 1)).astype(np.float32)
    f64 = (np.float32(10000.0) ** (-np.arange(32, dtype=np.float32) / np.float32(32))).astype(np.float32)
    f32 = (np.float32(10000.0) ** (-np.arange(16, dtype=np.float32) / np.float32(16))).astype(np.float32)
    c["c_freq"] = np.concatenate([f64, f64, f32, f32]).astype(np.float32)
    dist = 255 - np.arange(512)
    d = np.maximum(dist, 0)
    large = 16 + (np.log(np.maximum(d, 16) / 16) / np.log(2048 / 16) * 16).astype(np.int32)
    bucket = np.where(d < 16, d, np.minimum(large, 31))
    onehot = (np.arange(32)[:, None] == bucket[None]).astype(np.float32) * np.float32(HD ** 0.5)
    ok = np.concatenate([np.tile((dist >= 0) & (d <= w) & (d % s == 0), (HG, 1)) for w, s in GROUPS])
    c["c_onehot"] = onehot
    c["c_ok"] = np.stack([ok.astype(np.float32), np.where(ok, 0.0, NEG).astype(np.float32)], 1)
    lam0 = np.array([0.8 - 0.6 * math.exp(-0.3 * n) for n in range(DEPTH)])
    c["c_lam"] = np.concatenate([lam0, 1.0 - lam0]).astype(np.float32)
    return c


def program(nc, a, out):
    bias_rows = nc.dram_tensor("bias_rows", (2, 18, 512), F32R, kind="Internal").ap()

    with ExitStack() as ctx:
        def sb(name, shape, dt=F32):
            return ctx.enter_context(nc.sbuf_tensor(name, shape, dt))

        def psum(name, shape):
            return ctx.enter_context(nc.psum_tensor(name, shape, F32))

        def sem(name):
            return ctx.enter_context(nc.semaphore(name))

        raw = sb("raw", [P, RAW, UNIT])
        whi = sb("whi", [P, PARTS, UNIT], F32R)
        wlo = sb("wlo", [P, PARTS, UNIT], F32R)
        X = sb("X", [P, TILES, DM])
        XH = sb("XH", [P, KB, S], F32R)
        XL = sb("XL", [P, KB, S], F32R)
        MH = sb("MH", [P, UK, S], F32R)
        ML = sb("ML", [P, UK, S], F32R)
        YH = sb("YH", [P, KB, S], F32R)
        YL = sb("YL", [P, KB, S], F32R)
        gains = sb("gains", [P, 2, DM])
        arena = sb("arena", [P, 17100])

        def room(lo, *dims):
            n = int(np.prod(dims))
            ap = arena[:, lo:lo + n]
            if len(dims) == 1:
                return ap
            names = "abcd"[:len(dims)]
            kw = {names[i]: dims[i] for i in range(1, len(dims))}
            return ap.rearrange(f"p ({' '.join(names)}) -> p {' '.join(names)}", **kw)

        Z = room(0, TILES, D_IN)
        DUP = room(6808, TILES, 384)
        QT = room(7576, 21, S)
        PR = room(12952, 2, 4, S)
        PT = room(15000, 2, TILES, 512)
        RL = room(12952, IDX_HEADS, S)
        RT, RTP = (gains[:].rearrange("p a b -> p (a b)")[:, lo:hi] for lo, hi in ((0, 1152), (1152, 1664)))
        CO = gains[:].rearrange("p a b -> p (a b)")[:, 512:1024].rearrange("p (m h d) -> p m h d", m=TILES, d=HD)
        CB = gains[:].rearrange("p a b -> p (a b)")[:, 1664:1920]
        CS = room(7576, TILES, 4, HD)
        NG = room(10240, TILES, DM)
        H = room(0, TILES, COLS)
        TMP = room(2048, TILES, COLS)
        PP = room(4096, TILES, DM)
        SG = room(8192, TILES, COLS)
        PB = room(14400, TILES, D_PLE)
        Z2 = room(0, TILES, RQ0)
        QT2 = room(6912, 18, S)
        PR2 = room(11520, 2, 3, S)
        PT2 = room(13056, 2, TILES, 384)
        BR = YH, YL
        QK = room(0, TILES, 2048)
        VR = room(4096, TILES, 2048)
        QTR = room(8192, 16, S)
        SCT = room(12288, RH, 384)
        RTR = room(13056, 2, TILES, 2, P)
        GZ = room(8192, TILES, COLS)
        SZ = room(9216, TILES, COLS)
        M = room(10240, TILES, DM)
        TMP2 = room(12288, TILES, COLS)
        H2 = room(0, TILES, 256)
        swap = sb("swap", [P, 2, COLS])
        BIN = swap[:]
        tri = swap[:, 0].rearrange("p (m s) -> p m s", m=TILES)
        causal = swap[:, 1].rearrange("p (m s) -> p m s", m=TILES)

        ident = sb("ident", [P, P])
        flip = sb("flip", [P, P], F32R)
        identb = sb("identb", [P, P], BF16)
        maskb = sb("maskb", [P, 2, P], BF16)
        amask = sb("amask", [P, TILES, S], BF16)
        decay = sb("decay", [P, RH, 2, P])
        rot = sb("rot", [P, 2, TILES, P])
        cosd = sb("cosd", [P, TILES, 96])
        sind = sb("sind", [P, TILES, 96])
        freq = sb("freq", [P, 96])
        posi = sb("posi", [P, TILES], I32)
        posf = sb("posf", [P, TILES])
        small = sb("small", [P, 424])
        bforget, sink = small[:, 0:8], small[:, 8:16]
        subln, lamv, lamc = small[:, 16:144], small[:, 144:400], small[:, 400:404]
        lsum, lam = small[:, 404:408], small[:, 408:410]
        cur = sb("cur", [P, 90])
        pre = sb("pre", [P, 2, DEPTH, KB])
        prec = sb("prec", [P, 2, KB])
        stat = sb("stat", [P, 3, 5, 8])
        mx, nm, ls = (sb(n, [P, 12, 4]) for n in ("mx", "nm", "ls"))
        rl, es, ds_ = (sb(n, [P, 12, 4]) for n in ("rl", "es", "ds_"))
        IW = sb("IW", [P, TILES, IDX_HEADS])
        SCO = sb("SCO", [P, S])
        m8 = sb("m8", [P, 8])
        LF = sb("LF", [P, 5, TILES, 4])
        bns = sb("bns", [P, 4, 6])
        bna = sb("bna", [P, 4, 2])

        G = psum("G", [P, 4, 512])
        T = psum("T", [P, 2, 512])
        A = psum("A", [P, 2, 512])

        s_raw = [Tally(sem(f"s_raw{n}"), (UNITS1 // RAW, UNITS2 // RAW + more), step=16)
                 for n, more in enumerate((1, 1, FJ - 1, FJ - 1))]
        s_hi = Tally(sem("s_hi"), (UNITS1, UNITS2))
        s_lo = Tally(sem("s_lo"), (UNITS1, UNITS2), credit=RAW)
        s_used = Tally(sem("s_used"), (UNITS1, UNITS2), credit=PARTS)
        s_half = Tally(sem("s_half"), (2, 2))
        s_evac = Tally(sem("s_evac"), (CH1, 29), credit=2)
        s_t = Tally(sem("s_t"), (TS1, TS2))
        s_thi = Tally(sem("s_thi"), (TS1 - 26, TS2 - 35))
        s_tfree = Tally(sem("s_tfree"), (TS1, TS2), credit=2)
        s_x = Tally(sem("s_x"), (3, 2), credit=1)
        s_xh = Tally(sem("s_xh"), (3, 2), credit=1)
        s_ng = Tally(sem("s_ng"), (8, 0))
        s_sq = Tally(sem("s_sq"), (8, 0))
        s_ss = Tally(sem("s_ss"), (2, 0))
        s_ms = Tally(sem("s_ms"), (5, 6))
        s_sd = Tally(sem("s_sd"), (5, 6))
        s_rs = Tally(sem("s_rs"), (2, 0))
        s_cur = Tally(sem("s_cur"), (2, 0))
        s_rope = Tally(sem("s_rope"), (2, 0))
        s_prope = Tally(sem("s_prope"), (3, 0))
        s_lf = Tally(sem("s_lf"), (3, 0))
        s_lg = Tally(sem("s_lg"), (2, 0))
        s_dot = Tally(sem("s_dot"), (3, 0))
        s_rl = Tally(sem("s_rl"), (3, 0))
        s_rlf = Tally(sem("s_rlf"), (2, 0), credit=1)
        s_am = Tally(sem("s_am"), (2, 0))
        s_log = Tally(sem("s_log"), (len(JOBS1), len(JOBS2)))
        s_nm = Tally(sem("s_nm"), (len(JOBS1), len(JOBS2)))
        s_exp = Tally(sem("s_exp"), (len(JOBS1), len(JOBS2)), credit=2)
        s_pv = Tally(sem("s_pv"), (len(JOBS1), len(JOBS2)))
        s_o = Tally(sem("s_o"), (len(JOBS1), len(JOBS2)), credit=2)
        s_mix = Tally(sem("s_mix"), (1, 0))
        s_act = Tally(sem("s_act"), (8, FJ))
        s_h = Tally(sem("s_h"), (8, FJ))
        s_gain = Tally(sem("s_gain"), (2, 4), step=16)
        s_p = Tally(sem("s_p"), (1, 0), step=16)
        s_pp = Tally(sem("s_pp"), (2, 0), credit=2)
        s_sg = Tally(sem("s_sg"), (4, 0))
        s_sgf = Tally(sem("s_sgf"), (2, 0), credit=1)
        s_bin = [Tally(sem(f"s_bin{n}"), (0, n0), step=16) for n, n0 in ((0, 12), (1, 11))]
        s_br = [Tally(sem(f"s_br{n}"), (0, 6), step=32) for n in (0, 1)]
        s_rot = Tally(sem("s_rot"), (0, 4))
        s_sc = Tally(sem("s_sc"), (0, RH))
        s_sd2 = Tally(sem("s_sd2"), (0, RH))
        s_ro = Tally(sem("s_ro"), (0, RH))
        s_yr = Tally(sem("s_yr"), (0, RH))
        s_sz = Tally(sem("s_sz"), (0, 8))
        s_m = Tally(sem("s_m"), (0, 2))
        s_yb = Tally(sem("s_yb"), (0, 4))
        s_xin = sem("s_xin")
        s_const = sem("s_const")
        s_const2 = sem("s_const2")
        s_const3 = sem("s_const3")
        s_bconst = sem("s_bconst")
        s_rot0 = sem("s_rot0")
        s_tab = sem("s_tab")
        s_ang = sem("s_ang")
        s_sin = sem("s_sin")
        s_bmm = sem("s_bmm")
        s_bvec = sem("s_bvec")
        s_brow = sem("s_brow")
        s_le = sem("s_le")
        s_out = sem("s_out")

        block = ctx.enter_context(nc.Block())
        N_CONST, N_CONST2 = 7, 5

        @block.sync
        def _(sp):
            def unit(blk, L, u, src, kb, cols, slot):
                sp.wait_ge(s_lo.sem, s_lo.at(blk, L, u - RAW + 1))
                dst = raw[:, slot, 0:kb * cols].rearrange("p (k n) -> p k n", n=cols)
                return sp.dma_start(dst, src).then_inc(s_raw[slot].sem, 16)

            def rows(w, L, r0, kb, c0, cols):
                return w[bass.ds(L, 1), r0:r0 + kb * P, :][:, :, bass.ds(c0, cols)].rearrange(
                    "l (k p) n -> p (l k) n", p=P)

            def const(dst, src, sem_=s_const):
                sp.dma_start(dst, src).then_inc(sem_, 16)

            with nc.allow_non_contiguous_dma(reason="small parameters"):
                const(freq[:], a["c_freq"].partition_broadcast(P))
                const(posi[:], a["positions"].rearrange("b (m p) -> p (b m)", p=P))
                const(X[:], a["x"].rearrange("b (m p) d -> p (b m) d", p=P), s_xin)
                const(ident[:], a["c_ident"], s_xin)
                for n, name in enumerate(("norm_pre_mix", "norm_pre_mlp")):
                    const(pre[:, n], a[name].rearrange("l (k p) -> p l k", p=P), s_xin)
                for n, name in enumerate(("lambda_q1", "lambda_k1", "lambda_q2", "lambda_k2")):
                    const(lamv[:, n * 64:n * 64 + 64], a[name].rearrange("l n -> (l n)").partition_broadcast(P))
                const(lamc, a["c_lam"].partition_broadcast(P))

            with sp.Fori(0, DEPTH) as L:
                w = a["w_in"]
                with sp.Fori(0, 3) as i:
                    for c in range(2):
                        for k in range(2):
                            u = 2 * c + k
                            unit(0, L, 4 * i + u, rows(w, L, 512 * k, UK, i * 1024 + c * COLS, COLS), UK, COLS, u)
                for k in range(2):
                    unit(0, L, 12 + k, rows(w, L, 512 * k, UK, 6 * COLS, LAST1), UK, LAST1, k)
                w = a["w_out"]
                for n in range(4):
                    u = U_OUT + n
                    unit(0, L, u, rows(w, L, 512 * (n // 2), UK, n % 2 * COLS, COLS), UK, COLS, u % RAW)
                sp.wait_ge(s_mix.sem, s_mix.at(0, L, 1))
                for n, name in enumerate(("norm_post_mix", "norm_post_mlp")):
                    sp.dma_start(gains[:, n:n + 1, :], a[name][bass.ds(L, 1), :].partition_broadcast(P)).then_inc(
                        s_gain.sem, 16)
                sp.dma_start(PB[:], a["p"][bass.ds(L, 1)].rearrange("l b (m p) d -> p (l b m) d", p=P)).then_inc(
                    s_p.sem, 16)
                up, down = a["w_mlp_up"], a["w_mlp_down"]
                for k in range(2):
                    unit(0, L, U_MLP + k, rows(up, L, 512 * k, UK, 0, COLS), UK, COLS, (U_MLP + k) % RAW)
                with sp.Fori(0, 7) as i:
                    for k in range(2):
                        unit(0, L, 4 * i + U_MLP + 2 + k, rows(up, L, 512 * k, UK, i * COLS + COLS, COLS),
                             UK, COLS, (U_MLP + 2 + k) % RAW)
                    for n in range(2):
                        src = down[bass.ds(L, 1)][:, bass.ds(i * COLS, COLS), n * COLS:(n + 1) * COLS].rearrange(
                            "l (k p) n -> p (l k) n", p=P)
                        unit(0, L, 4 * i + U_MLP + 4 + n, src, UK, COLS, (U_MLP + 4 + n) % RAW)
                unit(0, L, U_PLE0, rows(a["w_ple_proj"], L, 0, 2, 0, COLS), 2, COLS, U_PLE0 % RAW)
                for n in range(2):
                    unit(0, L, U_DN7 + n, rows(down, L, 7 * COLS, UK, n * COLS, COLS), UK, COLS, (U_DN7 + n) % RAW)
                unit(0, L, U_PLE1, rows(a["w_ple_proj"], L, 0, 2, COLS, COLS), 2, COLS, U_PLE1 % RAW)
                for n in range(4):
                    u = U_PLE1 + 1 + n
                    unit(0, L, u, rows(a["w_ple_gate"], L, 512 * (n % 2), UK, n // 2 * COLS, COLS), UK, COLS, u % RAW)

            sp.wait_ge(s_mix.sem, s_mix.at(0, DEPTH, 0))
            with sp.Fori(0, DEPTH) as L:
                w = a["w_in_2"]

                def bias_in(c, c0, cols, slot):
                    sp.wait_ge(s_evac.sem, s_evac.at(1, L, c - 1))
                    src = a["b_in_2"][bass.ds(L, 1), :][:, bass.ds(c0, cols)].partition_broadcast(P)
                    sp.dma_start(BIN[:, slot:slot + 1, 0:cols], src).then_inc(s_bin[slot].sem, 16)

                def w_in_chunks(i, u0, c0, col0, chunks=2):
                    for c in range(chunks):
                        for k in range(2):
                            u = 2 * c + k
                            unit(1, L, 4 * i + u0 + u, rows(w, L, 512 * k, UK, i * 1024 + (col0 + c * COLS), COLS),
                                 UK, COLS, (u0 + u) % RAW)
                        bias_in(2 * i + c0 + c, i * 1024 + (col0 + c * COLS), COLS, (c0 + c) % 2)

                with sp.Fori(0, 3) as i:
                    w_in_chunks(i, 0, 0, 0)
                for k in range(2):
                    unit(1, L, 12 + k, rows(w, L, 512 * k, UK, 6 * COLS, LAST2), UK, LAST2, k)
                bias_in(6, 6 * COLS, LAST2, 0)
                sp.wait_ge(s_x.sem, s_x.at(1, L, 0))
                for n, name in enumerate(("ln1_g_2", "ln1_b_2")):
                    sp.dma_start(gains[:, n:n + 1, :], a[name][bass.ds(L, 1), :].partition_broadcast(P)).then_inc(
                        s_gain.sem, 16)
                w_in_chunks(0, V_RET, 7, RQ0, 1)
                sp.wait_ge(s_brow, 32)
                sp.wait_ge(s_t.sem, s_t.at(1, L, T2_QK))
                for q, (_, m, h) in enumerate(JOBS2):
                    if q >= 2:
                        sp.wait_ge(s_log.sem, s_log.at(1, L, q - 1))
                    n = (m + 1) * P
                    for part in range(2):
                        src = bass.AP(bias_rows.tensor, (18 * part + h) * 512 + (1 - m) * P,
                                      [[1, P], [HG * 512, 3], [1, n]]).bitcast(F32)
                        sp.dma_start(BR[part][:, 3 * (q % 2):3 * (q % 2) + 3, 0:n].bitcast(F32), src).then_inc(s_br[q % 2].sem, 16)
                with sp.Fori(0, 3) as i:
                    w_in_chunks(i, V_RET + 2, 8, RQ0 + COLS)
                w_in_chunks(0, V_RET + 14, 14, RQ0 + 7 * COLS, 1)
                with sp.Fori(0, 4) as i:
                    w_in_chunks(i, V_GATE, 15, RQ0 + 8 * COLS)
                for n in range(2):
                    unit(1, L, V_AP + n, rows(a["w_attn_proj_2"], L, 0, 3, n * COLS, COLS), 3, COLS, (V_AP + n) % RAW)
                for n in range(8):
                    u = V_RP + n
                    unit(1, L, u, rows(a["w_ret_proj_2"], L, 512 * (n % 4), UK, n // 4 * COLS, COLS), UK, COLS, u % RAW)
                for n in range(4):
                    u = V_OUT + n
                    unit(1, L, u, rows(a["w_out_2"], L, 512 * (n // 2), UK, n % 2 * COLS, COLS), UK, COLS, u % RAW)

                gate, up, down = a["w_ffn_gate_2"], a["w_ffn_up_2"], a["w_ffn_down_2"]

                def gate_up(j, u, k, slot):
                    sp.wait_ge(s_lo.sem, s_lo.at(1, L, u - RAW + 1))
                    dst = raw[:, slot].rearrange("p (k g n) -> p k g n", k=UK, g=2)
                    for g, wt in enumerate((gate, up)):
                        src = wt[bass.ds(L, 1), 512 * k:512 * k + 512, :][:, :, bass.ds(j * 256, 256)].rearrange(
                            "l (k p) n -> p (l k) n", p=P)
                        sp.dma_start(dst[:, :, g, :], src).then_inc(s_raw[slot].sem, 16)

                for k in range(2):
                    gate_up(0, V_FFN + k, k, (V_FFN + k) % RAW)
                with sp.Fori(0, FJ - 1) as i:
                    for k in range(2):
                        gate_up(i + 1, 4 * i + V_FFN + 2 + k, k, (V_FFN + 2 + k) % RAW)
                    for n in range(2):
                        src = down[bass.ds(L, 1)][:, bass.ds(i * 256, 256), n * COLS:(n + 1) * COLS].rearrange(
                            "l (k p) n -> p (l k) n", p=P)
                        unit(1, L, 4 * i + V_FFN + 4 + n, src, 2, COLS, (V_FFN + 4 + n) % RAW)
                for n in range(2):
                    unit(1, L, V_FFN + 42 + n, rows(down, L, (FJ - 1) * 256, 2, n * COLS, COLS), 2, COLS,
                         (V_FFN + 42 + n) % RAW)
                sp.wait_ge(s_x.sem, s_x.at(1, L, 1))
                for n, name in enumerate(("ln2_g_2", "ln2_b_2")):
                    sp.dma_start(gains[:, n:n + 1, :], a[name][bass.ds(L, 1), :].partition_broadcast(P)).then_inc(
                        s_gain.sem, 16)
            sp.wait_ge(s_x.sem, s_x.at(1, DEPTH, 0))
            sp.dma_start(out.rearrange("b (m p) d -> p (b m) d", p=P), X[:]).then_inc(s_out, 16)
            sp.wait_ge(s_out, 16)

        def landed(blk, L, i, c):
            o, slot = i + c // RAW, c % RAW
            k = o + 1
            if blk and c >= V_FFN:
                if slot < 2:
                    k = o + 2
                elif c >= UNITS2 - 2:
                    k = o + FJ
                else:
                    k = o * 2 - (2 * (V_FFN // RAW) - 17)
            return s_raw[slot].at(blk, L, k)

        def size(blk, c):
            if blk == 0:
                return UK * LAST1 if c in (12, 13) else 2 * COLS if c in (U_PLE0, U_PLE1) else UNIT
            if c in (12, 13):
                return UK * LAST2
            if c in (V_AP, V_AP + 1):
                return 3 * COLS
            small_unit = c >= UNITS2 - 2 or (c >= V_FFN + 4 and c % RAW < 2)
            return 2 * COLS if small_unit else UNIT

        def logit_set(q):
            g = G[:, 2 * (q % 2):2 * (q % 2) + 2, :]
            return g.rearrange("p b (u s) -> p (b u) s", s=S)

        def logit(q, u):
            return G[:, 2 * (q % 2) + u % 2, u // 2 * S:(u // 2 + 1) * S]

        def rope(eng, engine, scratch, col, heads, d, tab):
            h = d // 2
            x = Z[:, :, col:col + heads * d].rearrange("p m (h d) -> p m h d", d=d)
            u = scratch[:, 0:TILES * heads * d].rearrange("p (m h d) -> p m h d", m=TILES, d=d)
            sin = lambda a_, b_: sind[:, :, tab + a_:tab + b_].unsqueeze(2).to_broadcast([P, TILES, heads, b_ - a_])
            cos = cosd[:, :, tab:tab + d].unsqueeze(2).to_broadcast([P, TILES, heads, d])
            engine.tensor_tensor(u[:, :, :, 0:h], x[:, :, :, h:d], sin(0, h), ALU.mult)
            engine.tensor_tensor(u[:, :, :, h:d], x[:, :, :, 0:h], sin(h, d), ALU.mult)
            eng.drain()
            engine.tensor_tensor(x, x, cos, ALU.mult)
            eng.drain()
            return engine.tensor_tensor(x, x, u, ALU.add)

        def pair(n):
            return A[:, :, :] if n == 2 else G[:, 2 * n:2 * n + 2, :]

        @block.tensor
        def _(pe):
            def unit(blk, L, i, c, hx, lx, k0, kb, cols, dst, first, last, halves=False):
                hi = whi[:, c % PARTS, 0:kb * cols].rearrange("p (k n) -> p k n", n=cols)
                lo = wlo[:, c % PARTS, 0:kb * cols].rearrange("p (k n) -> p k n", n=cols)
                pe.wait_ge(s_hi.sem, s_hi.at(blk, L, 4 * i + c + 1))
                for k in range(kb):
                    for m in range(TILES):
                        rows = slice(m * P, (m + 1) * P)
                        nc.tensor.matmul(dst(m), hx[:, k0 + k, rows], hi[:, k, :], start=first and k == 0, stop=False)
                        nc.tensor.matmul(dst(m), lx[:, k0 + k, rows], hi[:, k, :], start=False, stop=False)
                pe.wait_ge(s_lo.sem, s_lo.at(blk, L, 4 * i + c + 1))
                order = [(k, m) for m in range(TILES) for k in range(kb)] if halves else \
                    [(k, m) for k in range(kb) for m in range(TILES)]
                for k, m in order:
                    mm = nc.tensor.matmul(dst(m), hx[:, k0 + k, m * P:(m + 1) * P], lo[:, k, :],
                                          start=False, stop=last and k == kb - 1)
                    if halves and (k, m) == (kb - 1, 0):
                        mm.then_inc(s_half.sem, 1)
                mm.then_inc(s_used.sem, 1)

            def bank_pair(n, cols=COLS):
                return lambda m: pair(n)[:, m, 0:cols]

            def chunk(blk, L, i, c, group, cols=COLS, hx=XH, lx=XL):
                for k in range(2):
                    unit(blk, L, i, c + k, hx, lx, UK * k, UK, cols, bank_pair(group, cols), k == 0, k == 1)

            def transposes(blk, L, i, t, blocks):
                pe.wait_ge(s_tfree.sem, s_tfree.at(blk, L, 2 * i + t - 1))
                for n, src in enumerate(blocks):
                    tr = nc.tensor.transpose(T[:, t % 2, n * P:(n + 1) * P], src, ident[:])
                tr.then_inc(s_t.sem, 1)

            def both(src, blocks):
                return [src[:, m, b * P:(b + 1) * P] for b in blocks for m in range(TILES)]

            def first_chunk(blk, L, c, t, xh, x, group=0):
                for k, (ready, n) in enumerate(((s_xh, xh), (s_x, x))):
                    pe.wait_ge(ready.sem, ready.at(blk, L, n))
                    turn(blk, L, 0, t + 2 * k, X[:, :, k * COLS:(k + 1) * COLS], UK)
                for k in range(2):
                    pe.wait_ge(s_tfree.sem, s_tfree.at(blk, L, t + 2 + 2 * k))
                    unit(blk, L, 0, c + k, XH, XL, UK * k, UK, COLS, bank_pair(group), k == 0, k == 1)

            def second_chunk(blk, L, c, between):
                unit(blk, L, 0, c, XH, XL, 0, UK, COLS, bank_pair(0), True, False)
                between()
                unit(blk, L, 0, c + 1, XH, XL, UK, UK, COLS, bank_pair(0), False, True)

            def turn(blk, L, i, t, src, nblocks, per=2):
                for b in range(0, nblocks, per):
                    transposes(blk, L, i, t + b // per, both(src, range(b, min(b + per, nblocks))))

            def job_outputs(blk, L, q, jobs, t0):
                kind, m, x = jobs[q]
                pe.wait_ge(s_tfree.sem, s_tfree.at(blk, L, t0 + job_end(jobs, q)))
                if jobs is JOBS1 and q == 0:
                    pe.wait_ge(s_evac.sem, s_evac.at(0, L, CH1))
                pe.wait_ge(s_o.sem, s_o.at(blk, L, q - 1))
                for u in range(3 if kind == "E" else 4):
                    for kt in range(m + 1):
                        if kind == "E":
                            v = Z2[:, kt, 2 * ATTN_W + (u * HG + x) * HD:][:, 0:HD]
                            mm = nc.tensor.matmul(A[:, q % 2, 0:HD], PT2[:, q % 2, kt, u * P:(u + 1) * P], v,
                                                  start=(u == 0 and kt == 0), stop=(u == 2 and kt == m))
                        else:
                            col = {"A": A_V + u * HD, "B": B_V + u * HD, "D": D_V + u // 2 * HD,
                                   "C": C_V + (2 * (u // 2) + x) * HD}[kind]
                            mm = nc.tensor.matmul(A[:, q % 2, u * HD:(u + 1) * HD], PT[:, q % 2, kt, u * P:(u + 1) * P],
                                                  Z[:, kt, col:col + HD], start=kt == 0, stop=kt == m)
                mm.then_inc(s_pv.sem, 1)

            def job_turn(blk, L, q, jobs, t0, probs):
                kind, m, _ = jobs[q]
                pe.wait_ge(s_exp.sem, s_exp.at(blk, L, q + 1))
                for kt in range(m + 1):
                    t = t0 + job_banks(jobs, q) + kt
                    transposes(blk, L, 0, t, [probs[:, q % 2, u, kt * P:(kt + 1) * P]
                                              for u in range(3 if kind == "E" else 4)])

            pe.wait_ge(s_bconst, 48)
            nc.tensor.matmul(T[0:18, 0, :], arena[0:32, 256:274], arena[0:32, 512:1024], start=True, stop=True).then_inc(s_bmm, 1)
            pe.sem_inc(s_used.sem, s_used.credit)
            pe.wait_ge(s_xin, 64)
            pe.wait_ge(s_bvec, 1)

            def logits1(L, q):
                kind, m, x = JOBS1[q]
                n = (m + 1) * P
                rows = slice(m * P, (m + 1) * P)
                if kind == "A":
                    pe.wait_ge(s_am.sem, s_am.at(0, L, m + 1))
                if kind in "CD":
                    q0 = Q_TURN_C if kind == "C" else Q_TURN_D
                    pe.wait_ge(s_tfree.sem, s_tfree.at(0, L, T_JOB + job_banks(JOBS1, q0)))
                if kind == "B":
                    pe.wait_ge(s_const3, 64)
                    pe.wait_ge(s_lf.sem, s_lf.at(0, L, 3))
                pe.wait_ge(s_exp.sem, s_exp.at(0, L, q - 1))
                for u in range(4):
                    dst = logit(q, u)
                    if kind == "C":
                        qb, kb = 13 + u // 2, 15 + u // 2
                        part = slice(32 * (2 * x + u % 2), 32 * (2 * x + u % 2) + 32)
                    else:
                        qb, kb = {"A": (5 + u // 2, 7 + u // 2), "B": (9 + u // 2, 11 + u // 2),
                                  "D": (17 + u // 2, 19 + u // 2)}[kind]
                        part = slice(HD * (u % 2), HD * (u % 2) + HD)
                    nc.tensor.matmul(dst[:, 0:n], QT[part, qb, rows], QT[part, kb, 0:n], start=True, stop=False)
                    if kind == "A":
                        mm = nc.tensor.matmul(dst[:, 0:n], identb[:], amask[:, m, 0:n], start=False, stop=True)
                        continue
                    if kind == "B":
                        for kt in range(m + 1):
                            nc.tensor.matmul(dst[:, kt * P:n], LF[:, 4, kt, u:u + 1].to_broadcast([P, P]),
                                             tri[:, kt, kt * P:n], start=False, stop=False)
                    if kind == "D" and m == 1:
                        nc.tensor.matmul(dst[:, 0:P], identb[:], maskb[:, 1], start=False, stop=False)
                    mm = nc.tensor.matmul(dst[:, m * P:n], identb[:], maskb[:, 0], start=False, stop=True)
                mm.then_inc(s_log.sem, 1)

            def logits2(L, q):
                _, m, h = JOBS2[q]
                n = (m + 1) * P
                part = slice(HD * (h % 2), HD * (h % 2) + HD)
                pe.wait_ge(s_exp.sem, s_exp.at(1, L, q - 1))
                pe.wait_ge(s_br[q % 2].sem, s_br[q % 2].at(1, L, q // 2 + 1))
                dst = logit_set(q)
                for g in range(3):
                    b = 3 * g + h // 2
                    nc.tensor.matmul(dst[:, g, 0:n], QT2[part, b, m * P:(m + 1) * P], QT2[part, 9 + b, 0:n],
                                     start=True, stop=False)
                    for b_part in range(2):
                        mm = nc.tensor.matmul(dst[:, g, 0:n], flip[:], BR[b_part][:, 3 * (q % 2) + g, 0:n],
                                              start=False, stop=b_part == 1)
                mm.then_inc(s_log.sem, 1)

            def run_jobs(blk, L, jobs, t0, logits, probs, beside=None):
                for q in range(len(jobs) + 2):
                    if beside:
                        beside(q, False)
                    if q < len(jobs):
                        logits(L, q)
                    if beside:
                        beside(q, True)
                    if 1 <= q <= len(jobs):
                        job_turn(blk, L, q - 1, jobs, t0, probs)
                    if q >= 2:
                        job_outputs(blk, L, q - 2, jobs, t0)

            with pe.Fori(0, DEPTH) as L:
                first_chunk(0, L, 0, 0, 0, 0)
                for c in range(1, 4):
                    pe.wait_ge(s_evac.sem, s_evac.at(0, L, c - 1))
                    chunk(0, L, 0, 2 * c, c % 2)

                zb = lambda col: [Z[:, m, col:col + P] for m in range(TILES)]
                db = lambda col: [DUP[:, m, col:col + P] for m in range(TILES)]

                def turn_qk(t, *blocks):
                    for b in range(0, len(blocks), 2):
                        transposes(0, L, 0, T_QK + t + b // 2, sum(blocks[b:b + 2], []))

                def dots(m, heads, n_dot):
                    n = (m + 1) * P
                    for h in heads:
                        part = slice(HD * (h % 2), HD * (h % 2) + HD)
                        j = (h - heads[0]) // 2
                        mm = nc.tensor.matmul(A[:, h % 2, j * n:(j + 1) * n], QT[part, h // 2, m * P:n],
                                              QT[part, 4, 0:n], start=True, stop=True)
                    mm.then_inc(s_dot.sem, 1)

                def w_in_unit(c, k, cols=COLS):
                    bank = 2 if c == CH1 - 1 else c % 2
                    unit(0, L, 0, 2 * c + k, XH, XL, UK * k, UK, cols, bank_pair(bank, cols), k == 0, k == 1)

                pe.wait_ge(s_rope.sem, s_rope.at(0, L, 1))
                turn_qk(0, *[zb(A_IQ + n * P) for n in range(4)], db(0))
                pe.wait_ge(s_evac.sem, s_evac.at(0, L, 3))
                w_in_unit(4, 0)
                pe.wait_ge(s_tfree.sem, s_tfree.at(0, L, T_QK + 3))
                dots(0, range(IDX_HEADS), 1)
                w_in_unit(4, 1)
                pe.wait_ge(s_rl.sem, s_rl.at(0, L, 1))
                dots(1, range(4), 2)
                pe.wait_ge(s_prope.sem, s_prope.at(0, L, 1))
                turn_qk(3, zb(A_Q), zb(A_Q + P), zb(A_K), zb(A_K + P))
                pe.wait_ge(s_evac.sem, s_evac.at(0, L, 4))
                w_in_unit(5, 0)
                pe.wait_ge(s_rl.sem, s_rl.at(0, L, 2))
                dots(1, range(4, 8), 3)
                turn_qk(5, zb(B_Q), zb(B_Q + P), zb(B_K), zb(B_K + P))
                w_in_unit(5, 1)
                pe.wait_ge(s_tfree.sem, s_tfree.at(0, L, T_JOB))
                pe.wait_ge(s_evac.sem, s_evac.at(0, L, 5))
                pe.wait_ge(s_rl.sem, s_rl.at(0, L, 3))

                def beside(q, logits_made):
                    if not logits_made:
                        if q == Q_TURN_D + 1:
                            pe.wait_ge(s_rope.sem, s_rope.at(0, L, 2))
                            pe.wait_ge(s_prope.sem, s_prope.at(0, L, 3))
                            pe.wait_ge(s_tfree.sem, s_tfree.at(0, L, T_JOB + job_end(JOBS1, Q_TURN_D - 1)))
                            turn_qk(T_JOB - T_QK + job_banks(JOBS1, Q_TURN_D) - 2, zb(D_Q), zb(D_Q + P), db(P), db(2 * P))
                    elif q == 0:
                        w_in_unit(6, 0, LAST1)
                        pe.wait_ge(s_evac.sem, s_evac.at(0, L, 6))
                    elif q == Q_TURN_C + 1:
                        pe.wait_ge(s_prope.sem, s_prope.at(0, L, 2))
                        pe.wait_ge(s_tfree.sem, s_tfree.at(0, L, T_JOB + job_end(JOBS1, Q_TURN_C - 1)))
                        turn_qk(T_JOB - T_QK + job_banks(JOBS1, Q_TURN_C) - 2, zb(C_Q), zb(C_Q + P), zb(C_K), zb(C_K + P))
                        w_in_unit(6, 1, LAST1)
                        pe.wait_ge(s_tfree.sem, s_tfree.at(0, L, T_JOB + job_banks(JOBS1, Q_TURN_C)))
                    elif q == Q_TURN_D + 1:
                        pe.wait_ge(s_tfree.sem, s_tfree.at(0, L, T_JOB + job_banks(JOBS1, Q_TURN_D)))

                run_jobs(0, L, JOBS1, T_JOB, logits1, PR, beside)

                pe.wait_ge(s_o.sem, s_o.at(0, L, len(JOBS1)))
                turn(0, L, 0, T_MIX, Z[:, :, MIX0:MIX0 + DM], UK)
                pe.wait_ge(s_tfree.sem, s_tfree.at(0, L, T_MIX + 2))
                unit(0, L, 0, U_OUT, XH, XL, 0, UK, COLS, bank_pair(1), True, False)
                pe.wait_ge(s_mix.sem, s_mix.at(0, L, 1))
                turn(0, L, 0, T_MIX + 2, Z[:, :, MIX0 + UK * P:MIX0 + DM], UK)
                unit(0, L, 0, U_OUT + 1, XH, XL, 0, UK, COLS, bank_pair(0), True, False)
                pe.wait_ge(s_tfree.sem, s_tfree.at(0, L, T_N2))
                for n in range(2):
                    unit(0, L, 0, U_OUT + 2 + n, XH, XL, UK, UK, COLS, bank_pair(1 - n), False, True, n == 1)


                def inner_turn(i, j):
                    pe.wait_ge(s_h.sem, s_h.at(0, L, i + j + 1))
                    turn(0, L, i, T_MLP + 2 * j, H, UK)

                def down(i, c, first, last, t):
                    pe.wait_ge(s_tfree.sem, s_tfree.at(0, L, 2 * i + t))
                    for n in range(2):
                        unit(0, L, i, c + n, MH, ML, 0, UK, COLS, bank_pair(1 + n), first, last, last and n == 1)

                first_chunk(0, L, U_MLP, T_N2, 1, 1, 2)
                pe.wait_ge(s_p.sem, s_p.at(0, L, 1))
                turn(0, L, 0, T_P, PB, 2, per=1)
                second_chunk(0, L, U_MLP + 2, lambda: inner_turn(0, 0))
                down(0, U_MLP + 4, True, False, T_MLP + 2)
                inner_turn(0, 1)
                with pe.Fori(0, 6) as i:
                    chunk(0, L, i, U_MLP + 6, 0)
                    down(i, U_MLP + 8, False, False, T_MLP + 4)
                    inner_turn(i, 2)
                unit(0, L, 0, U_PLE0, YH, YL, 0, 2, COLS, bank_pair(0), True, True)
                down(0, U_DN7, False, True, T_MLP + 16)
                pe.wait_ge(s_sq.sem, s_sq.at(0, L, 6))
                pe.wait_ge(s_ng.sem, s_ng.at(0, L, 6))
                unit(0, L, 0, U_PLE1, YH, YL, 0, 2, COLS, bank_pair(1), True, True)
                pe.wait_ge(s_pp.sem, s_pp.at(0, L, 1))
                first_chunk(0, L, U_PLE1 + 1, T_PX, 2, 2)
                pe.wait_ge(s_pp.sem, s_pp.at(0, L, 2))
                chunk(0, L, 0, U_PLE1 + 3, 1)

            with pe.Fori(0, DEPTH) as L:
                def w_in_chunk(i, c, u):
                    pe.wait_ge(s_evac.sem, s_evac.at(1, L, 2 * i + c - 1))
                    chunk(1, L, i, u, c % 2)

                first_chunk(1, L, 0, 0, 0, 0)
                with pe.Fori(0, 2) as i:
                    for c in range(1, 3):
                        w_in_chunk(i, c, 2 * c)
                w_in_chunk(0, 5, 10)
                pe.wait_ge(s_evac.sem, s_evac.at(1, L, 5))
                turn(1, L, 0, T2_QK, Z2, 18)
                chunk(1, L, 0, 12, 2, LAST2)

                def v_there(q, logits_made):
                    if q == 2 and logits_made:
                        pe.wait_ge(s_evac.sem, s_evac.at(1, L, SEG1))

                pe.wait_ge(s_tfree.sem, s_tfree.at(1, L, T2_JOB))
                pe.wait_ge(s_evac.sem, s_evac.at(1, L, 6))
                run_jobs(1, L, JOBS2, T2_JOB, logits2, PR2, v_there)
                pe.wait_ge(s_o.sem, s_o.at(1, L, len(JOBS2)))
                turn(1, L, 0, T2_YA, Z2, 3, per=1)

                def scores(h):
                    for kt in range(TILES):
                        for b in range(2):
                            o = A[:, h % 2, 0:S] if kt == 0 else A[:, h % 2, S:S + P]
                            mm = nc.tensor.matmul(o, QTR[:, 8 + 2 * h + b, kt * P:(kt + 1) * P],
                                                  QTR[:, 2 * h + b, kt * P:S], start=b == 0, stop=b == 1)
                    mm.then_inc(s_sc.sem, 1)

                def outputs(h):
                    v = lambda kt: VR[:, kt, h * RDV:(h + 1) * RDV]
                    nc.tensor.matmul(A[:, 0], SCT[:, h, 0:P], v(0), start=True, stop=True)
                    nc.tensor.matmul(A[:, 1], SCT[:, h, P:S], v(0), start=True, stop=False)
                    nc.tensor.matmul(A[:, 1], SCT[:, h, S:S + P], v(1), start=False, stop=True).then_inc(s_ro.sem, 1)

                with pe.Fori(0, 2) as i:
                    for c in range(2):
                        w_in_chunk(i, SEG1 + c, V_RET + 2 * c)
                w_in_chunk(0, 11, V_RET + 8)
                pe.wait_ge(s_rot.sem, s_rot.at(1, L, 4))
                turn(1, L, 0, T2_RET, QK, 16)
                w_in_chunk(0, 12, V_RET + 10)
                pe.wait_ge(s_tfree.sem, s_tfree.at(1, L, T2_YB))
                scores(0)
                scores(1)
                w_in_chunk(0, 13, V_RET + 12)
                pe.wait_ge(s_sd2.sem, s_sd2.at(1, L, 2))
                scores(2)
                scores(3)
                w_in_chunk(0, 14, V_RET + 14)

                for h in range(RH):
                    c = 15 + h
                    pe.wait_ge(s_evac.sem, s_evac.at(1, L, c - 1))
                    unit(1, L, 0, V_GATE + 2 * h, XH, XL, 0, UK, COLS, bank_pair(c % 2), True, False)
                    if h:
                        pe.wait_ge(s_yr.sem, s_yr.at(1, L, h))
                    else:
                        pe.wait_ge(s_sd2.sem, s_sd2.at(1, L, RH))
                        pe.wait_ge(s_evac.sem, s_evac.at(1, L, 15))
                    outputs(h)
                    unit(1, L, 0, V_GATE + 2 * h + 1, XH, XL, UK, UK, COLS, bank_pair(c % 2), False, True)
                w_in_chunk(0, 19, V_GATE + 8)
                w_in_chunk(0, 20, V_GATE + 10)
                pe.wait_ge(s_yb.sem, s_yb.at(1, L, 4))
                turn(1, L, 0, T2_YB, QK[:, :, DM:], KB)
                w_in_chunk(0, 21, V_GATE + 12)
                w_in_chunk(0, 22, V_GATE + 14)
                for n in range(2):
                    turn(1, L, 0, T2_YB + 4 + 2 * n, QK[:, :, n * COLS:(n + 1) * COLS], UK)
                    pe.wait_ge(s_evac.sem, s_evac.at(1, L, 22 + n))
                    unit(1, L, 0, V_AP + n, MH, ML, 0, 3, COLS, bank_pair(1 - n), True, True)
                pe.wait_ge(s_tfree.sem, s_tfree.at(1, L, T2_M))
                for n in range(2):
                    pe.wait_ge(s_evac.sem, s_evac.at(1, L, 24 + n))
                    for k in range(4):
                        if n == 1 and k == 2:
                            pe.wait_ge(s_m.sem, s_m.at(1, L, 1))
                            turn(1, L, 0, T2_M, M, UK)
                        hx, lx = (XH, XL) if k < 2 else (YH, YL)
                        unit(1, L, 0, V_RP + 4 * n + k, hx, lx, UK * (k % 2), UK, COLS, bank_pair(1 - n), k == 0, k == 3)
                pe.wait_ge(s_tfree.sem, s_tfree.at(1, L, T2_M + 2))
                unit(1, L, 0, V_OUT, XH, XL, 0, UK, COLS, bank_pair(1), True, False)
                pe.wait_ge(s_m.sem, s_m.at(1, L, 2))
                turn(1, L, 0, T2_M + 2, M[:, :, COLS:DM], UK)
                unit(1, L, 0, V_OUT + 1, XH, XL, 0, UK, COLS, bank_pair(0), True, False)
                pe.wait_ge(s_tfree.sem, s_tfree.at(1, L, T2_FX))
                for n in range(2):
                    unit(1, L, 0, V_OUT + 2 + n, XH, XL, UK, UK, COLS, bank_pair(1 - n), False, True, n == 1)


                def inner_turn2(i, j):
                    pe.wait_ge(s_h.sem, s_h.at(1, L, i + j + 1))
                    turn(1, L, i, T2_FFN + 2 * j, H2, 2, per=1)

                def down2(i, c, first, last, t):
                    pe.wait_ge(s_tfree.sem, s_tfree.at(1, L, 2 * i + t))
                    for n in range(2):
                        unit(1, L, i, c + n, MH, ML, 0, 2, COLS, bank_pair(1 + n), first, last, last and n == 1)

                first_chunk(1, L, V_FFN, T2_FX, 1, 1, 2)
                second_chunk(1, L, V_FFN + 2, lambda: inner_turn2(0, 0))
                down2(0, V_FFN + 4, True, False, T2_FFN + 2)
                inner_turn2(0, 1)
                with pe.Fori(0, FJ - 2) as i:
                    chunk(1, L, i, V_FFN + 6, 0)
                    down2(i, V_FFN + 8, False, False, T2_FFN + 4)
                    inner_turn2(i, 2)
                down2(0, V_FFN + 42, False, True, T2_FFN + 2 * FJ)

        @block.scalar
        def _(act):
            def act_(out_, in_, func, **kw):
                return nc.scalar.activation(out_, in_, func, **kw)

            def hi(blk, L, i, c):
                n, slot = size(blk, c), c % RAW
                act.wait_ge(s_raw[slot].sem, landed(blk, L, i, c))
                act.wait_ge(s_used.sem, s_used.at(blk, L, 4 * i + c - 1))
                act_(whi[:, c % PARTS, 0:n], raw[:, slot, 0:n], ACT.Copy).then_inc(s_hi.sem, 1)

            def his(blk, L, i, *cs):
                for c in cs:
                    hi(blk, L, i, c)

            def turn_hi(blk, L, i, t, n, dst, per=2, gain=None):
                for b in range(0, n, per):
                    tt = t + b // per
                    act.wait_ge(s_t.sem, s_t.at(blk, L, 2 * i + tt + 1))
                    k = min(per, n - b)
                    src = T[:, tt % 2, 0:k * S].rearrange("p (k s) -> p k s", s=S)
                    if gain is None:
                        ins = act_(dst[:, b:b + k, :], src, ACT.Copy)
                    else:
                        for kk in range(k):
                            ins = act_(dst[:, b + kk, :], src[:, kk, :], ACT.Copy, scale=gain[:, b + kk:b + kk + 1])
                    ins.then_inc(s_thi.sem, 1)

            def turn_copy(blk, L, t, n, dst):
                for b in range(0, n, 2):
                    tt = t + b // 2
                    act.wait_ge(s_t.sem, s_t.at(blk, L, tt + 1))
                    k = min(2, n - b)
                    act_(dst[:, b:b + k, :], T[:, tt % 2, 0:k * S].rearrange("p (k s) -> p k s", s=S),
                         ACT.Copy).then_inc(s_tfree.sem, 1)

            def root(blk, L, k, norm, n):
                act.wait_ge(s_ms.sem, s_ms.at(blk, L, k))
                act_(stat[:, 1, norm, 0:n], stat[:, 0, norm, 0:n], ACT.Sqrt).then_inc(s_sd.sem, 1)

            def exps(blk, L, q, jobs, probs):
                kind, m, _ = jobs[q]
                n = (m + 1) * P
                act.wait_ge(s_nm.sem, s_nm.at(blk, L, q + 1))
                src = logit_set(q)
                if kind == "E":
                    act_(probs[:, q % 2, :, 0:n], src[:, 0:3, 0:n], ACT.Exp, bias=nm[:, q, 0:1], scale=SCALE[kind],
                         accum_out=ls[:, q, 0:1]).then_inc(s_exp.sem, 1)
                    return
                if kind == "D":
                    act_(es[:, q, :], ds_[:, q, :], ACT.Exp)
                for u in range(4):
                    ins = act_(probs[:, q % 2, u, 0:n], logit(q, u)[:, 0:n], ACT.Exp, bias=nm[:, q, u:u + 1],
                               scale=SCALE[kind], accum_out=ls[:, q, u:u + 1])
                ins.then_inc(s_exp.sem, 1)

            def const(dst, src, sem_=s_const2):
                act.dma_start(dst, src).then_inc(sem_, 16)

            with nc.allow_non_contiguous_dma(reason="small parameters"):
                const(arena[0:32, 256:274], a["rel_bias_2"], s_bconst)
                const(arena[0:32, 512:1024], a["c_onehot"], s_bconst)
                const(arena[0:18, 1024:2048].rearrange("p (a b) -> p a b", a=2), a["c_ok"], s_bconst)
                const(arena[:, 2560:2688], a["c_flip"])
                const(room(0, 2, P), a["c_masks"])
                const(bforget, a["b_forget"].rearrange("l n -> (l n)").partition_broadcast(P))
                const(sink, a["sinks"].rearrange("l n -> (l n)").partition_broadcast(P))
                const(subln, a["diff_subln"].rearrange("l n -> (l n)").partition_broadcast(P))
            act.sem_inc(s_exp.sem, s_exp.credit)
            act.wait_ge(s_tab, 1)
            act_(lsum, lsum, ACT.Exp).then_inc(s_le, 1)
            act.wait_ge(s_ang, 1)
            act_(cosd[:], sind[:], ACT.Sin, scale=0.5)
            act.drain()
            act_(sind[:], sind[:], ACT.Sin).then_inc(s_sin, 1)
            act.wait_ge(s_xin, 64)
            act.wait_ge(s_bvec, 1)
            for n in range(2):
                act.dma_start(bias_rows[n].bitcast(F32), BR[n][0:18, 0:2, :].rearrange("p k s -> p (k s)").bitcast(
                    F32)).then_inc(s_brow, 16)

            with act.Fori(0, DEPTH) as L:
                act.wait_ge(s_cur.sem, s_cur.at(0, L, 1))
                turn_hi(0, L, 0, 0, UK, XH, gain=prec[:, 0])
                hi(0, L, 0, 0)
                turn_hi(0, L, 0, 2, UK, XH[:, UK:KB], gain=prec[:, 0, UK:KB])
                hi(0, L, 0, 1)
                act.wait_ge(s_x.sem, s_x.at(0, L, 0))
                for m in range(TILES):
                    ins = act_(room(12288, TILES, DM)[:, m], X[:, m, :], ACT.Square, accum_out=stat[:, 0, 0, m:m + 1])
                ins.then_inc(s_ss.sem, 1)
                root(0, L, 1, 0, 2)

                def project(i, c, cols=COLS):
                    act.wait_ge(s_used.sem, s_used.at(0, L, 4 * i + 2 * c + 2))
                    for m in range(TILES):
                        dst = Z[:, m, c * COLS:c * COLS + cols] if isinstance(i, int) else \
                            Z[:, m, bass.ds(i * 1024 + c * COLS, cols)]
                        src = pair(2 if c == CH1 - 1 else c % 2)[:, m, 0:cols]
                        ins = act_(dst, src, ACT.Copy, scale=stat[:, 2, 0, m:m + 1])
                    ins.then_inc(s_evac.sem, 1)

                act.wait_ge(s_rs.sem, s_rs.at(0, L, 1))
                for c in range(3):
                    his(0, L, 0, 2 * c + 2, 2 * c + 3)
                    project(0, c)

                def relus(n_dot, m, heads):
                    n, nj = (m + 1) * P, len(heads) // 2
                    act.wait_ge(s_dot.sem, s_dot.at(0, L, n_dot))
                    act.wait_ge(s_rlf.sem, s_rlf.at(0, L, m))
                    dst = RL[:, heads[0]:heads[0] + len(heads), 0:n].rearrange("p (j b) s -> p b j s", b=2)
                    act_(dst, A[:, :, 0:nj * n].rearrange("p b (j s) -> p b j s", s=n), ACT.Relu).then_inc(s_rl.sem, 1)

                hi(0, L, 0, 8)
                turn_copy(0, L, T_QK, 5, QT)
                hi(0, L, 0, 9)
                project(0, 3)
                hi(0, L, 0, 10)
                relus(1, 0, range(IDX_HEADS))
                hi(0, L, 0, 11)
                project(0, 4)
                relus(2, 1, range(4))
                act.wait_ge(s_lf.sem, s_lf.at(0, L, 1))
                act_(LF[:, 1], LF[:, 1], ACT.Exp).then_inc(s_lg.sem, 1)
                turn_copy(0, L, T_QK + 3, 4, QT[:, 5:9])
                hi(0, L, 0, 12)
                act.wait_ge(s_lf.sem, s_lf.at(0, L, 2))
                act_(LF[:, 2], LF[:, 2], ACT.Ln).then_inc(s_lg.sem, 1)
                relus(3, 1, range(4, 8))
                turn_copy(0, L, T_QK + 5, 4, QT[:, 9:13])
                hi(0, L, 0, 13)
                project(0, 5)
                for q in range(len(JOBS1)):
                    exps(0, L, q, JOBS1, PR)
                    if q == Q_TURN_C + 1:
                        turn_copy(0, L, T_JOB + job_banks(JOBS1, Q_TURN_C) - 2, 4, QT[:, 13:17])
                        project(0, 6, LAST1)
                    elif q == Q_TURN_D:
                        turn_copy(0, L, T_JOB + job_banks(JOBS1, Q_TURN_D) - 2, 4, QT[:, 17:21])
                    elif q in (3, 4):
                        hi(0, L, 0, 11 + q)
                turn_hi(0, L, 0, T_MIX, UK, XH)
                root(0, L, 2, 1, 8)
                hi(0, L, 0, U_OUT + 2)
                turn_hi(0, L, 0, T_MIX + 2, UK, XH[:, UK:KB])

                def squares(k, c, bank, used):
                    for m in range(TILES):
                        if c == 1 and m == 0:
                            act.wait_ge(s_half.sem, s_half.at(0, L, k // 2))
                        elif c == m:
                            act.wait_ge(s_used.sem, s_used.at(0, L, used))
                        act_(room(8192, 2, TILES, COLS)[:, c, m], pair(bank)[:, m, :], ACT.Square,
                             accum_out=stat[:, 0, k, 2 * c + m:2 * c + m + 1]).then_inc(s_sq.sem, 1)

                his(0, L, 0, U_OUT + 3, U_OUT + 4)
                squares(2, 0, 1, U_OUT + 3)
                squares(2, 1, 0, U_OUT + 4)
                root(0, L, 3, 2, 2)

                turn_hi(0, L, 0, T_N2, KB, XH, gain=prec[:, 1])
                hi(0, L, 0, U_OUT + 5)
                act.wait_ge(s_x.sem, s_x.at(0, L, 1))
                for m in range(TILES):
                    ins = act_(room(12288, TILES, DM)[:, m], X[:, m, :], ACT.Square, accum_out=stat[:, 0, 3, m:m + 1])
                ins.then_inc(s_ss.sem, 1)
                root(0, L, 4, 3, 2)
                act.wait_ge(s_rs.sem, s_rs.at(0, L, 2))

                def inner(i, j, used, bank=0):
                    act.wait_ge(s_used.sem, s_used.at(0, L, 4 * i + used))
                    for m in range(TILES):
                        ins = act_(H[:, m, :], pair(bank)[:, m, :], ACT.Relu, scale=stat[:, 2, 3, m:m + 1])
                    ins.then_inc(s_act.sem, 1)

                hi(0, L, 0, U_MLP + 2)
                inner(0, 0, U_MLP + 2, 2)
                act.wait_ge(s_brow, 32)
                turn_hi(0, L, 0, T_P, 2, YH, per=1)
                hi(0, L, 0, U_MLP + 3)
                turn_hi(0, L, 0, T_MLP, UK, MH)
                with act.Fori(0, 6) as i:
                    his(0, L, i, U_MLP + 4, U_MLP + 5)
                    inner(i, 1, U_MLP + 4)
                    his(0, L, i, U_MLP + 6, U_MLP + 7)
                    turn_hi(0, L, i, T_MLP + 2, UK, MH)
                his(0, L, 0, U_MLP + 28, U_MLP + 29)
                inner(0, 7, U_MLP + 28)
                hi(0, L, 0, U_PLE0)
                turn_hi(0, L, 0, T_MLP + 14, UK, MH)
                his(0, L, 0, U_DN7, U_DN7 + 1, U_PLE1)
                squares(4, 0, 1, U_DN7 + 1)
                squares(4, 1, 2, U_DN7 + 2)
                hi(0, L, 0, U_PLE1 + 1)
                root(0, L, 5, 4, 2)

                for n, unit in enumerate((U_PLE0, U_PLE1)):
                    act.wait_ge(s_used.sem, s_used.at(0, L, unit + 1))
                    act_(PP[:, :, n * COLS:(n + 1) * COLS], pair(n), ACT.Copy).then_inc(s_pp.sem, 1)
                turn_hi(0, L, 0, T_PX, KB, XH)
                his(0, L, 0, U_PLE1 + 2, U_PLE1 + 3, U_PLE1 + 4)
                for n in range(2):
                    act.wait_ge(s_used.sem, s_used.at(0, L, U_PLE1 + 3 + 2 * n))
                    act.wait_ge(s_sgf.sem, s_sgf.at(0, L, n))
                    for m in range(TILES):
                        act_(SG[:, m], pair(n)[:, m], ACT.Sigmoid).then_inc(s_sg.sem, 1)

            with act.Fori(0, DEPTH) as L:
                his(1, L, 0, 0, 1)
                turn_hi(1, L, 0, 0, KB, XH)
                with act.Fori(0, 2) as i:
                    his(1, L, i, 2, 3, 4, 5)
                his(1, L, 0, 10, 11, 12)
                turn_copy(1, L, T2_QK, 18, QT2)
                hi(1, L, 0, 13)
                for q in range(len(JOBS2)):
                    exps(1, L, q, JOBS2, PR2)
                    if q in (2, 4):
                        hi(1, L, 0, 13 + q // 2)
                turn_hi(1, L, 0, T2_YA, 3, MH, per=1)
                with act.Fori(0, 2) as i:
                    his(1, L, i, V_RET + 2, V_RET + 3, V_RET + 4, V_RET + 5)
                hi(1, L, 0, V_RET + 10)
                turn_copy(1, L, T2_RET, 16, QTR)
                his(1, L, 0, *range(V_RET + 11, V_GATE + 2))

                def gate(c, func, dst, src):
                    act.wait_ge(s_evac.sem, s_evac.at(1, L, c + 1))
                    act_(dst, src, func).then_inc(s_sz.sem, 1)

                for h in range(RH):
                    hi(1, L, 0, V_GATE + 2 * h + 2)
                    root(1, L, h + 1, h % 2, 2)
                    hi(1, L, 0, V_GATE + 2 * h + 3)
                    gate(15 + h, ACT.Silu, SZ, GZ)
                for c in range(19, 23):
                    hi(1, L, 0, 2 * c + 2)
                    if c == 20:
                        turn_hi(1, L, 0, T2_YB, KB, YH)
                    if c == 22:
                        turn_hi(1, L, 0, T2_YB + 4, 4, XH)
                    hi(1, L, 0, 2 * c + 3)
                    gt = VR[:, :, (c - 19) * COLS:(c - 18) * COLS]
                    gate(c, ACT.Sigmoid, gt, gt)

                hi(1, L, 0, V_RP)
                turn_hi(1, L, 0, T2_YB + 6, 4, XH[:, 4:8])
                his(1, L, 0, *range(V_RP + 1, V_RP + 8))
                turn_hi(1, L, 0, T2_M, 4, XH)
                his(1, L, 0, V_OUT, V_OUT + 1, V_OUT + 2)
                turn_hi(1, L, 0, T2_M + 2, 4, XH[:, 4:8])
                his(1, L, 0, V_OUT + 3, V_FFN)
                root(1, L, 5, 2, 2)

                turn_hi(1, L, 0, T2_FX, KB, XH)
                hi(1, L, 0, V_FFN + 1)

                def inner2(i, j, used, bank=0):
                    act.wait_ge(s_used.sem, s_used.at(1, L, 4 * i + used))
                    act_(H2, pair(bank)[:, :, 0:256], ACT.Silu).then_inc(s_act.sem, 1)

                hi(1, L, 0, V_FFN + 2)
                inner2(0, 0, V_FFN + 2, 2)
                hi(1, L, 0, V_FFN + 3)
                turn_hi(1, L, 0, T2_FFN, 2, MH, per=1)
                with act.Fori(0, FJ - 2) as i:
                    his(1, L, i, V_FFN + 4, V_FFN + 5)
                    inner2(i, 1, V_FFN + 4)
                    his(1, L, i, V_FFN + 6, V_FFN + 7)
                    turn_hi(1, L, i, T2_FFN + 2, 2, MH, per=1)
                e = 4 * (FJ - 2)
                his(1, L, 0, V_FFN + 4 + e, V_FFN + 5 + e)
                inner2(0, FJ - 1, V_FFN + 4 + e)
                his(1, L, 0, V_FFN + 6 + e, V_FFN + 7 + e)
                turn_hi(1, L, 0, T2_FFN + 2 * (FJ - 1), 2, MH, per=1)
                root(1, L, 6, 3, 2)

        @block.gpsimd
        def _(pool):
            tt, ts = nc.gpsimd.tensor_tensor, nc.gpsimd.tensor_scalar
            for dst, src in ((tri, "c_tri"), (causal, "c_causal"), (decay[:], "c_decay"), (rot[:], "c_rot")):
                pool.dma_start(dst, a[src]).then_inc(s_const3, 16)
            pool.wait_ge(s_const, 16 * N_CONST)
            for n in range(2):
                tt(lamv[:, n * 128:n * 128 + 64], lamv[:, n * 128:n * 128 + 64], lamv[:, n * 128 + 64:n * 128 + 128], ALU.mult)
            pool.drain()
            half = 16
            while half:
                for n in range(2):
                    v = lamv[:, n * 128:n * 128 + 64].rearrange("p (l d) -> p l d", d=32)
                    dst = v[:, :, 0:half] if half > 1 else lsum[:, 2 * n:2 * n + 2].unsqueeze(2)
                    ins = tt(dst, v[:, :, 0:half], v[:, :, half:2 * half], ALU.add)
                if half > 1:
                    pool.drain()
                half //= 2
            ins.then_inc(s_tab, 1)
            part = room(2900, TILES, 96)
            pool.wait_ge(s_le, 1)
            tt(lam, lsum[:, 0:2], lsum[:, 2:4], ALU.subtract)
            pool.drain()
            tt(lam, lam, lamc[:, 0:2], ALU.add)
            pool.wait_ge(s_const2, 16 * N_CONST2)
            for n in range(DEPTH):
                ts(subln[:, n * HD:(n + 1) * HD], subln[:, n * HD:(n + 1) * HD], lamc[:, 2 + n:3 + n], None, ALU.mult)
            pool.drain()
            pool.sem_inc(s_pp.sem, s_pp.credit)
            pool.wait_ge(s_sin, 1)
            tt(part, cosd[:], cosd[:], ALU.mult)
            pool.drain()
            ts(cosd[:], part, -2.0, 1.0, ALU.mult, ALU.add)
            ts(sind[:, :, 0:32], sind[:, :, 0:32], -1.0, None, ALU.mult)
            ts(sind[:, :, 64:80], sind[:, :, 64:80], -1.0, None, ALU.mult).then_inc(s_rot0, 1)
            pool.wait_ge(s_xin, 64)

            with pool.Fori(0, DEPTH) as L:
                pool.wait_ge(s_pp.sem, s_pp.at(0, L, 0))
                nc.gpsimd.tensor_copy(prec[:], pre[:, :, bass.ds(L, 1), :].rearrange("p n l k -> p (n l) k")).then_inc(
                    s_cur.sem, 1)
                nc.gpsimd.tensor_copy(cur[:, 0:4], bforget[:, bass.ds(L * 4, 4)])
                nc.gpsimd.tensor_copy(cur[:, 4:8], sink[:, bass.ds(L * 4, 4)])
                nc.gpsimd.tensor_copy(cur[:, 12:13], lam[:, bass.ds(L, 1)])
                nc.gpsimd.tensor_copy(cur[:, 16:80], subln[:, bass.ds(L * HD, HD)])
                pool.drain()
                ts(cur[:, 8:12], cur[:, 4:8], 1.0 / SCALE["D"], None, ALU.mult).then_inc(s_cur.sem, 1)
                pool.wait_ge(s_evac.sem, s_evac.at(0, L, 1))
                rope(pool, nc.gpsimd, RTP, A_Q, 4, HD, 0)
                pool.drain()
                rope(pool, nc.gpsimd, RTP, A_K, 4, HD, 0).then_inc(s_prope.sem, 1)
                pool.drain()
                pool.wait_ge(s_evac.sem, s_evac.at(0, L, 5))
                rope(pool, nc.gpsimd, RTP, C_Q, 8, 32, 64)
                pool.drain()
                pool.wait_ge(s_evac.sem, s_evac.at(0, L, 6))
                rope(pool, nc.gpsimd, RTP, C_K, 8, 32, 64).then_inc(s_prope.sem, 1)
                pool.drain()
                pool.wait_ge(s_evac.sem, s_evac.at(0, L, CH1))
                rope(pool, nc.gpsimd, RTP, D_K, 2, HD, 0)
                pool.drain()
                for kv in range(2):
                    for r in range(2):
                        ins = nc.gpsimd.tensor_copy(DUP[:, :, P + (2 * kv + r) * HD:P + (2 * kv + r + 1) * HD],
                                                    Z[:, :, D_K + kv * HD:D_K + (kv + 1) * HD])
                ins.then_inc(s_prope.sem, 1)

        @block.vector
        def _(dve):
            tt, ts, stt = nc.vector.tensor_tensor, nc.vector.tensor_scalar, nc.vector.scalar_tensor_tensor

            def lo(blk, L, i, c):
                n, slot = size(blk, c), c % RAW
                dve.wait_ge(s_hi.sem, s_hi.at(blk, L, 4 * i + c + 1))
                tt(wlo[:, c % PARTS, 0:n], raw[:, slot, 0:n], whi[:, c % PARTS, 0:n].bitcast(F32),
                   ALU.subtract).then_inc(s_lo.sem, 1)

            def los(blk, L, i, *cs):
                for c in cs:
                    lo(blk, L, i, c)

            def turn_lo(blk, L, i, t, n, hx, lx, per=2, gain=None):
                for b in range(0, n, per):
                    tt_ = t + b // per
                    dve.wait_ge(s_thi.sem, s_thi.at(blk, L, 2 * i + split_no(blk, tt_) + 1))
                    k = min(per, n - b)
                    src = T[:, tt_ % 2, 0:k * S].rearrange("p (k s) -> p k s", s=S)
                    if gain is None:
                        ins = tt(lx[:, b:b + k, :], src, hx[:, b:b + k, :].bitcast(F32), ALU.subtract)
                    else:
                        for kk in range(k):
                            ins = stt(out=lx[:, b + kk, :], in0=src[:, kk, :], scalar=gain[:, b + kk:b + kk + 1],
                                      in1=hx[:, b + kk, :].bitcast(F32), op0=ALU.mult, op1=ALU.subtract)
                    ins.then_inc(s_tfree.sem, 1)

            def mean(norm, n, width, halves=False):
                if halves:
                    tt(stat[:, 0, norm, 0:n], stat[:, 0, norm, 0:n], stat[:, 0, norm, n:2 * n], ALU.add)
                    dve.drain()
                return ts(stat[:, 0, norm, 0:n], stat[:, 0, norm, 0:n], 1.0 / width, EPS, ALU.mult, ALU.add)

            def invert(blk, L, k, norm, n):
                dve.wait_ge(s_sd.sem, s_sd.at(blk, L, k))
                return nc.vector.reciprocal(stat[:, 2, norm, 0:n], stat[:, 1, norm, 0:n])

            def prep(blk, L, q, jobs):
                kind, m, _ = jobs[q]
                n = (m + 1) * P
                dve.wait_ge(s_log.sem, s_log.at(blk, L, q + 1))
                if kind == "E":
                    nc.vector.tensor_reduce(mx[:, q, 0:1], logit_set(q)[:, 0:3, 0:n], AX.XY, ALU.max)
                    dve.drain()
                    ts(nm[:, q, 0:1], mx[:, q, 0:1], -SCALE[kind], None, ALU.mult).then_inc(s_nm.sem, 1)
                    return
                g = G[:, 2 * (q % 2):2 * (q % 2) + 2, :].rearrange("p b (h s) -> p h b s", s=S)
                nc.vector.tensor_reduce(mx[:, q, :].rearrange("p (h b) -> p h b", b=2), g[:, :, :, 0:n], AX.X, ALU.max)
                dve.drain()
                if kind == "D":
                    tt(mx[:, q, :], mx[:, q, :], cur[:, 8:12], ALU.max)
                    dve.drain()
                ins = ts(nm[:, q, :], mx[:, q, :], -SCALE[kind], None, ALU.mult)
                if kind == "D":
                    dve.drain()
                    ins = tt(ds_[:, q, :], cur[:, 4:8], nm[:, q, :], ALU.add)
                ins.then_inc(s_nm.sem, 1)

            def copy_turned(blk, L, q, jobs, t0, dst):
                kind, m, _ = jobs[q]
                w = (3 if kind == "E" else 4) * P
                for kt in range(m + 1):
                    t = t0 + job_banks(jobs, q) + kt
                    dve.wait_ge(s_t.sem, s_t.at(blk, L, t + 1))
                    nc.vector.tensor_copy(dst[:, q % 2, kt, 0:w], T[:, t % 2, 0:w]).then_inc(s_tfree.sem, 1)

            def outputs(blk, L, q, jobs):
                kind, m, x = jobs[q]
                dve.wait_ge(s_pv.sem, s_pv.at(blk, L, q + 1))
                if kind == "E":
                    nc.vector.reciprocal(rl[:, q, 0:1], ls[:, q, 0:1])
                    dve.drain()
                    ts(Z2[:, m, x * HD:(x + 1) * HD], A[:, q % 2, 0:HD], rl[:, q, 0:1], None,
                       ALU.mult).then_inc(s_o.sem, 1)
                    return
                if kind == "D":
                    tt(ls[:, q, :], ls[:, q, :], es[:, q, :], ALU.add)
                    dve.drain()
                nc.vector.reciprocal(rl[:, q, :], ls[:, q, :])
                dve.drain()
                src = A[:, q % 2, 0:4 * HD].rearrange("p (u d) -> p u d", d=HD)
                by = rl[:, q, :].unsqueeze(2).to_broadcast([P, 4, HD])
                if kind != "C":
                    dst = Z[:, m, MIX0 + MIXCOL[kind]:MIX0 + MIXCOL[kind] + 4 * HD].rearrange("p (u d) -> p u d", d=HD)
                    tt(dst, src, by, ALU.mult).then_inc(s_o.sem, 1)
                    return
                odd = rl[:, q, :].rearrange("p (h m) -> p h m", m=2)[:, :, 1]
                ts(odd, odd, cur[:, 12:13], -1.0, ALU.mult, ALU.mult)
                dve.drain()
                both = CB.rearrange("p (u d) -> p u d", d=HD)
                tt(both, src, by, ALU.mult)
                dve.drain()
                two = CB.rearrange("p (h m d) -> p h m d", m=2, d=HD)
                tt(CO[:, m, :, :].rearrange("p (h x) d -> p h x d", x=2)[:, :, x, :], two[:, :, 0, :], two[:, :, 1, :], ALU.add).then_inc(s_o.sem, 1)

            def run_jobs(blk, L, jobs, t0, dst, beside=None):
                for q in range(len(jobs) + 2):
                    if q < len(jobs):
                        prep(blk, L, q, jobs)
                    if 1 <= q <= len(jobs):
                        copy_turned(blk, L, q - 1, jobs, t0, dst)
                    if q >= 2:
                        outputs(blk, L, q - 2, jobs)
                    if beside:
                        beside(q)

            for t in (s_lo, s_tfree, s_evac, s_rlf, s_o, s_sgf):
                dve.sem_inc(t.sem, t.credit)
            dve.wait_ge(s_const, 16 * N_CONST)
            nc.vector.tensor_copy(posf[:], posi[:])
            dve.drain()
            turns = room(2700, TILES, 96)
            for m in range(TILES):
                ts(sind[:, m, :], freq[:], posf[:, m:m + 1], None, ALU.mult)
            dve.drain()
            magic = 12582912.0
            ts(turns, sind[:], 1.0 / (2 * math.pi), magic, ALU.mult, ALU.add)
            dve.drain()
            ts(turns, turns, magic, None, ALU.subtract)
            c1 = 6.28125
            c2 = float(np.float32(round((2 * math.pi - c1) * 2 ** 21) / 2 ** 21))
            for c in (c1, c2, 2 * math.pi - c1 - c2):
                dve.drain()
                stt(out=sind[:], in0=turns, scalar=-c, in1=sind[:], op0=ALU.mult, op1=ALU.add)
            dve.drain()
            ts(sind[:], sind[:], 3.1415925, -3.1415925, ALU.min, ALU.max).then_inc(s_ang, 1)
            dve.wait_ge(s_const2, 16 * N_CONST2)
            nc.vector.tensor_copy(flip[:], arena[:, 2560:2688])
            ok = arena[0:18, 1024:2048].rearrange("p (a b) -> p a b", a=2)
            rowsb = arena[0:18, 2048:2560]
            dve.wait_ge(s_bmm, 1)
            tt(rowsb, T[0:18, 0, :], ok[:, 0], ALU.mult)
            dve.drain()
            tt(rowsb, rowsb, ok[:, 1], ALU.add)
            dve.drain()
            parts = [b[0:18, 0:2, :].rearrange("p k s -> p (k s)") for b in BR]
            nc.vector.tensor_copy(parts[0], rowsb)
            dve.drain()
            tt(parts[1], rowsb, parts[0].bitcast(F32), ALU.subtract).then_inc(s_bvec, 1)
            nc.vector.tensor_copy(maskb[:], room(0, 2, P))
            dve.wait_ge(s_xin, 64)
            nc.vector.tensor_copy(identb[:], ident[:])
            dve.drain()
            dve.sem_inc(s_xh.sem, 1)
            dve.sem_inc(s_x.sem, 1)

            def times_gain(L, norm, row, c, bank, *tiles):
                cols = slice(c * COLS, (c + 1) * COLS)
                for m in tiles:
                    dve.wait_ge(s_sq.sem, s_sq.at(0, L, 2 * (norm - 2 + c) + m + 1))
                    tt(NG[:, m, cols], pair(bank)[:, m, :], gains[:, row, cols], ALU.mult).then_inc(s_ng.sem, 1)

            def add_normed(norm):
                dve.drain()
                for c, done in enumerate((s_xh, s_x)):
                    for m in range(TILES):
                        xc = X[:, m, c * COLS:(c + 1) * COLS]
                        ins = stt(out=xc, in0=NG[:, m, c * COLS:(c + 1) * COLS], scalar=stat[:, 2, norm, m:m + 1],
                                  in1=xc, op0=ALU.mult, op1=ALU.add)
                    ins.then_inc(done.sem, 1)

            with dve.Fori(0, DEPTH) as L:
                turn_lo(0, L, 0, 0, UK, XH, XL, gain=prec[:, 0])
                turn_lo(0, L, 0, 2, UK, XH[:, UK:KB], XL[:, UK:KB], gain=prec[:, 0, UK:KB])
                los(0, L, 0, 0, 1)
                dve.wait_ge(s_ss.sem, s_ss.at(0, L, 1))
                mean(0, 2, DM).then_inc(s_ms.sem, 1)
                invert(0, L, 1, 0, 2).then_inc(s_rs.sem, 1)

                los(0, L, 0, *range(2, 8))
                dve.wait_ge(s_evac.sem, s_evac.at(0, L, 3))
                dve.wait_ge(s_rot0, 1)
                dve.wait_ge(s_const3, 64)
                rope(dve, nc.vector, RT, A_IQ, 9, HD, 0)
                ts(IW[:], Z[:, :, A_IW:A_IW + IDX_HEADS], IDX_HEADS ** -0.5 * HD ** -0.5, None, ALU.mult)
                dve.drain()
                for r in range(2):
                    ins = nc.vector.tensor_copy(DUP[:, :, r * HD:(r + 1) * HD], Z[:, :, A_IK:A_IK + HD])
                ins.then_inc(s_rope.sem, 1)
                los(0, L, 0, 8, 9, 10)

                def scores(m):
                    n = (m + 1) * P
                    sc = SCO[:, 0:n]
                    dve.drain()
                    dve.wait_ge(s_rl.sem, s_rl.at(0, L, 1 + 2 * m))
                    ts(sc, RL[:, 0, 0:n], IW[:, m, 0:1], None, ALU.mult)
                    for h in range(1, IDX_HEADS):
                        dve.drain()
                        ins = stt(out=sc, in0=RL[:, h, 0:n], scalar=IW[:, m, h:h + 1], in1=sc, op0=ALU.mult, op1=ALU.add)
                    ins.then_inc(s_rlf.sem, 1)
                    dve.drain()
                    tt(sc, sc, causal[:, m, 0:n], ALU.add)

                def pick(m, keys):
                    sc = SCO[:, 0:(m + 1) * P]
                    for _ in range(keys // 8):
                        dve.drain()
                        nc.vector.max(m8[:], sc)
                        dve.drain()
                        nc.vector.match_replace(out=sc, in_to_replace=m8[:], in_values=sc, imm_value=TAKEN)

                def mask(m):
                    n = (m + 1) * P
                    sc = SCO[:, 0:n]
                    dve.drain()
                    ts(sc, sc, TAKEN / 2, NEG, ALU.is_gt, ALU.mult)
                    dve.drain()
                    tt(amask[:, m, 0:n], sc, causal[:, m, 0:n], ALU.min).then_inc(s_am.sem, 1)

                def gates(step):
                    if step == 0:
                        dve.wait_ge(s_cur.sem, s_cur.at(0, L, 2))
                        dve.wait_ge(s_evac.sem, s_evac.at(0, L, 5))
                        tt(LF[:, 0], Z[:, :, B_F:B_F + 4], cur[:, 0:4].unsqueeze(1).to_broadcast([P, TILES, 4]), ALU.add)
                        dve.drain()
                        stt(out=LF[:, 1], in0=LF[:, 0], scalar=-1.0, in1=LF[:, 0], op0=ALU.mult,
                            op1=ALU.min).then_inc(s_lf.sem, 1)
                        ts(LF[:, 3], LF[:, 0], 0.0, None, ALU.min)
                        return
                    dve.wait_ge(s_lg.sem, s_lg.at(0, L, step))
                    if step == 1:
                        ts(LF[:, 2], LF[:, 1], 1.0, None, ALU.add).then_inc(s_lf.sem, 1)
                        return
                    tt(LF[:, 3], LF[:, 3], LF[:, 2], ALU.subtract)
                    dve.drain()
                    ts(LF[:, 4], LF[:, 3], -1.0 / SCALE["B"], None, ALU.mult).then_inc(s_lf.sem, 1)

                scores(0)
                pick(0, TOPK // 2)
                gates(0)
                pick(0, TOPK // 4)
                gates(1)
                lo(0, L, 0, 11)
                pick(0, TOPK // 4)
                mask(0)
                gates(2)
                lo(0, L, 0, 12)
                scores(1)

                def beside(q):
                    if q == 0:
                        lo(0, L, 0, 13)
                    elif q == 3:
                        dve.wait_ge(s_evac.sem, s_evac.at(0, L, CH1))
                        rope(dve, nc.vector, RT, D_Q, 4, HD, 0).then_inc(s_rope.sem, 1)
                    if q in (0, 1, 4, 5):
                        pick(1, TOPK // 4)
                    if q == 5:
                        mask(1)
                    elif q in (6, 7):
                        lo(0, L, 0, 8 + q)

                run_jobs(0, L, JOBS1, T_JOB, PT, beside)
                turn_lo(0, L, 0, T_MIX, UK, XH, XL)
                dve.drain()
                tt(CS, CO, CO, ALU.mult)
                dve.drain()
                nc.vector.tensor_reduce(stat[:, 0, 1, :], CS.rearrange("p m h d -> p (m h) d"), AX.X, ALU.add)
                dve.drain()
                mean(1, 8, HD).then_inc(s_ms.sem, 1)
                invert(0, L, 2, 1, 8)
                dve.drain()
                co = CO.rearrange("p m h d -> p (m h) d")
                tt(co, co, stat[:, 2, 1, :].unsqueeze(2).to_broadcast([P, 8, HD]), ALU.mult)
                dve.drain()
                c0 = MIX0 + MIXCOL["C"]
                for m in range(TILES):
                    ins = tt(Z[:, m, c0:c0 + 256].rearrange("p (h d) -> p h d", d=HD), CO[:, m],
                             cur[:, 16:80].unsqueeze(1).to_broadcast([P, 4, HD]), ALU.mult)
                ins.then_inc(s_mix.sem, 1)

                lo(0, L, 0, U_OUT + 2)
                turn_lo(0, L, 0, T_MIX + 2, UK, XH[:, UK:KB], XL[:, UK:KB])
                los(0, L, 0, U_OUT + 3, U_OUT + 4)
                dve.wait_ge(s_gain.sem, s_gain.at(0, L, 2))
                times_gain(L, 2, 0, 0, 1, 0, 1)
                times_gain(L, 2, 0, 1, 0, 0)
                dve.wait_ge(s_sq.sem, s_sq.at(0, L, 4))
                mean(2, 2, DM, halves=True).then_inc(s_ms.sem, 1)
                times_gain(L, 2, 0, 1, 0, 1)
                invert(0, L, 3, 2, 2)
                add_normed(2)

                turn_lo(0, L, 0, T_N2, KB, XH, XL, gain=prec[:, 1])
                lo(0, L, 0, U_OUT + 5)
                dve.wait_ge(s_ss.sem, s_ss.at(0, L, 2))
                mean(3, 2, DM).then_inc(s_ms.sem, 1)
                invert(0, L, 4, 3, 2).then_inc(s_rs.sem, 1)
                dve.drain()

                def inner(i, j, bank=0):
                    dve.wait_ge(s_act.sem, s_act.at(0, L, i + j + 1))
                    for m in range(TILES):
                        ins = stt(out=H[:, m, :], in0=pair(bank)[:, m, :], scalar=stat[:, 2, 3, m:m + 1], in1=H[:, m, :],
                                  op0=ALU.mult, op1=ALU.mult)
                    ins.then_inc(s_h.sem, 1)

                lo(0, L, 0, U_MLP + 2)
                inner(0, 0, 2)
                turn_lo(0, L, 0, T_P, 2, YH, YL, per=1)
                lo(0, L, 0, U_MLP + 3)
                turn_lo(0, L, 0, T_MLP, UK, MH, ML)
                with dve.Fori(0, 6) as i:
                    los(0, L, i, U_MLP + 4, U_MLP + 5)
                    inner(i, 1)
                    los(0, L, i, U_MLP + 6, U_MLP + 7)
                    turn_lo(0, L, i, T_MLP + 2, UK, MH, ML)
                los(0, L, 0, U_MLP + 28, U_MLP + 29)
                inner(0, 7)
                lo(0, L, 0, U_PLE0)
                turn_lo(0, L, 0, T_MLP + 14, UK, MH, ML)
                los(0, L, 0, U_DN7, U_DN7 + 1)
                times_gain(L, 4, 1, 0, 1, 0, 1)
                times_gain(L, 4, 1, 1, 2, 0)
                dve.wait_ge(s_sq.sem, s_sq.at(0, L, 8))
                mean(4, 2, DM, halves=True).then_inc(s_ms.sem, 1)
                times_gain(L, 4, 1, 1, 2, 1)
                lo(0, L, 0, U_PLE1)
                invert(0, L, 5, 4, 2)
                add_normed(4)

                turn_lo(0, L, 0, T_PX, KB, XH, XL)
                los(0, L, 0, U_PLE1 + 1, U_PLE1 + 2, U_PLE1 + 3, U_PLE1 + 4)
                for n, done in enumerate((s_xh, s_x)):
                    cols = slice(n * COLS, (n + 1) * COLS)
                    for m in range(TILES):
                        dve.wait_ge(s_sg.sem, s_sg.at(0, L, 2 * n + m + 1))
                        ins = tt(TMP[:, m], SG[:, m], PP[:, m, cols], ALU.mult)
                    ins.then_inc(s_sgf.sem, 1)
                    dve.drain()
                    tt(X[:, :, cols], X[:, :, cols], TMP, ALU.add).then_inc(done.sem, 1)
                    dve.drain()

            with dve.Fori(0, DEPTH) as L:
                turn_lo(1, L, 0, 0, KB, XH, XL)
                los(1, L, 0, 0, 1)

                def project(i, c, dst, cols=COLS):
                    dve.wait_ge(s_used.sem, s_used.at(1, L, 4 * i + 2 * c + 2))
                    dve.wait_ge(s_bin[c % 2].sem, s_bin[c % 2].at(1, L, i + c // 2 + 1))
                    bank = 2 if c == SEG1 - 1 else c % 2
                    tt(dst, pair(bank)[:, :, 0:cols], BIN[:, c % 2, 0:cols].unsqueeze(1).to_broadcast([P, TILES, cols]),
                       ALU.add).then_inc(s_evac.sem, 1)

                with dve.Fori(0, 2) as i:
                    for c in range(2):
                        los(1, L, i, 2 * c + 2, 2 * c + 3)
                        project(i, c, Z2[:, :, bass.ds(i * 1024 + c * COLS, COLS)])
                los(1, L, 0, 10, 11)
                project(0, 4, Z2[:, :, 4 * COLS:5 * COLS])
                lo(1, L, 0, 12)
                project(0, 5, Z2[:, :, 5 * COLS:6 * COLS])
                lo(1, L, 0, 13)

                def beside(q):
                    if q == 1:
                        project(0, 6, Z2[:, :, 6 * COLS:6 * COLS + LAST2], LAST2)
                    elif q in (3, 5):
                        lo(1, L, 0, 14 + q // 5)

                run_jobs(1, L, JOBS2, T2_JOB, PT2, beside)
                turn_lo(1, L, 0, T2_YA, 3, MH, ML, per=1)

                def rotate(i, c):
                    x = QK[:, :, bass.ds(i * 1024 + c * COLS, COLS)].rearrange("p m (h e d) -> p m h e d", e=2, d=P)
                    x1, x2 = x[:, :, :, 0], x[:, :, :, 1]
                    cos, sin = (rot[:, n].unsqueeze(2).to_broadcast([P, TILES, 2, P]) for n in range(2))
                    u = RTR[:]
                    tt(u[:, 0], x2, sin, ALU.mult)
                    tt(u[:, 1], x1, sin, ALU.mult)
                    dve.drain()
                    tt(x1, x1, cos, ALU.mult)
                    tt(x2, x2, cos, ALU.mult)
                    dve.drain()
                    tt(x1, x1, u[:, 0], ALU.subtract)
                    ins = tt(x2, x2, u[:, 1], ALU.add)
                    return ins

                with dve.Fori(0, 2) as i:
                    for c in range(2):
                        los(1, L, i, V_RET + 2 + 2 * c, V_RET + 3 + 2 * c)
                        project(i, SEG1 + c, QK[:, :, bass.ds(i * 1024 + c * COLS, COLS)])
                        dve.drain()
                        rotate(i, c).then_inc(s_rot.sem, 1)
                def decayed(h):
                    dve.wait_ge(s_sc.sem, s_sc.at(1, L, h + 1))
                    tt(SCT[:, h, 0:S], A[:, h % 2, 0:S], decay[:, h].rearrange("p a b -> p (a b)"), ALU.mult)
                    tt(SCT[:, h, S:S + P], A[:, h % 2, S:S + P], decay[:, h, 0], ALU.mult).then_inc(s_sd2.sem, 1)

                for c in range(11, 15):
                    los(1, L, 0, 2 * c + 2, 2 * c + 3)
                    project(0, c, VR[:, :, (c - 11) * COLS:(c - 10) * COLS])
                    if c in (12, 13):
                        decayed(2 * (c - 12))
                        decayed(2 * (c - 12) + 1)

                def normalise(h):
                    dve.wait_ge(s_ro.sem, s_ro.at(1, L, h + 1))
                    for m in range(TILES):
                        nc.vector.bn_stats(bns[:, 2 * (h % 2) + m, :], A[:, m, :])
                    dve.drain()
                    for m in range(TILES):
                        nc.vector.bn_aggr(bna[:, 2 * (h % 2) + m, :], bns[:, 2 * (h % 2) + m, :])
                    dve.drain()
                    b = bna[:, 2 * (h % 2):2 * (h % 2) + 2, :]
                    ts(stat[:, 0, h % 2, 0:2], b[:, :, 1], LN_EPS, None, ALU.add).then_inc(s_ms.sem, 1)
                    invert(1, L, h + 1, h % 2, 2)
                    dve.drain()
                    for m in range(TILES):
                        ins = ts(QK[:, m, h * RDV:(h + 1) * RDV], A[:, m, :], b[:, m, 0:1], stat[:, 2, h % 2, m:m + 1],
                                 ALU.subtract, ALU.mult)
                    ins.then_inc(s_yr.sem, 1)

                for h in range(RH):
                    lo(1, L, 0, V_GATE + 2 * h + 2)
                    normalise(h)
                    lo(1, L, 0, V_GATE + 2 * h + 3)
                    project(0, 15 + h, GZ)
                    dve.wait_ge(s_sz.sem, s_sz.at(1, L, h + 1))
                    y = QK[:, :, h * RDV:(h + 1) * RDV]
                    tt(y, y, SZ, ALU.mult).then_inc(s_yb.sem, 1)
                for c in range(19, 23):
                    lo(1, L, 0, 2 * c + 2)
                    if c == 20:
                        turn_lo(1, L, 0, T2_YB, KB, YH, YL)
                    if c == 22:
                        turn_lo(1, L, 0, T2_YB + 4, 4, XH, XL)
                    else:
                        lo(1, L, 0, 2 * c + 3)
                    project(0, c, VR[:, :, (c - 19) * COLS:(c - 18) * COLS])
                lo(1, L, 0, V_AP + 1)

                lo(1, L, 0, V_RP)
                dve.wait_ge(s_sz.sem, s_sz.at(1, L, 8))

                def gated(n, used, gate_col, dst):
                    dve.wait_ge(s_used.sem, s_used.at(1, L, used))
                    tt(dst, pair(1 - n), VR[:, :, gate_col + n * COLS:gate_col + (n + 1) * COLS],
                       ALU.mult).then_inc(s_evac.sem, 1)

                gated(0, V_AP + 1, 0, M[:, :, 0:COLS])
                turn_lo(1, L, 0, T2_YB + 6, 4, XH[:, 4:8], XL[:, 4:8])
                lo(1, L, 0, V_RP + 1)
                gated(1, V_AP + 2, 0, M[:, :, COLS:DM])
                for n in range(2):
                    los(1, L, 0, *(range(V_RP + 2, V_RP + 6) if n == 0 else [V_OUT]))
                    gated(n, V_RP + 4 + 4 * n, DM, TMP2)
                    dve.drain()
                    mc = M[:, :, n * COLS:(n + 1) * COLS]
                    tt(mc, mc, TMP2, ALU.add).then_inc(s_m.sem, 1)
                    dve.drain()
                    if n == 0:
                        los(1, L, 0, V_RP + 6, V_RP + 7)
                        turn_lo(1, L, 0, T2_M, 4, XH, XL)
                lo(1, L, 0, V_OUT + 1)
                lo(1, L, 0, V_OUT + 2)
                turn_lo(1, L, 0, T2_M + 2, 4, XH[:, 4:8], XL[:, 4:8])

                def residual(c, bank, used, half=None):
                    for m in range(TILES):
                        if half and m == 0:
                            dve.wait_ge(s_half.sem, s_half.at(1, L, half))
                        elif m == (1 if half else 0):
                            dve.wait_ge(s_used.sem, s_used.at(1, L, used))
                        xc = X[:, m, c * COLS:(c + 1) * COLS]
                        ins = stt(out=xc, in0=xc, scalar=ALPHA, in1=pair(bank)[:, m], op0=ALU.mult, op1=ALU.add)
                        dve.drain()
                        nc.vector.bn_stats(bns[:, 2 * m + c, :], xc)
                    return ins

                def layer_norm(k, norm, gain):
                    dve.drain()
                    for m in range(TILES):
                        nc.vector.bn_aggr(bna[:, m, :], bns[:, 2 * m:2 * m + 2, :].rearrange("p a b -> p (a b)"))
                    dve.drain()
                    ts(stat[:, 0, norm, 0:2], bna[:, 0:2, 1], LN_EPS, None, ALU.add).then_inc(s_ms.sem, 1)
                    dve.wait_ge(s_gain.sem, s_gain.at(1, L, gain))
                    for c, done in enumerate((s_xh, s_x)):
                        cols = slice(c * COLS, (c + 1) * COLS)
                        for m in range(TILES):
                            xc = X[:, m, cols]
                            stt(out=xc, in0=xc, scalar=bna[:, m, 0:1], in1=gains[:, 0, cols], op0=ALU.subtract,
                                op1=ALU.mult)
                        if c == 0:
                            invert(1, L, k, norm, 2)
                        dve.drain()
                        for m in range(TILES):
                            xc = X[:, m, cols]
                            ins = stt(out=xc, in0=xc, scalar=stat[:, 2, norm, m:m + 1], in1=gains[:, 1, cols],
                                      op0=ALU.mult, op1=ALU.add)
                        ins.then_inc(done.sem, 1)

                lo(1, L, 0, V_OUT + 3)
                residual(0, 1, V_OUT + 3).then_inc(s_evac.sem, 1)
                lo(1, L, 0, V_FFN)
                residual(1, 0, V_OUT + 4, 1).then_inc(s_evac.sem, 1)
                layer_norm(5, 2, 2)

                turn_lo(1, L, 0, T2_FX, KB, XH, XL)
                lo(1, L, 0, V_FFN + 1)

                def inner2(i, j, bank=0):
                    dve.wait_ge(s_act.sem, s_act.at(1, L, i + j + 1))
                    tt(H2, H2, pair(bank)[:, :, 256:512], ALU.mult).then_inc(s_h.sem, 1)

                lo(1, L, 0, V_FFN + 2)
                inner2(0, 0, 2)
                lo(1, L, 0, V_FFN + 3)
                turn_lo(1, L, 0, T2_FFN, 2, MH, ML, per=1)
                with dve.Fori(0, FJ - 2) as i:
                    los(1, L, i, V_FFN + 4, V_FFN + 5)
                    inner2(i, 1)
                    los(1, L, i, V_FFN + 6, V_FFN + 7)
                    turn_lo(1, L, i, T2_FFN + 2, 2, MH, ML, per=1)
                e = 4 * (FJ - 2)
                los(1, L, 0, V_FFN + 4 + e, V_FFN + 5 + e)
                inner2(0, FJ - 1)
                los(1, L, 0, V_FFN + 6 + e, V_FFN + 7 + e)
                turn_lo(1, L, 0, T2_FFN + 2 * (FJ - 1), 2, MH, ML, per=1)
                residual(0, 1, UNITS2 - 1)
                residual(1, 2, UNITS2, 2)
                layer_norm(6, 3, 4)


def kernel(**inputs):
    import concourse.bacc as bacc
    from concourse.bass_utils import run_bass_kernel_spmd

    nc = bacc.Bacc("TRN2", target_bir_lowering=False, num_devices=1)
    arrays = {f"in_{k}": np.ascontiguousarray(v) for k, v in {**inputs, **constants()}.items()}
    a = {k[3:]: nc.dram_tensor(k, v.shape, mybir.dt.from_np(v.dtype), kind="ExternalInput").ap()
         for k, v in arrays.items()}
    out = nc.dram_tensor("out", (1, S, DM), F32, kind="ExternalOutput").ap()
    program(nc, a, out)
    return run_bass_kernel_spmd(nc, [arrays], core_ids=[0]).results[0]["out"]
```
